# Optimizing a Trainium2 kernel written in Bass

```python
import math
import jax, jax.numpy as jnp
from jax import lax
import numpy as np

D_MODEL = 1024
BATCH = 1
SEQ = 512
DEPTH = 2

GRID_W = 64
CTX_LEN = 256
D_FF = 4 * D_MODEL
CONV_K = 4
CONV_LEFT = 2
GDN_HEADS = 4
GDN_DK = 128
GDN_DV = 128
GDN_W = GDN_HEADS * GDN_DK
GDN_CHUNK = 64
LRU_W = D_MODEL - GDN_HEADS * GDN_DV
LRU_BLOCKS = 8
LRU_BW = LRU_W // LRU_BLOCKS
LRU_C = 8.0
EV_IN = 4 * GDN_W + 4 * GDN_HEADS + 2 * LRU_W
DIFF_HEADS = 8
DIFF_D = D_MODEL // DIFF_HEADS // 2
DIFF_DV = 2 * DIFF_D
Q_BLOCK = 128
ROPE_THETA = 10000.0
N_EVEN = (DEPTH + 1) // 2
N_ODD = DEPTH // 2
DEEPNORM_ALPHA = (2 * DEPTH) ** 0.25
DEEPNORM_BETA = (8 * DEPTH) ** -0.25
NORM_EPS = 1e-6

kernel_name = 'hybrid_gdn_rglru_diffattn_prefix_trunk'

F32 = jnp.float32

def _layernorm(x, g, b):
    xf = x.astype(F32)
    mu = jnp.mean(xf, -1, keepdims=True)
    var = jnp.mean(jnp.square(xf - mu), -1, keepdims=True)
    return ((xf - mu) * lax.rsqrt(var + NORM_EPS) * g + b).astype(x.dtype)

def _rmsnorm(x, g):
    xf = x.astype(F32)
    return xf * lax.rsqrt(jnp.mean(xf * xf, -1, keepdims=True) + NORM_EPS) * g.astype(F32)

def _l2norm(x):
    return x * lax.rsqrt(jnp.sum(x * x, -1, keepdims=True) + NORM_EPS)

def _modulate(h, shift, scale):
    return h * (1 + scale) + shift

def _dwconv(x, w):
    k = w.shape[0]
    return lax.conv_general_dilated(x, w[:, None, :], window_strides=(1,),
                                    padding=[(CONV_LEFT, k - 1 - CONV_LEFT)],
                                    dimension_numbers=('NWC', 'WIO', 'NWC'),
                                    feature_group_count=x.shape[-1])

def _axial_rope_tables(row, col):
    half = DIFF_D // 2
    inv = ROPE_THETA ** (-(jnp.arange(0, half, 2, dtype=F32) / half))
    ang_r = row.astype(F32)[:, None] * inv
    ang_c = col.astype(F32)[:, None] * inv
    ang = jnp.concatenate([ang_r, ang_r, ang_c, ang_c], axis=-1)
    return jnp.cos(ang), jnp.sin(ang)

def _rope(t, cos, sin):
    t1, t2, t3, t4 = jnp.split(t.astype(F32), 4, axis=-1)
    rot = jnp.concatenate([-t2, t1, -t4, t3], axis=-1)
    return (t.astype(F32) * cos + rot * sin).astype(t.dtype)

def _gdn_chunk(q, k, v, beta, g, s0):
    bsz, nh, L, _ = q.shape
    n = L // GDN_CHUNK
    chunks = lambda t: t.reshape(bsz, nh, n, GDN_CHUNK, *t.shape[3:])
    q, k, v, beta, g = chunks(q), chunks(k), chunks(v), chunks(beta), chunks(g)
    gam = jnp.cumsum(g, axis=-1)
    idx = jnp.arange(GDN_CHUNK)
    incl = idx[:, None] >= idx[None, :]
    strict = idx[:, None] > idx[None, :]
    decay = jnp.exp(jnp.where(incl, gam[..., :, None] - gam[..., None, :], -jnp.inf))
    kb = k * beta[..., None]
    a_strict = jnp.where(strict, jnp.einsum('bhnid,bhnjd->bhnij', kb, k) * decay, 0.0)
    eye = jnp.eye(GDN_CHUNK, dtype=F32)
    t_mat = lax.linalg.triangular_solve(eye + a_strict, jnp.broadcast_to(eye, a_strict.shape),
                                        left_side=True, lower=True, unit_diagonal=True)
    u = t_mat @ (v * beta[..., None])
    w = t_mat @ (kb * jnp.exp(gam)[..., None])
    qk = jnp.einsum('bhnid,bhnjd->bhnij', q, k) * decay
    q_dec = q * jnp.exp(gam)[..., None]
    k_dec = k * jnp.exp(gam[..., -1:] - gam)[..., None]
    c_dec = jnp.exp(gam[..., -1])

    def step(s, xs):
        u_c, w_c, qk_c, qd_c, kd_c, cd_c = xs
        v_new = u_c - w_c @ s
        o = qd_c @ s + qk_c @ v_new
        s = s * cd_c[..., None, None] + jnp.einsum('bhcd,bhce->bhde', kd_c, v_new)
        return s, o

    xs = tuple(jnp.moveaxis(t, 2, 0) for t in (u, w, qk, q_dec, k_dec, c_dec))
    s_fin, o = lax.scan(step, s0, xs)
    o = jnp.moveaxis(o, 0, 2).reshape(bsz, nh, L, -1)
    return o, s_fin

def _gdn_prep(qkv, a, b, conv_w, a_log, dt_bias):
    bsz, L, _ = qkv.shape
    qkv = jax.nn.silu(_dwconv(qkv, conv_w)).astype(F32)
    q, k, v = jnp.split(qkv, 3, axis=-1)
    heads = lambda t: t.reshape(bsz, L, GDN_HEADS, -1).transpose(0, 2, 1, 3)
    q = _l2norm(heads(q)) * GDN_DK ** -0.5
    k = _l2norm(heads(k))
    v = heads(v)
    a = a.astype(F32).reshape(bsz, L, 2, GDN_HEADS)
    g = -jnp.exp(a_log.astype(F32)) * jax.nn.softplus(a + dt_bias.astype(F32))
    beta = jax.nn.sigmoid(b.astype(F32).reshape(bsz, L, 2, GDN_HEADS))
    return q, k, v, g.transpose(2, 0, 3, 1), beta.transpose(2, 0, 3, 1)

def _gdn_bidir(ctx_in, lat_in):
    qc, kc, vc, gc, bc = ctx_in
    ql, kl, vl, gl, bl = lat_in
    s0 = jnp.zeros((qc.shape[0], GDN_HEADS, GDN_DK, GDN_DV), F32)
    flip = lambda t: jnp.flip(t, axis=2)
    oc_f, s_f = _gdn_chunk(qc, kc, vc, bc[0], gc[0], s0)
    ol_f, _ = _gdn_chunk(ql, kl, vl, bl[0], gl[0], s_f)
    oc_b, s_b = _gdn_chunk(flip(qc), flip(kc), flip(vc), flip(bc[1]), flip(gc[1]), s0)
    ol_b, _ = _gdn_chunk(flip(ql), flip(kl), flip(vl), flip(bl[1]), flip(gl[1]), s_b)
    return oc_f + flip(oc_b), ol_f + flip(ol_b)

def _gdn_out(o, z, norm_g):
    bsz, _, L, _ = o.shape
    o = _rmsnorm(o.transpose(0, 2, 1, 3), norm_g)
    zz = jax.nn.silu(z.astype(F32)).reshape(bsz, L, GDN_HEADS, GDN_DV)
    return (o * zz).reshape(bsz, L, GDN_W)

def _lru_coeffs(xr, gate_w, gate_b, lam):
    bsz, L, _ = xr.shape
    xb = xr.reshape(bsz, L, LRU_BLOCKS, LRU_BW)
    gates = jnp.einsum('blnc,gncd->gblnd', xb, gate_w.astype(F32)).reshape(2, bsz, L, LRU_W)
    gates = gates + gate_b.astype(F32)[:, None, None, :]
    r = jax.nn.sigmoid(gates[0])
    i = jax.nn.sigmoid(gates[1])
    log_a = -LRU_C * r * jax.nn.softplus(-lam.astype(F32))
    a = jnp.exp(log_a)
    u = jnp.sqrt(-jnp.expm1(2.0 * log_a)) * (i * xr)
    return a, u

def _lin_scan(a, u, h0):
    u = u.at[:, 0].add(a[:, 0] * h0)
    comb = lambda l, r: (l[0] * r[0], r[0] * l[1] + r[1])
    _, h = lax.associative_scan(comb, (a, u), axis=1)
    return h

def _lru_bidir(xr_c, xr_l, gate_w, gate_b, lam):
    h0 = jnp.zeros((xr_c.shape[0], LRU_W), F32)
    flip = lambda t: jnp.flip(t, axis=1)
    a, u = _lru_coeffs(xr_c, gate_w[0], gate_b[0], lam[0])
    hc_f = _lin_scan(a, u, h0)
    a, u = _lru_coeffs(xr_l, gate_w[0], gate_b[0], lam[0])
    hl_f = _lin_scan(a, u, hc_f[:, -1])
    a, u = _lru_coeffs(flip(xr_c), gate_w[1], gate_b[1], lam[1])
    hc_b = _lin_scan(a, u, h0)
    a, u = _lru_coeffs(flip(xr_l), gate_w[1], gate_b[1], lam[1])
    hl_b = _lin_scan(a, u, hc_b[:, -1])
    return hc_f + flip(hc_b), hl_f + flip(hl_b)

def _even_mixer(u_ctx, u_lat, w_in, w_out, qkv_conv, a_log, dt_bias, gdn_norm,
                lru_conv_w, lru_conv_b, lru_gate_w, lru_gate_b, lru_lambda, need_ctx):
    cuts = [3 * GDN_W, 4 * GDN_W, 4 * GDN_W + 2 * GDN_HEADS, 4 * GDN_W + 4 * GDN_HEADS,
            4 * GDN_W + 4 * GDN_HEADS + LRU_W]

    def local(u):
        qkv, z, a, b, xr, gate = jnp.split(u @ w_in, cuts, axis=-1)
        gdn = _gdn_prep(qkv, a, b, qkv_conv, a_log, dt_bias)
        xr = (_dwconv(xr, lru_conv_w) + lru_conv_b).astype(F32)
        return gdn, z, xr, gate

    gdn_c, z_c, xr_c, gate_c = local(u_ctx)
    gdn_l, z_l, xr_l, gate_l = local(u_lat)
    o_c, o_l = _gdn_bidir(gdn_c, gdn_l)
    h_c, h_l = _lru_bidir(xr_c, xr_l, lru_gate_w, lru_gate_b, lru_lambda)

    def merge(o, z, h, gate, dtype):
        y = jnp.concatenate([_gdn_out(o, z, gdn_norm), h * jax.nn.gelu(gate.astype(F32))], axis=-1)
        return (y.astype(w_out.dtype) @ w_out).astype(dtype)

    y_lat = merge(o_l, z_l, h_l, gate_l, u_lat.dtype)
    y_ctx = merge(o_c, z_c, h_c, gate_c, u_ctx.dtype) if need_ctx else None
    return y_ctx, y_lat

def _diff_attend(q, k, v, lam):
    s = jnp.einsum('bqhmd,bkhmd->bhmqk', q, k).astype(F32) * DIFF_D ** -0.5
    p = jax.nn.softmax(s, axis=-1)
    p = p[:, :, 0] - lam * p[:, :, 1]
    return jnp.einsum('bhqk,bkhv->bqhv', p.astype(v.dtype), v)

def _diff_mixer(u_ctx, u_lat, w_qkv, w_out, lam_vec, subln, cos, sin, layer_idx, need_ctx):
    lam_init = 0.8 - 0.6 * math.exp(-0.3 * layer_idx)
    lv = lam_vec.astype(F32)
    lam = jnp.exp(jnp.sum(lv[0] * lv[1])) - jnp.exp(jnp.sum(lv[2] * lv[3])) + lam_init

    def heads(u):
        bsz, L, _ = u.shape
        q, k, v = jnp.split(u @ w_qkv, 3, axis=-1)
        return (q.reshape(bsz, L, DIFF_HEADS, 2, DIFF_D), k.reshape(bsz, L, DIFF_HEADS, 2, DIFF_D),
                v.reshape(bsz, L, DIFF_HEADS, DIFF_DV))

    qc, kc, vc = heads(u_ctx)
    ql, kl, vl = heads(u_lat)
    cb, sb = cos[None, :, None, None, :], sin[None, :, None, None, :]
    ql, kl = _rope(ql, cb, sb), _rope(kl, cb, sb)
    k_all = jnp.concatenate([kc, kl], axis=1)
    v_all = jnp.concatenate([vc, vl], axis=1)
    bsz, L = ql.shape[:2]
    nb = L // Q_BLOCK
    qb = jnp.moveaxis(ql.reshape(bsz, nb, Q_BLOCK, DIFF_HEADS, 2, DIFF_D), 1, 0)
    o_l = lax.map(lambda qblk: _diff_attend(qblk, k_all, v_all, lam), qb)
    o_l = jnp.moveaxis(o_l, 0, 1).reshape(bsz, L, DIFF_HEADS, DIFF_DV)

    def out(o, dtype):
        y = _rmsnorm(o, subln) * (1.0 - lam_init)
        y = y.reshape(o.shape[0], o.shape[1], D_MODEL).astype(w_out.dtype)
        return (y @ w_out).astype(dtype)

    y_lat = out(o_l, u_lat.dtype)
    y_ctx = out(_diff_attend(qc, kc, vc, lam), u_ctx.dtype) if need_ctx else None
    return y_ctx, y_lat

def _mlp(u, w1, w2):
    return jnp.square(jax.nn.relu(u @ w1)) @ w2

def setup_inputs(seed: int = 0) -> dict:
    key = jax.random.key(seed)
    ks = jax.random.split(key, 24)
    nrm = lambda k, shape, s: jax.random.normal(k, shape, F32) * s
    x = nrm(ks[0], (BATCH, SEQ, D_MODEL), 1.0)
    c = nrm(ks[1], (BATCH, D_MODEL), 1.0)
    ctx = nrm(ks[2], (BATCH, CTX_LEN, D_MODEL), 1.0)
    c_ctx = nrm(ks[3], (D_MODEL,), 1.0)
    ada_w = nrm(ks[4], (DEPTH, D_MODEL, 6 * D_MODEL), 0.5 * D_MODEL ** -0.5)
    ada_b = nrm(ks[5], (DEPTH, 6 * D_MODEL), 0.02)
    ln_g = 1.0 + nrm(ks[6], (DEPTH, 2, D_MODEL), 0.02)
    ln_b = nrm(ks[7], (DEPTH, 2, D_MODEL), 0.02)
    mlp_w1 = nrm(ks[8], (DEPTH, D_MODEL, D_FF), D_MODEL ** -0.5)
    mlp_w2 = nrm(ks[9], (DEPTH, D_FF, D_MODEL), DEEPNORM_BETA * D_FF ** -0.5)
    mix_w_out = nrm(ks[10], (DEPTH, D_MODEL, D_MODEL), DEEPNORM_BETA * D_MODEL ** -0.5)
    ev_w_in = nrm(ks[11], (N_EVEN, D_MODEL, EV_IN), D_MODEL ** -0.5)
    ev_qkv_conv = nrm(ks[12], (N_EVEN, CONV_K, 3 * GDN_W), CONV_K ** -0.5)
    ev_a_log = jnp.log(jax.random.uniform(ks[13], (N_EVEN, 2, GDN_HEADS), F32, 1.0, 16.0))
    dt = jnp.exp(jax.random.uniform(ks[14], (N_EVEN, 2, GDN_HEADS), F32, math.log(1e-3), math.log(1e-1)))
    ev_dt_bias = dt + jnp.log(-jnp.expm1(-dt))
    ev_gdn_norm = 1.0 + nrm(ks[15], (N_EVEN, GDN_DV), 0.02)
    ev_lru_conv_w = nrm(ks[16], (N_EVEN, CONV_K, LRU_W), CONV_K ** -0.5)
    ev_lru_conv_b = nrm(ks[17], (N_EVEN, LRU_W), 0.02)
    ev_lru_gate_w = nrm(ks[18], (N_EVEN, 2, 2, LRU_BLOCKS, LRU_BW, LRU_BW), LRU_BW ** -0.5)
    ev_lru_gate_b = nrm(ks[19], (N_EVEN, 2, 2, LRU_W), 0.02)
    a_c = jax.random.uniform(ks[20], (N_EVEN, 2, LRU_W), F32, 0.9, 0.999)
    sig = a_c ** (1.0 / LRU_C)
    ev_lru_lambda = jnp.log(sig) - jnp.log1p(-sig)
    od_w_qkv = nrm(ks[21], (N_ODD, D_MODEL, 3 * D_MODEL), D_MODEL ** -0.5)
    od_lambda = nrm(ks[22], (N_ODD, 4, DIFF_D), 0.1)
    od_subln = 1.0 + nrm(ks[23], (N_ODD, DIFF_DV), 0.02)
    return {'x': x, 'c': c, 'ctx': ctx, 'c_ctx': c_ctx, 'ada_w': ada_w, 'ada_b': ada_b,
            'ln_g': ln_g, 'ln_b': ln_b, 'mlp_w1': mlp_w1, 'mlp_w2': mlp_w2, 'mix_w_out': mix_w_out,
            'ev_w_in': ev_w_in, 'ev_qkv_conv': ev_qkv_conv, 'ev_a_log': ev_a_log, 'ev_dt_bias': ev_dt_bias,
            'ev_gdn_norm': ev_gdn_norm, 'ev_lru_conv_w': ev_lru_conv_w, 'ev_lru_conv_b': ev_lru_conv_b,
            'ev_lru_gate_w': ev_lru_gate_w, 'ev_lru_gate_b': ev_lru_gate_b, 'ev_lru_lambda': ev_lru_lambda,
            'od_w_qkv': od_w_qkv, 'od_lambda': od_lambda, 'od_subln': od_subln}

def reference(x, c, ctx, c_ctx, ada_w, ada_b, ln_g, ln_b, mlp_w1, mlp_w2, mix_w_out,
              ev_w_in, ev_qkv_conv, ev_a_log, ev_dt_bias, ev_gdn_norm, ev_lru_conv_w, ev_lru_conv_b,
              ev_lru_gate_w, ev_lru_gate_b, ev_lru_lambda, od_w_qkv, od_lambda, od_subln):
    n_lat = x.shape[1]
    rows = n_lat // GRID_W
    row = jnp.repeat(jnp.arange(rows), GRID_W)
    col = jnp.tile(jnp.arange(GRID_W), rows)
    cos, sin = _axial_rope_tables(row, col)
    silu_c = jax.nn.silu(c)
    silu_cc = jax.nn.silu(c_ctx)
    h_lat, h_ctx = x, ctx
    for i in range(DEPTH):
        last = i == DEPTH - 1
        m_l = [m[:, None, :] for m in jnp.split(silu_c @ ada_w[i] + ada_b[i], 6, axis=-1)]
        m_c = jnp.split(silu_cc @ ada_w[i] + ada_b[i], 6, axis=-1)
        u_l = _modulate(h_lat, m_l[0], m_l[1])
        u_c = _modulate(h_ctx, m_c[0], m_c[1])
        j = i // 2
        if i % 2 == 0:
            y_c, y_l = _even_mixer(u_c, u_l, ev_w_in[j], mix_w_out[i], ev_qkv_conv[j], ev_a_log[j],
                                   ev_dt_bias[j], ev_gdn_norm[j], ev_lru_conv_w[j], ev_lru_conv_b[j],
                                   ev_lru_gate_w[j], ev_lru_gate_b[j], ev_lru_lambda[j], not last)
        else:
            y_c, y_l = _diff_mixer(u_c, u_l, od_w_qkv[j], mix_w_out[i], od_lambda[j], od_subln[j],
                                   cos, sin, i, not last)
        h_lat = _layernorm(DEEPNORM_ALPHA * h_lat + m_l[2] * y_l, ln_g[i, 0], ln_b[i, 0])
        f_l = _mlp(_modulate(h_lat, m_l[3], m_l[4]), mlp_w1[i], mlp_w2[i])
        h_lat = _layernorm(DEEPNORM_ALPHA * h_lat + m_l[5] * f_l, ln_g[i, 1], ln_b[i, 1])
        if not last:
            h_ctx = _layernorm(DEEPNORM_ALPHA * h_ctx + m_c[2] * y_c, ln_g[i, 0], ln_b[i, 0])
            f_c = _mlp(_modulate(h_ctx, m_c[3], m_c[4]), mlp_w1[i], mlp_w2[i])
            h_ctx = _layernorm(DEEPNORM_ALPHA * h_ctx + m_c[5] * f_c, ln_g[i, 1], ln_b[i, 1])
    return h_lat


_drawn_inputs = setup_inputs


def setup_inputs(seed=0):
    import zlib

    import numpy as np

    out = dict(_drawn_inputs(seed))
    spreads = {}
    factors = {'ev_a_log': 7.06,
     'ev_dt_bias': 3.977,
     'ev_gdn_norm': 49.096,
     'ev_lru_conv_b': 5.166,
     'ev_lru_gate_b': 45.725,
     'od_lambda': 8.0,
     'od_subln': 43.002}
    for name, (base, spread) in spreads.items():
        noise = np.random.default_rng([zlib.crc32(name.encode()), seed]).standard_normal(out[name].shape)
        drawn = base * np.exp(spread * noise) if base else spread * noise
        out[name] = __import__('jax').numpy.asarray(drawn.astype(out[name].dtype))
    for name, factor in factors.items():
        out[name] = (out[name] * factor).astype(out[name].dtype)
    return out
```

```python
import math
from contextlib import ExitStack

import numpy as np
import concourse.bass as bass
from concourse import mybir

F32 = mybir.dt.float32
F32R = mybir.dt.float32r
ACT = mybir.ActivationFunctionType
ALU = mybir.AluOpType
AX = mybir.AxisListType

P = 128
D = 1024
KD = D // P
CTX, LAT = 256, 512
TOK = CTX + LAT
NT = TOK // P
DFF = 4 * D
HEADS = 4
GAP = 2
CW = TOK + GAP
LO = CTX + GAP
EPS = 1e-6
ALPHA = 4 ** 0.25
LAM_INIT = 0.8 - 0.6 * math.exp(-0.3)
QC, KC, VC, ZC, AC, XC, GC = 0, 512, 1024, 1536, 2048, 2064, 2576
GELU0 = math.sqrt(2 / math.pi)
GELU1 = GELU0 * 0.044715
LEVELS = 6
BWD_TILE = [1, 0, 5, 4, 3, 2]
PIECES = [(0, CTX, 0), (CTX, TOK, 1)]


def gdn_constants():
    j, i = np.arange(P)[:, None], np.arange(P)[None, :]
    same = (j // 64) == (i // 64)
    out = [(j <= i) & same, (j >= i) & same,
           (j % 64 == 63) & same, (j % 64 == 0) & same]
    for first in (63, 64, 127, 0):
        out.append(np.broadcast_to(j == first, (P, P)))
    out += [(j <= i) & same, (j >= i) & same]
    for lev in range(LEVELS):
        b = 1 << lev
        blk = (j // (2 * b)) == (i // (2 * b))
        out.append(blk & ((i // b) % 2 == 1) & ((j // b) % 2 == 0))
        out.append(blk & ((i // b) % 2 == 0) & ((j // b) % 2 == 1))
    return np.stack(out, 1).astype(np.float32)


def rope_constants():
    half = 32
    inv = (np.float32(10000.0) ** (-(np.arange(0, half, 2, dtype=np.float32) / np.float32(half)))).astype(np.float32)
    t = np.arange(LAT)
    ar = (t // 64).astype(np.float32)[:, None] * inv
    ac = (t % 64).astype(np.float32)[:, None] * inv
    ang = np.concatenate([ar, ar, ac, ac], -1).T.astype(np.float32)
    ang = np.concatenate([ang, ang], 0)
    rot = np.zeros((P, P), np.float32)
    for m in range(P):
        if (m // 16) % 2 == 0:
            rot[m + 16, m] = -1.0
        else:
            rot[m - 16, m] = 1.0
    return np.concatenate([rot, np.cos(ang), np.sin(ang)], 1).astype(np.float32)


CG_CUM, CG_LAST, CG_ROW, CG_INCL, CG_LEV = 0, 2, 4, 8, 10
NG = 10 + 2 * LEVELS


def trunk(nc, I, out, dbg=None):
    with ExitStack() as ctx:
        def at(name, kb, shape, dt=F32):
            return nc.alloc_sbuf_tensor_at(name, shape, dt, offset=int(kb * 1024))

        def sems(names):
            return [ctx.enter_context(nc.semaphore(n)) for n in names.split()]

        ident = at("ident", 2, [P, P])
        ones = at("ones", 2.5, [P, P])
        prmA = at("prmA", 3, [P, 112])
        prmB = at("prmB", 3.5, [P, 46])
        ada = at("ada", 3.75, [P, 96, 2])
        convw = at("convw", 4.5, [P, 48])
        sil = at("sil", 4.75, [P, 2, KD])
        nlam = at("nlam", 4.875, [P, 8])
        subg = at("subg", 4.9375, [P, 2])
        silt = at("silt", 5, [P, 2, KD])
        cols = at("cols", 5.125, [P, 2, KD])
        onesD = at("onesD", 5.25, [P, P])
        eps2 = at("eps2", 5.8125, [P, 2])
        hT = at("hT", 6, [P, KD, TOK])
        raw = at("raw", 30, [P, 2, KD, 256])
        whi = at("whi", 46, [P, 2, KD, P], F32R)
        wlo = at("wlo", 54, [P, 2, KD, P], F32R)
        uhi = at("uhi", 62, [P, KD, TOK], F32R)
        ulo = at("ulo", 86, [P, KD, TOK], F32R)
        uf = at("uf", 110, [P, 2, TOK])
        adab = at("adab", 1.125, [P, 96])
        csp = at("csp", 1.5, [P, KD, 4], F32R)
        sel = at("sel", 1.75, [4, 2])
        grow = at("grow", 111.5, [4, 2, 512])
        xtok = at("xtok", 116, [P, NT, D])
        aw = at("aw", 140, [P, 2, KD, 512])
        arow = at("arow", 172, [2, 2, 512])
        rowsA = at("rowsA", 177, [P, P])
        rowsB = at("rowsB", 177.5, [P, P])
        rowsC = at("rowsC", 178, [P, P])
        araw = [at("araw0", 140, [P, 3, KD, P]), at("araw1", 176.5, [P, 3, KD, P])]
        ahi = at("ahi", 116, [P, 3, KD, P], F32R)
        alo = at("alo", 128, [P, 3, KD, P], F32R)
        zT = at("zT", 116, [P, 4, TOK])
        gT = at("gT", 128, [P, 4, TOK])
        xrT = at("xrT", 140, [P, 4, CW])
        qtok = at("qtok", 152.5, [P, NT, HEADS, P])
        ktok = at("ktok", 164.5, [P, NT, HEADS, P])
        vtok = at("vtok", 176.5, [P, NT, HEADS, P])
        cbuf = at("cbuf", 188.5, [P, 2, CW + 3])
        ybuf = at("ybuf", 194.75, [P, 2, CW])
        tbuf = at("tbuf", 201, [P, 2, CW])
        wab = at("wab", 110, [P, KD, 16])
        wabhi = at("wabhi", 110.5, [P, KD, 16], F32R)
        wablo = at("wablo", 111, [P, KD, 16], F32R)
        nsq = at("nsq", 196.5, [P, 2, P])
        abT = at("abT", 197.75, [16, TOK])
        sm = at("sm", 111.5, [P, 1150])
        la = at("la", 62, [P, 4, TOK])
        lw = at("lw", 74, [P, 4, TOK])
        lx = at("lx", 86, [P, 4, TOK])
        trr = [at("trr0", 98, [P, TOK]), at("trr1", 54, [P, TOK])]
        tii = [at("tii0", 101, [P, TOK]), at("tii1", 57, [P, TOK])]
        thh = [at("thh0", 104, [P, TOK]), at("thh1", 197, [P, TOK])]
        aa2 = [at("aa20", 107, [P, TOK]), at("aa21", 200, [P, TOK])]
        gw = at("gw", 188.5, [P, 16, P])
        yl = at("yl", 42, [P, 4, TOK])
        gc = at("gc", 30, [P, NG, P])
        kT = at("kT", 41, [P, HEADS, TOK])
        qT = at("qT", 53, [P, HEADS, TOK])
        dg = [at(f"dg{d}", 65 + 16 * d, [P, 4, P]) for d in range(2)]
        dm = [at(f"dm{d}", 67 + 16 * d, [P, 4, P]) for d in range(2)]
        att = [at(f"att{d}", 69 + 16 * d, [P, 4, P]) for d in range(2)]
        ot = [[at(f"ot{d}{e}", 71 + 2 * e + 16 * d, [P, 4, P]) for e in range(2)] for d in range(2)]
        xx = [at(f"xx{d}", 75 + 16 * d, [P, 4, P]) for d in range(2)]
        xt = [at(f"xt{d}", 77 + 16 * d, [P, 4, P]) for d in range(2)]
        pm = [at(f"pm{d}", 79 + 16 * d, [P, 4, P]) for d in range(2)]
        tt = [at(f"tt{d}", 97 + 2 * d, [P, 4, P]) for d in range(2)]
        wt = [at(f"wt{d}", 101 + 2 * d, [P, 4, P]) for d in range(2)]
        kd = [at(f"kd{d}", 105 + 2 * d, [P, 4, P]) for d in range(2)]
        bv = at("bv0", 109, [P, 4, P])
        bv = [bv, at("bv1", 116 + 88.5, [P, 4, P])]
        qk = [[at(f"qk{d}{b}", 188.5 + 4 * d + 2 * b, [P, 4, P]) for b in range(2)] for d in range(2)]
        qd = [[at(f"qd{d}{b}", 196.5 + 4 * d + 2 * b, [P, 4, P]) for b in range(2)] for d in range(2)]
        S = at("S", 140, [P, 8, P])
        vn = [at(f"vn{s}", 144 + 4 * s, [P, 8, P]) for s in range(2)]
        oT = at("oT", 152.5, [P, HEADS, TOK])
        osq = at("osq", 140, [P, HEADS, TOK])
        eps1 = at("eps1", 1.875, [P, 1])
        k1 = at("k1", 116, [P, KD, TOK])
        v1 = at("v1", 140, [P, NT, D])
        q1 = at("q1", 164, [P, KD, LAT])
        kb = at("kb", 180, [P, 2, TOK])
        rc = at("rc", 186, [P, P + 2 * LAT])
        rt1 = at("rt1", 191, [P, LAT])
        rt2 = at("rt2", 193, [P, LAT])
        pp = at("pp", 180, [P, 2, 2, TOK])
        pc = at("pc", 192, [P, 2, TOK])
        pT = at("pT", 198, [P, 2, TOK])
        nmx = at("nmx", 204, [P, 2, 2])
        rsm = at("rsm", 204.125, [P, 2, 2])
        rrc = at("rrc", 204.25, [P, 2, 2])
        oo = at("oo", 62, [P, 4, D])
        ors = at("ors", 204.5, [P, 2, 32])
        oq = at("oq", 205, [P, 2, P])
        y1 = at("y1", 116, [P, KD, LAT])
        h1hi = at("h1hi", 116, [P, KD, TOK], F32R)
        h1lo = at("h1lo", 140, [P, KD, TOK], F32R)
        rt = at("rt", 164, [P, 2, TOK])
        hh = at("hh", 170, [P, 2, TOK])
        lsq = at("lsq", 176, [P, 2, TOK])
        lstd = at("lstd", 182, [P, TOK])
        lrs = at("lrs", 185, [P, TOK])
        acc = at("acc", 198, [P, TOK])
        lrow = at("lrow", 195.5, [P, 2 * P])
        otok = at("otok", 116, [P, 4, D])

        G = ctx.enter_context(nc.psum_tensor("G", [P, 4, 512], F32))
        X = ctx.enter_context(nc.psum_tensor("X", [P, 4, 512], F32))
        Gf = G[:].rearrange("p a b -> p (a b)")
        Xf = X[:].rearrange("p a b -> p (a b)")

        (const_in, ones_ready, rows_in, cols_in, x_in, sil_t, sil_ready, rows_mm, prm_ready, tr_x, h0_ready) = sems(
            "const_in ones_ready rows_in cols_in x_in sil_t sil_ready rows_mm prm_ready tr_x h0_ready")
        ada_in = sems("ada_in0 ada_in1")
        araw_in = sems("araw_in0 araw_in1 araw_in2 araw_in3 araw_in4 araw_in5")
        (csp_hi, csp_lo, a_hi, a_lo_pool, a_lo_dve, a_mm, a_row, a_col) = sems("csp_hi csp_lo a_hi a_lo_pool a_lo_dve a_mm a_row a_col")
        (ada_mm, ada_row, ada_col, ada_ready) = sems("ada_mm ada_row ada_col ada_ready")
        (uf_ready, uhi_ready, ulo_ready) = sems("uf_ready uhi_ready ulo_ready")
        raw_in = sems("raw_in0 raw_in1")
        (w_hi, w_lo, mm_done, evac_done, res_done) = sems("w_hi w_lo mm_done evac_done res_done")
        (pad_zero, conv_step, tanh_done, silu_done, tr_done, tok_done, z_tanh, z_done, g_sq, g_in, g_tanh, g_done) = sems(
            "pad_zero conv_step tanh_done silu_done tr_done tok_done z_tanh z_done g_sq g_in g_tanh g_done")
        (ab_rows, wab_in, wab_hi, wab_lo, ab_mm, ab_ready, bc_in) = sems("ab_rows wab_in wab_hi wab_lo ab_mm ab_ready bc_in")
        (dve_chain, act_chain, act_small, dve_small, cum_mm, gates_mm, gates_ready, gate_tanh, lru_at, lru_w, lru_sqrt, lru_y,
         gw_zero, gw_in) = sems(
            "dve_chain act_chain act_small dve_small cum_mm gates_mm gates_ready gate_tanh lru_at lru_w lru_sqrt lru_y gw_zero gw_in")
        (gc_in, nsq_ready, ss_ready, qkn_ready, qkT_mm, qkT_ready, state_zero) = sems(
            "gc_in nsq_ready ss_ready qkn_ready qkT_mm qkT_ready state_zero")
        (gd_row, gd_g, gd_exp, gd_diff, gd_dec, gd_dmask, gd_at0, gd_brow, gd_qk, gd_qk_ready, gd_at, gd_qd) = sems(
            "gd_row gd_g gd_exp gd_diff gd_dec gd_dmask gd_at0 gd_brow gd_qk gd_qk_ready gd_at gd_qd")
        (lv_ot, lv_p, lv_pm, lv_e, lv_et, lv_x, lv_xt, bk_ready, kd_ready, bv_ready, wt_mm, wt_ready) = sems(
            "lv_ot lv_p lv_pm lv_e lv_et lv_x lv_xt bk_ready kd_ready bv_ready wt_mm wt_ready")
        (ch_v, ch_vnf, ch_vnb, ch_s, ch_o, ch_state, ch_out) = sems("ch_v ch_vnf ch_vnb ch_s ch_o ch_state ch_out")
        (o_sq, o_ms, o_std, o_z, o_y, glo_ready) = sems("o_sq o_ms o_std o_z o_y glo_ready")
        (ln_mean, ln_xc, ln_sq, ln_var, ln_std, ln_rstd, ln_xn, ln_h) = sems(
            "ln_mean ln_xc ln_sq ln_var ln_std ln_rstd ln_xn ln_h")
        (acc_step,) = sems("acc_step")
        (sq_sum, rn_sqrt) = sems("sq_sum rn_sqrt")
        (relu_done, hh_done, h1hi_done, h1lo_done) = sems("relu_done hh_done h1hi_done h1lo_done")
        (rope_in, lam_in, lam_ready, rot_mm, rope_step, kq_ready, vtr_mm, v_ready) = sems(
            "rope_in lam_in lam_ready rot_mm rope_step kq_ready vtr_mm v_ready")
        (sc_mm, mx_ready, ex_ready, pc_ready, pt_mm, pt_ready, pv_mm, o_ready) = sems(
            "sc_mm mx_ready ex_ready pc_ready pt_mm pt_ready pv_mm o_ready")
        (osq1, oss1, on_ready, ot_mm, y1_ready) = sems("osq1 oss1 on_ready ot_mm y1_ready")
        (fin_mm, fin_ready, out_done) = sems("fin_mm fin_ready out_done")

        U_OUT0, U_MLP0, U_QKV, U_OUT1, U_MLP1, U_END = 24, 32, 96, 120, 128, 192
        R_OUT0, R_MLP0, R_OUT1, R_MLP1 = 0, 8, 40, 48
        E_QKV = 24
        EV_COLS = [c + 256 * t for c, n in ((QC, 6), (XC, 2), (ZC, 2), (GC, 2)) for t in range(n)]

        def pair_source(n):
            def view(w, r0, c0):
                return w[r0:r0 + D, c0:c0 + 256].rearrange("(k p) n -> p k n", p=P)
            u = 2 * n
            if u < U_OUT0:
                return view(I["ev_w_in"][0], 0, EV_COLS[n])
            if u < U_MLP0:
                return view(I["mix_w_out"][0], 0, 256 * (n - U_OUT0 // 2))
            if U_QKV <= u < U_OUT1:
                j = n - U_QKV // 2
                return view(I["od_w_qkv"][0], 0, (D + 256 * j) if j < 8 else 256 * (j - 8))
            if U_OUT1 <= u < U_MLP1:
                return view(I["mix_w_out"][1], 0, 256 * (n - U_OUT1 // 2))
            layer, m = (0, n - U_MLP0 // 2) if u < U_QKV else (1, n - U_MLP1 // 2)
            quarter, j = m // 8, m % 8
            if j < 4:
                return view(I["mlp_w1"][layer], 0, D * quarter + 256 * j)
            return view(I["mlp_w2"][layer], D * quarter, 256 * (j - 4))

        ADA0 = 4
        ADA1 = 16
        ADAN = 96 - ADA1
        ADA_PER = KD
        A_UNITS = ADAN // ADA_PER
        assert A_UNITS <= 10

        def a_by_pool(i):
            return i % 2 == 0

        def ada_tiles(u):
            return range(ADA_PER * u, ADA_PER * (u + 1)) if u < A_UNITS else ()

        def a_buf(i):
            return araw[i % 6 // 3][:, i % 3]

        def wait_a_lo(eng, i):
            if a_by_pool(i):
                eng.wait_ge(a_lo_pool, i // 2 + 1)
            else:
                eng.wait_ge(a_lo_dve, i // 2 + 1)

        block = ctx.enter_context(nc.Block())

        def small(o, n):
            return sm[:, o:o + n]
        abS = small(0, 96).rearrange("p (t w d h) -> p t w d h", t=6, w=2, d=2)
        spx = small(96, 56)
        spa, spz, sps, spp, spm = (small(152 + 56 * q, 56) for q in range(5))
        gS = small(432, 48)
        bS = small(480, 48)
        gamS = small(528, 48)
        glS = small(576, 48)
        bES = small(624, 48)
        cdS = small(672, 96)
        rnS = small(768, 48)
        hbS = small(816, 16)
        hsS = small(832, 8)
        nhsS = small(840, 8)
        albc = small(848, 8)
        dtbc = small(856, 8)
        ssS = small(864, 48)

        def m3(ap, a):
            return ap.rearrange("p (t r) -> p t r", t=a)

        def bc_cols(ap4):
            return ap4.unsqueeze(2).to_broadcast([P, 4, P])

        def bc_mask(ap):
            return ap.unsqueeze(1).to_broadcast([P, 4, P])

        ADA_LAT, ADA_CTX = 0, 1

        def adacol(layer, q, k, who):
            return ada[:, layer * 48 + q * 8 + k, who:who + 1]

        def half_of(d, s):
            return s if d == 0 else 1 - s

        def tile_of(d, p):
            return p if d == 0 else BWD_TILE[p]

        @block.sync
        def _(sp):
            sp.dma_start(ident[:], I["c_eye"]).then_inc(const_in, 16)
            sp.dma_start(sel[0:2], I["c_eye"][0:2, 0:2]).then_inc(const_in, 16)
            sp.dma_start(sel[2:4], I["c_eye"][0:2, 0:2]).then_inc(const_in, 16)
            sp.dma_start(cols[:, 0], I["c"][0].rearrange("(p j) -> p j", p=P)).then_inc(cols_in, 16)
            sp.dma_start(cols[:, 1], I["c_ctx"].rearrange("(p j) -> p j", p=P)).then_inc(cols_in, 16)

            def load_ada(n):
                if n >= 2:
                    sp.wait_ge(ada_mm, n - 1)
                sp.dma_start(aw[:, n % 2], I["ada_w"][n // 12].rearrange("(p j) n -> p j n", p=P)[
                    :, :, (n % 12) * 512:(n % 12 + 1) * 512]).then_inc(ada_in[n % 2], 16)

            load_ada(0)
            sp.dma_start(xtok[:, 0:2], I["ctx"][0].rearrange("(t p) d -> p t d", p=P)).then_inc(x_in, 16)
            sp.dma_start(xtok[:, 2:6], I["x"][0].rearrange("(t p) d -> p t d", p=P)).then_inc(x_in, 16)
            load_ada(1)
            sp.dma_start(rowsA[0:32], I["ln_g"].rearrange("l j (k p) -> (l j k) p", p=P)).then_inc(rows_in, 16)
            sp.dma_start(rowsA[32:64], I["ln_b"].rearrange("l j (k p) -> (l j k) p", p=P)).then_inc(rows_in, 16)
            sp.dma_start(rowsA[64:112], I["ev_qkv_conv"].rearrange("a t (k p) -> (a t k) p", p=P)).then_inc(rows_in, 16)
            sp.dma_start(rowsB[0:16], I["ev_lru_conv_w"].rearrange("a t (k p) -> (a t k) p", p=P)).then_inc(rows_in, 16)
            sp.dma_start(rowsB[16:20], I["ev_lru_conv_b"].rearrange("a (k p) -> (a k) p", p=P)).then_inc(rows_in, 16)
            sp.dma_start(rowsB[20:36], I["ev_lru_gate_b"].rearrange("a d g (k p) -> (a d g k) p", p=P)).then_inc(rows_in, 16)
            sp.dma_start(rowsB[36:44], I["ev_lru_lambda"].rearrange("a d (k p) -> (a d k) p", p=P)).then_inc(rows_in, 16)
            sp.dma_start(rowsB[44:45], I["ev_gdn_norm"]).then_inc(rows_in, 16)
            sp.dma_start(rowsB[45:46], I["od_subln"]).then_inc(rows_in, 16)
            sp.dma_start(rowsC[0:96], I["ada_b"].rearrange("l (k p) -> (l k) p", p=P)).then_inc(rows_in, 16)
            for n in range(2, ADA0):
                load_ada(n)
            def load_pair(n):
                if n >= 2:
                    sp.wait_ge(w_lo, 2 * (n - 1))
                sp.dma_start(raw[:, n % 2], pair_source(n)).then_inc(raw_in[n % 2], 16)

            def load_atile(i):
                if i >= 6:
                    wait_a_lo(sp, i - 6)
                n = ADA1 + i
                sp.dma_start(a_buf(i), I["ada_w"][n // 48].rearrange("(p j) n -> p j n", p=P)[
                    :, :, (n % 48) * P:(n % 48 + 1) * P]).then_inc(araw_in[i % 6], 16)

            load_pair(0)
            load_pair(1)
            sp.wait_ge(ada_mm, ADA0)
            sp.wait_ge(prm_ready, 1)
            for i in range(6):
                load_atile(i)
            sp.wait_ge(ulo_ready, 8)
            sp.dma_start(wab[:], I["ev_w_in"][0][:, AC:AC + 16].rearrange("(k p) n -> p k n", p=P)).then_inc(wab_in, 16)
            for u in range(A_UNITS):
                for j in range(ADA_PER):
                    if ADA_PER * u + j + 6 < ADAN:
                        load_atile(ADA_PER * u + j + 6)
                    if u % 2 == 0 and j == 2:
                        load_pair(u // 2 + 2)
            sp.wait_ge(a_col, ADAN // 4)
            sp.dma_start(albc, I["ev_a_log"].rearrange("a d h -> a (d h)").to_broadcast([P, 8])).then_inc(bc_in, 16)
            sp.dma_start(dtbc, I["ev_dt_bias"].rearrange("a d h -> a (d h)").to_broadcast([P, 8])).then_inc(bc_in, 16)

            for n in range(A_UNITS // 2 + 2, U_OUT0 // 2):
                load_pair(n)
            sp.wait_ge(gw_zero, 1)
            for e in range(2):
                for d in range(2):
                    for g in range(2):
                        sp.dma_start(gw[64 * e:64 * e + 64, (2 * d + g) * 4:(2 * d + g) * 4 + 4, 64 * e:64 * e + 64],
                                     I["ev_lru_gate_w"][0, d, g].rearrange("(c e) i j -> e i c j", e=2)[e]).then_inc(gw_in, 16)
            sp.wait_ge(w_lo, U_OUT0)
            sp.dma_start(gc[:], I["c_gdn"]).then_inc(gc_in, 16)
            sp.wait_ge(wt_ready, 12)
            for n in range(U_OUT0 // 2, U_QKV // 2 + 2):
                load_pair(n)
            sp.wait_ge(ln_h, 16)
            sp.dma_start(rc[:], I["c_rope"]).then_inc(rope_in, 16)
            sp.dma_start(lrow[:], I["od_lambda"].rearrange("a r d -> a (r d)").to_broadcast([P, 256])).then_inc(lam_in, 16)
            for n in range(U_QKV // 2 + 2, U_END // 2):
                load_pair(n)
            for t in range(4):
                sp.wait_ge(fin_ready, 2 * (t + 1))
                sp.dma_start(out[0, t * P:(t + 1) * P, :], otok[:, t]).then_inc(out_done, 16)
            sp.wait_ge(out_done, 64)

        @block.gpsimd
        def _(pool):
            nc.gpsimd.memset(ones[:], 1.0).then_inc(ones_ready, 1)
            nc.gpsimd.memset(eps2[:], EPS / ALPHA ** 2).then_inc(ones_ready, 1)
            nc.gpsimd.memset(onesD[:], 1.0 / D).then_inc(ones_ready, 1)
            nc.gpsimd.memset(eps1[:], EPS).then_inc(ones_ready, 1)

            def modulate(m, ubase, layer, qs, span, ready, n_ready):
                for k in range(KD):
                    pool.wait_ge(ready, n_ready + k + 1)
                    if ubase or k >= 2:
                        pool.wait_ge(ulo_ready, ubase + max(0, k - 1))
                    for s, e, bank in PIECES:
                        if s >= span[0]:
                            who = ADA_CTX if bank == 0 else ADA_LAT
                            last = nc.gpsimd.tensor_scalar(uf[:, k % 2, s:e], hT[:, k, s:e], adacol(layer, qs + 1, k, who),
                                                           adacol(layer, qs, k, who), ALU.mult, ALU.add)
                    last.then_inc(uf_ready, 1)

            def sum_tiles(c, span, rbase):
                a, b = span
                for k in range(1, KD - 1):
                    pool.wait_ge(res_done, rbase + k + 1)
                    if k == 1:
                        if c:
                            pool.wait_ge(ln_mean, c)
                        first = hT[:, 0, a:b]
                    else:
                        pool.wait_ge(acc_step, 6 * c + k - 1)
                        first = acc[:, a:b]
                    nc.gpsimd.tensor_tensor(acc[:, a:b], first, hT[:, k, a:b], ALU.add).then_inc(acc_step, 1)

            pool.wait_ge(ada_ready, 2)
            modulate(0, 0, 0, 0, (0, TOK), h0_ready, 0)
            pool.wait_ge(ulo_ready, 8)
            nc.gpsimd.memset(cbuf[:], 0.0).then_inc(pad_zero, 1)
            for i in range(ADAN):
                if a_by_pool(i):
                    pool.wait_ge(a_hi, i + 1)
                    nc.gpsimd.tensor_tensor(alo[:, i % 3], a_buf(i), ahi[:, i % 3].bitcast(F32),
                                            ALU.subtract).then_inc(a_lo_pool, 1)
            pool.wait_ge(tok_done, 12)
            pool.wait_ge(conv_step, 64)
            nc.gpsimd.memset(gw[:], 0.0).then_inc(gw_zero, 1)
            pool.wait_ge(lru_y, 8)
            nc.gpsimd.memset(vn[0][:], 0.0).then_inc(state_zero, 1)
            nc.gpsimd.memset(vn[1][:], 0.0).then_inc(state_zero, 1)
            nc.gpsimd.memset(S[:], 0.0).then_inc(state_zero, 1)
            pool.wait_ge(gc_in, 16)

            for p in range(6):
                for d in range(2):
                    n = 2 * p + d
                    t = tile_of(d, p)
                    pool.wait_ge(gd_exp, n + 1)
                    pool.wait_ge(qkT_ready, 12)
                    nc.gpsimd.tensor_tensor(qd[d][p % 2][:], qd[d][p % 2][:], qT[:, :, t * P:(t + 1) * P],
                                            ALU.mult).then_inc(gd_qd, 1)
                for lev in range(LEVELS):
                    for d in range(2):
                        n = 2 * p + d
                        pool.wait_ge(gd_at, n + 1)
                        if lev >= 2 or p > 0:
                            pool.wait_ge(lv_p, 2 * (LEVELS * p + lev - 2) + d + 1)
                        if lev == 2:
                            pool.wait_ge(lv_xt, 2 * LEVELS * p + d + 1)
                        nc.gpsimd.tensor_tensor(ot[d][lev % 2][:], att[d][:], bc_mask(gc[:, CG_LEV + 2 * lev + d]),
                                                ALU.mult).then_inc(lv_ot, 1)
                for d in range(2):
                    n = 2 * p + d
                    t = tile_of(d, p)
                    r = slice(4 * d, 4 * d + 4)
                    if p > 0:
                        pool.wait_ge(wt_mm, n - 1)
                    nc.gpsimd.tensor_tensor(dg[d][:], ktok[:, t], bc_cols(m3(bES, 6)[:, p, r]), ALU.mult).then_inc(bk_ready, 1)
                    if p > 0:
                        pool.wait_ge(ch_o, 2 * p)
                    nc.gpsimd.tensor_tensor(kd[d][:], ktok[:, t], bc_cols(m3(glS, 6)[:, p, r]), ALU.mult).then_inc(kd_ready, 1)
                    nc.gpsimd.tensor_tensor(bv[d][:], vtok[:, t], bc_cols(m3(bS, 6)[:, p, r]), ALU.mult).then_inc(bv_ready, 1)

            for k in range(4, KD):
                pool.wait_ge(ch_o, 12)
                pool.wait_ge(uhi_ready, 8 + k - 3)
                nc.gpsimd.tensor_tensor(ulo[:, k], gT[:, k % 4], uhi[:, k].bitcast(F32), ALU.subtract).then_inc(glo_ready, 1)

            pool.wait_ge(ada_ready, 5)
            sum_tiles(0, (0, TOK), R_OUT0)
            modulate(1, 16, 0, 3, (0, TOK), ln_h, 0)
            sum_tiles(1, (0, TOK), R_MLP0 + 24)
            modulate(2, 24, 1, 0, (0, TOK), ln_h, 8)
            sum_tiles(2, (CTX, TOK), R_OUT1)
            modulate(3, 40, 1, 3, (CTX, TOK), ln_h, 16)
            sum_tiles(3, (CTX, TOK), R_MLP1 + 24)

        @block.scalar
        def _(act):
            chain = [0]

            def link(ins):
                chain[0] += 1
                ins.then_inc(act_chain, 1)
                act.wait_ge(act_chain, chain[0])

            def split_hi(par, unit):
                act.wait_ge(raw_in[(par // 2) % 2], 16 * (unit // 4 + 1))
                if unit >= 2:
                    act.wait_ge(mm_done, unit - 1)
                nc.scalar.activation(whi[:, par % 2], raw[:, (par // 2) % 2, :, (par % 2) * P:(par % 2 + 1) * P],
                                     ACT.Copy).then_inc(w_hi, 1)

            def slot(par, piece):
                start, stop, bank = piece
                return G[:, 2 * (par % 2) + bank, 0:stop - start]

            act.wait_ge(cols_in, 32)
            nc.scalar.activation(silt[:], cols[:], ACT.Tanh, scale=0.5).then_inc(sil_t, 1)
            for k in range(KD):
                act.wait_ge(tr_x, k + 1)
                for pc_ in PIECES:
                    last = nc.scalar.activation(hT[:, k, pc_[0]:pc_[1]], slot(k, pc_), ACT.Copy)
                last.then_inc(h0_ready, 1)
            act.wait_ge(sil_ready, 1)
            nc.scalar.activation(csp[:, :, 0:2], sil[:].rearrange("p w k -> p k w"), ACT.Copy).then_inc(csp_hi, 1)
            for n in range(ADA0):
                act.wait_ge(ada_mm, n + 1)
                if n >= 2:
                    act.wait_ge(ada_col, n - 1)
                nc.scalar.activation(arow[:, n % 2], X[0:2, n % 2, :], ACT.Copy).then_inc(ada_row, 1)

            def round_u(m, k, span, units):
                act.wait_ge(uf_ready, 8 * m + k + 1)
                if units:
                    act.wait_ge(mm_done, units)
                nc.scalar.activation(uhi[:, k, span[0]:span[1]], uf[:, k % 2, span[0]:span[1]], ACT.Copy).then_inc(uhi_ready, 1)

            def ada_hi(i):
                act.wait_ge(araw_in[i % 6], 16 * (i // 6 + 1))
                if i >= 3:
                    act.wait_ge(a_mm, i - 2)
                nc.scalar.activation(ahi[:, i % 3], a_buf(i), ACT.Copy).then_inc(a_hi, 1)

            split_hi(0, 0)
            for k in range(KD):
                round_u(0, k, (0, TOK), 0)
                if k == 4:
                    ada_hi(0)
                if k == 6:
                    ada_hi(1)
            act.wait_ge(wab_in, 16)
            nc.scalar.activation(wabhi[:], wab[:], ACT.Copy).then_inc(wab_hi, 1)

            def ada_rows(g):
                act.wait_ge(a_mm, 4 * g + 4)
                if g >= 2:
                    act.wait_ge(a_col, g - 1)
                nc.scalar.activation(grow[:, g % 2], X[0:4, 3, :], ACT.Copy).then_inc(a_row, 1)

            def ada_his(a, b):
                for i in range(a, min(b, ADAN)):
                    ada_hi(i)
                    if i % 4 == 0 and i > 0:
                        ada_rows(i // 4 - 1)

            def gates_in():
                act.wait_ge(ab_mm, 2)
                psab = X[:, 2, 0:96].rearrange("p (t w d h) -> p t w d h", t=6, w=2, d=2)
                nc.scalar.activation(abS[:, :, :, 0, :], psab[:, :, :, 0, :], ACT.Copy)
                for p in range(6):
                    last = nc.scalar.activation(abS[:, p, :, 1, :], psab[:, BWD_TILE[p], :, 1, :], ACT.Copy)
                last.then_inc(ab_ready, 1)

            def gates_exp():
                act.wait_ge(dve_small, 1)
                nc.scalar.activation(spz, spa, ACT.Exp).then_inc(act_small, 1)
                act.wait_ge(bc_in, 32)
                nc.scalar.activation(albc, albc, ACT.Exp).then_inc(act_small, 1)
                for w in range(6):
                    last = nc.scalar.activation(m3(bS, 6)[:, w].rearrange("p (d h) -> p d h", d=2), abS[:, w, 1], ACT.Tanh,
                                                scale=0.5)
                last.then_inc(act_small, 1)

            act.wait_ge(pad_zero, 1)
            for u in range(U_OUT0 + 2):
                if u + 1 < U_OUT0:
                    split_hi((u + 1) % 4, u + 1)
                if u < A_UNITS:
                    ada_his(ADA_PER * u + 2, ADA_PER * u + 5)
                if 1 <= u <= 12:
                    act.wait_ge(conv_step, 4 * u)
                    if u >= 3:
                        act.wait_ge(silu_done, u - 2)
                    nc.scalar.activation(tbuf[:, (u - 1) % 2], ybuf[:, (u - 1) % 2], ACT.Tanh).then_inc(tanh_done, 1)
                if u < A_UNITS:
                    ada_his(ADA_PER * u + 5, ADA_PER * u + 10)
                if u == A_UNITS - 1:
                    ada_rows(ADAN // 4 - 1)
                if u == 18:
                    act.wait_ge(ab_mm, 1)
                    nc.scalar.activation(abT[:, 0:CTX], X[0:16, 0, 0:CTX], ACT.Copy)
                    nc.scalar.activation(abT[:, CTX:TOK], X[0:16, 1, :], ACT.Copy).then_inc(ab_rows, 1)
                if 14 <= u < 20:
                    act.wait_ge(tok_done, 12)
                    for r in range(8):
                        n = 8 * (u - 14) + r
                        if n >= 2:
                            act.wait_ge(sq_sum, n - 1)
                        src = (qtok, ktok)[r // 4]
                        nc.scalar.activation(nsq[:, n % 2], src[:, u - 14, r % 4], ACT.Square,
                                             accum_out=ssS[:, n:n + 1]).then_inc(sq_sum, 1)
                if u == 20:
                    act.wait_ge(ss_ready, 1)
                    nc.scalar.activation(rnS, ssS, ACT.Sqrt).then_inc(rn_sqrt, 1)
                if u == 19:
                    gates_in()
                if u == 21:
                    gates_exp()
                if 2 <= u <= 13:
                    act.wait_ge(tr_done, u - 1)
                    dst = (qtok, ktok, vtok)[(u - 2) // 4]
                    nc.scalar.activation(dst[:, :, (u - 2) % 4, :], Xf[:, 0:TOK].rearrange("p (t c) -> p t c", t=NT),
                                         ACT.Copy).then_inc(tok_done, 1)
                if u >= U_OUT0:
                    continue
                act.wait_ge(mm_done, u + 1)
                if u < 16:
                    if u >= 2:
                        act.wait_ge(conv_step, 4 * (u - 1))
                    nc.scalar.activation(cbuf[:, u % 2, 2:2 + CTX], slot(u, PIECES[0]), ACT.Copy)
                    nc.scalar.activation(cbuf[:, u % 2, 4 + CTX:4 + TOK], slot(u, PIECES[1]), ACT.Copy).then_inc(evac_done, 1)
                else:
                    dst = zT if u < 20 else gT
                    for pc_ in PIECES:
                        last = nc.scalar.activation(dst[:, u % 4, pc_[0]:pc_[1]], slot(u, pc_), ACT.Copy, scale=0.5)
                    last.then_inc(evac_done, 1)
                    act.wait_ge(evac_done, u + 1)
                    if u < 20:
                        if u >= 18:
                            act.wait_ge(z_done, u - 17)
                        else:
                            act.wait_ge(silu_done, 12)
                        nc.scalar.activation(tbuf[:, u % 2, 0:TOK], zT[:, u % 4], ACT.Tanh).then_inc(z_tanh, 1)
                    else:
                        if u >= 22:
                            act.wait_ge(g_done, u - 21)
                        else:
                            act.wait_ge(z_done, u - 17)
                        nc.scalar.activation(tbuf[:, u % 2, 0:TOK], gT[:, u % 4], ACT.Square).then_inc(g_sq, 1)
                        act.wait_ge(g_in, 2 * (u - 19))
                        nc.scalar.activation(tbuf[:, u % 2, 0:TOK], tbuf[:, u % 2, 0:TOK], ACT.Tanh).then_inc(g_tanh, 1)

            act.wait_ge(dve_small, 4)
            act.wait_ge(cum_mm, 2)
            nc.scalar.activation(glS, glS, ACT.Exp).then_inc(act_small, 1)
            nc.scalar.activation(bES, gamS, ACT.Exp).then_inc(act_small, 1)
            nc.scalar.activation(cdS, X[:, 2, 128:224], ACT.Exp).then_inc(act_small, 1)

            for d in range(2):
                for c in range(4):
                    n = 4 * d + c
                    act.wait_ge(gates_mm, n + 1)
                    act.wait_ge(dve_small, 2)
                    if n >= 2:
                        act.wait_ge(lru_w, n - 1)
                    if d == 1:
                        act.wait_ge(lru_y, c + 1)
                    B = X if n % 2 else G
                    for pc_ in PIECES:
                        nc.scalar.activation(trr[n % 2][:, pc_[0]:pc_[1]], B[:, pc_[2], 0:pc_[1] - pc_[0]], ACT.Tanh, scale=0.5,
                                             bias=hbS[:, (2 * d) * 4 + c:(2 * d) * 4 + c + 1])
                    for pc_ in PIECES:
                        last = nc.scalar.activation(tii[n % 2][:, pc_[0]:pc_[1]], B[:, 2 + pc_[2], 0:pc_[1] - pc_[0]], ACT.Tanh,
                                                    scale=0.5, bias=hbS[:, (2 * d + 1) * 4 + c:(2 * d + 1) * 4 + c + 1])
                    last.then_inc(gate_tanh, 1)
                    act.wait_ge(gate_tanh, n + 1)
                    nc.scalar.activation(la[:, c], trr[n % 2][:], ACT.Exp, scale=hsS[:, n:n + 1], bias=hsS[:, n:n + 1])
                    nc.scalar.activation(thh[n % 2][:], trr[n % 2][:], ACT.Tanh, scale=nhsS[:, n:n + 1],
                                         bias=nhsS[:, n:n + 1]).then_inc(lru_at, 1)
                act.wait_ge(lru_w, 4 * d + 4)
                nc.scalar.activation(lw[:], lw[:], ACT.Sqrt, scale=0.25).then_inc(lru_sqrt, 1)

            act.wait_ge(lru_y, 8)
            for t in range(NT):
                for w, dst in ((0, qT), (1, kT)):
                    act.wait_ge(qkT_mm, 2 * t + w + 1)
                    nc.scalar.activation(dst[:, :, t * P:(t + 1) * P], X[:, w, :].rearrange("p (h c) -> p h c", h=4),
                                         ACT.Copy).then_inc(qkT_ready, 1)

            def chain_act(p, s):
                c = 2 * p + s
                act.wait_ge(ch_v, 2 * c + 1)
                act.wait_ge(state_zero, 3)
                if c >= 2:
                    act.wait_ge(ch_o, c - 1)
                h = 64 * half_of(0, s)
                nc.scalar.activation(vn[s][h:h + 64, 0:4], X[h:h + 64, 0, :].rearrange("p (r c) -> p r c", r=4),
                                     ACT.Copy).then_inc(ch_vnf, 1)

            for p in range(7):
                if p < 6:
                    for d in range(2):
                        n = 2 * p + d
                        act.wait_ge(gd_row, n + 1)
                        if p >= 2:
                            act.wait_ge(ch_o, 2 * (p - 1))
                        nc.scalar.activation(qd[d][p % 2][:], G[:, 2 * d, :].rearrange("p (r c) -> p r c", r=4),
                                             ACT.Exp).then_inc(gd_exp, 1)
                    for d in range(2):
                        n = 2 * p + d
                        act.wait_ge(gd_diff, n + 1)
                        nc.scalar.activation(dm[d][:], dm[d][:], ACT.Exp).then_inc(gd_dec, 1)
                for lev in range(LEVELS):
                    if p < 6 and lev > 0:
                        for d in range(2):
                            act.wait_ge(lv_p, 2 * (LEVELS * p + lev) + d + 1)
                            if lev > 1:
                                act.wait_ge(lv_et, 2 * (5 * p + lev - 2) + d + 1)
                            nc.scalar.activation(pm[d][:], G[:, 2 * d, :].rearrange("p (r c) -> p r c", r=4),
                                                 ACT.Copy).then_inc(lv_pm, 1)
                    if p >= 1 and lev in (1, 3):
                        chain_act(p - 1, lev // 2)
                if p < 6:
                    for d in range(2):
                        n = 2 * p + d
                        act.wait_ge(wt_mm, n + 1)
                        if p >= 1:
                            act.wait_ge(ch_o, 2 * p)
                        nc.scalar.activation(wt[d][:], G[:, 2 * d + 1, :].rearrange("p (r c) -> p r c", r=4), ACT.Copy,
                                             scale=-1.0).then_inc(wt_ready, 1)

            split_hi(0, U_OUT0)
            for k in range(4, KD):
                nc.scalar.activation(uhi[:, k], gT[:, k % 4], ACT.Copy).then_inc(uhi_ready, 1)
            act.wait_ge(ch_out, 12)
            for h in range(HEADS):
                nc.scalar.activation(osq[:, h], oT[:, h], ACT.Square).then_inc(o_sq, 1)
            for h in range(HEADS):
                act.wait_ge(o_ms, h + 1)
                B = (G, X)[h // 2]
                for s, e, bank in PIECES:
                    last = nc.scalar.activation(osq[:, h, s:e], B[:, 2 * (h % 2) + bank, 0:e - s], ACT.Sqrt, scale=1.0 / P,
                                                bias=eps1[:])
                last.then_inc(o_std, 1)
            for k in range(4):
                act.wait_ge(o_y, k + 1)
                nc.scalar.activation(uhi[:, k], oT[:, k], ACT.Copy).then_inc(uhi_ready, 1)
            for j in range(8):
                split_hi((j + 1) % 4, U_OUT0 + j + 1)

            def layer_norm(c, span, m=None, units=0):
                a, b = span
                for k in range(KD):
                    act.wait_ge(ln_xc, 8 * c + k + 1)
                    if k >= 2:
                        act.wait_ge(ln_var, 8 * c + k - 1)
                    nc.scalar.activation(lsq[:, k % 2, a:b], hT[:, k, a:b], ACT.Square).then_inc(ln_sq, 1)
                act.wait_ge(ln_var, 8 * c + 8)
                for s, e, bank in PIECES:
                    if s >= a:
                        last = nc.scalar.activation(lstd[:, s:e], X[:, 2 + bank, 0:e - s], ACT.Sqrt, bias=eps2[:, 0:1])
                last.then_inc(ln_std, 1)
                for k in range(KD):
                    act.wait_ge(ln_xn, 8 * c + k + 1)
                    nc.scalar.activation(hT[:, k, a:b], hT[:, k, a:b], ACT.Identity, scale=prmA[:, c * 8 + k:c * 8 + k + 1],
                                         bias=prmA[:, 32 + c * 8 + k:32 + c * 8 + k + 1]).then_inc(ln_h, 1)
                    if m is not None and k >= 1:
                        round_u(m, k - 1, span, units)
                if m is not None:
                    round_u(m, KD - 1, span, units)

            def mlp(layer, q, span, u0, h0, last_quarter):
                base = u0 + 16 * q
                def split(j):
                    pair_uses = (u0 // 4 + 4 * q) + (j // 4) + 1
                    act.wait_ge(raw_in[(j // 2) % 2], 16 * pair_uses)
                    act.wait_ge(mm_done, base + (j - 1))
                    nc.scalar.activation(whi[:, j % 2], raw[:, (j // 2) % 2, :, (j % 2) * P:(j % 2 + 1) * P],
                                         ACT.Copy).then_inc(w_hi, 1)
                def round_h(j):
                    act.wait_ge(hh_done, h0 + 8 * q + (j + 3))
                    act.wait_ge(mm_done, base)
                    nc.scalar.activation(h1hi[:, j, span[0]:span[1]], hh[:, j % 2, span[0]:span[1]],
                                         ACT.Copy).then_inc(h1hi_done, 1)
                for j in range(8):
                    split(j + 1)
                    act.wait_ge(mm_done, base + (j + 1))
                    act.wait_ge(hh_done, h0 + 8 * q + (j + 1))
                    for s, e, bank in PIECES:
                        if s >= span[0]:
                            last = nc.scalar.activation(rt[:, j % 2, s:e], G[:, 2 * (j % 2) + bank, 0:e - s], ACT.Relu)
                    last.then_inc(relu_done, 1)
                    if j >= 1:
                        round_h(j - 1)
                round_h(7)
                for f in range(8):
                    if not (last_quarter and f == 7):
                        split(8 + f + 1)

            layer_norm(0, (0, TOK), 1, U_MLP0)
            with act.Fori(0, 4) as q:
                mlp(0, q, (0, TOK), U_MLP0, 0, False)
            layer_norm(1, (0, TOK), 2, U_QKV)

            for u in range(U_QKV, U_OUT1):
                j = u - U_QKV
                if u + 1 < U_OUT1 + 1:
                    split_hi((u + 1) % 4, u + 1)
                if 9 <= j <= 16:
                    act.wait_ge(vtr_mm, j - 8)
                    nc.scalar.activation(v1[:, :, (j - 9) * P:(j - 8) * P], Xf[:, 1024:1024 + TOK].rearrange("p (t c) -> p t c", t=NT),
                                         ACT.Copy).then_inc(v_ready, 1)
                act.wait_ge(mm_done, u + 1)
                if j < 8:
                    if j >= 2:
                        act.wait_ge(kq_ready, j - 1)
                    nc.scalar.activation(k1[:, j, 0:CTX], slot(u, PIECES[0]), ACT.Copy)
                    nc.scalar.activation(kb[:, j % 2, CTX:TOK], slot(u, PIECES[1]), ACT.Copy).then_inc(evac_done, 1)
                elif j < 16:
                    act.wait_ge(kq_ready, min(8, j - 1))
                    if j >= 10:
                        act.wait_ge(vtr_mm, j - 9)
                    nc.scalar.activation(kb[:, j % 2, 0:CTX], slot(u, PIECES[0]), ACT.Copy)
                    nc.scalar.activation(kb[:, j % 2, CTX:TOK], slot(u, PIECES[1]), ACT.Copy).then_inc(evac_done, 1)
                else:
                    act.wait_ge(vtr_mm, min(8, j - 9))
                    if j >= 18:
                        act.wait_ge(kq_ready, j - 9)
                    nc.scalar.activation(kb[:, j % 2, CTX:TOK], slot(u, PIECES[1]), ACT.Copy, scale=0.125).then_inc(evac_done, 1)

            act.wait_ge(lam_ready, 1)
            nc.scalar.activation(nlam[:, 2:4], nlam[:, 0:2], ACT.Exp).then_inc(lam_ready, 1)
            for it in range(36):
                if it < 32:
                    for m in range(2):
                        act.wait_ge(mx_ready, 2 * it + m + 1)
                        if it >= 2:
                            act.wait_ge(pc_ready, it - 1)
                        nc.scalar.activation(pp[:, it % 2, m], Gf[:, 1024 * m:1024 * m + TOK], ACT.Exp,
                                             bias=nmx[:, it % 2, m:m + 1], accum_out=rsm[:, it % 2, m:m + 1]).then_inc(ex_ready, 1)
                if it >= 4:
                    i = it - 4
                    h, qt = i // 4, i % 4
                    act.wait_ge(o_ready, i + 1)
                    if i >= 2:
                        act.wait_ge(osq1, i - 1)
                    nc.scalar.activation(oq[:, i % 2], oo[:, qt, h * P:(h + 1) * P], ACT.Square,
                                         accum_out=ors[:, 0, 8 * qt + h:8 * qt + h + 1]).then_inc(osq1, 1)
                if 2 <= it <= 33:
                    i = it - 2
                    act.wait_ge(pt_mm, i + 1)
                    if i >= 2:
                        act.wait_ge(pv_mm, i - 1)
                    nc.scalar.activation(pT[:, i % 2], Xf[:, 0:TOK], ACT.Copy).then_inc(pt_ready, 1)
            act.wait_ge(oss1, 1)
            nc.scalar.activation(ors[:, 1], ors[:, 0], ACT.Sqrt).then_inc(act_small, 1)
            for k in range(KD):
                act.wait_ge(ot_mm, k + 1)
                nc.scalar.activation(y1[:, k], X[:, k % 2, :], ACT.Copy, scale=subg[:, 0:1]).then_inc(y1_ready, 1)
            act.wait_ge(y1_ready, 8)
            act.wait_ge(ot_mm, 8)
            for k in range(KD):
                nc.scalar.activation(uhi[:, k, CTX:TOK], y1[:, k], ACT.Copy).then_inc(uhi_ready, 1)
            for j in range(8):
                split_hi((j + 1) % 4, U_OUT1 + j + 1)
            layer_norm(2, (CTX, TOK), 3, U_MLP1)
            with act.Fori(0, 3) as q:
                mlp(1, q, (CTX, TOK), U_MLP1, 32, False)
            mlp(1, 3, (CTX, TOK), U_MLP1, 32, True)
            layer_norm(3, (CTX, TOK))
            for t in range(4):
                for w in range(2):
                    act.wait_ge(fin_mm, 2 * t + w + 1)
                    nc.scalar.activation(otok[:, t, 512 * w:512 * w + 512], G[:, w, :], ACT.Copy).then_inc(fin_ready, 1)

        @block.vector
        def _(dve):
            V = nc.vector
            chain = [0]

            def link(ins):
                chain[0] += 1
                ins.then_inc(dve_chain, 1)
                dve.wait_ge(dve_chain, chain[0])

            def split_lo(par, unit):
                dve.wait_ge(w_hi, unit + 1)
                V.tensor_tensor(wlo[:, par % 2], raw[:, (par // 2) % 2, :, (par % 2) * P:(par % 2 + 1) * P],
                                whi[:, par % 2].bitcast(F32), ALU.subtract).then_inc(w_lo, 1)

            def low_u(ubase, k, span):
                a, b = span
                dve.wait_ge(uhi_ready, ubase + k + 1)
                V.tensor_tensor(ulo[:, k, a:b], uf[:, k % 2, a:b], uhi[:, k, a:b].bitcast(F32), ALU.subtract).then_inc(ulo_ready, 1)

            dve.sem_inc(hh_done, 2)
            dve.sem_inc(h1lo_done, 2)
            dve.wait_ge(sil_t, 1)
            link(V.scalar_tensor_tensor(sil[:], silt[:], 1.0, cols[:], ALU.add, ALU.mult))
            V.tensor_scalar(sil[:], sil[:], 0.5, None, ALU.mult).then_inc(sil_ready, 1)
            dve.wait_ge(csp_hi, 1)
            V.tensor_tensor(csp[:, :, 2:4], sil[:].rearrange("p w k -> p k w"), csp[:, :, 0:2].bitcast(F32),
                            ALU.subtract).then_inc(csp_lo, 1)
            dve.wait_ge(rows_mm, 3)
            V.tensor_scalar(prmA[:], X[:, 2, 0:112], 1.0, None, ALU.mult)
            V.tensor_scalar(prmB[:], X[:, 2, 112:158], 1.0, None, ALU.mult)
            V.tensor_scalar(adab[:], X[:, 2, 160:256], 1.0, None, ALU.mult).then_inc(prm_ready, 1)
            dve.wait_ge(prm_ready, 1)
            V.tensor_scalar(convw[:], prmA[:, 64:112], 0.5, None, ALU.mult)
            link(V.tensor_scalar(subg[:, 0:1], prmB[:, 45:46], 1.0 - LAM_INIT, None, ALU.mult))
            dve.wait_ge(ada_col, ADA0)
            V.tensor_tensor(ada[:, 0:ADA1], X[:, 2, 256:256 + 2 * ADA1].rearrange("p (k w) -> p k w", w=2),
                            adab[:, 0:ADA1].unsqueeze(2).to_broadcast([P, ADA1, 2]), ALU.add).then_inc(ada_ready, 1)
            dve.wait_ge(ada_ready, 1)
            V.tensor_scalar(ada[:, KD:2 * KD], ada[:, KD:2 * KD], 1.0, None, ALU.add).then_inc(ada_ready, 1)
            dve.wait_ge(ada_ready, 2)
            split_lo(0, 0)
            for k in range(KD):
                low_u(0, k, (0, TOK))
            dve.wait_ge(wab_hi, 1)
            V.tensor_tensor(wablo[:], wab[:], wabhi[:].bitcast(F32), ALU.subtract).then_inc(wab_lo, 1)

            def ada_lo(u, j):
                i = ADA_PER * u + j
                if u < A_UNITS:
                    dve.wait_ge(a_hi, i + 1)
                    V.tensor_tensor(alo[:, i % 3], a_buf(i), ahi[:, i % 3].bitcast(F32), ALU.subtract).then_inc(a_lo_dve, 1)

            def softplus_in():
                dve.wait_ge(ab_ready, 1)
                dve.wait_ge(bc_in, 32)
                for p in range(6):
                    V.tensor_tensor(spx[:, 8 * p:8 * p + 8].rearrange("p (d h) -> p d h", d=2), abS[:, p, 0],
                                    dtbc.rearrange("p (d h) -> p d h", d=2), ALU.add)
                link(V.tensor_scalar(spx[:, 48:56], prmB[:, 36:44], -1.0, None, ALU.mult))
                link(V.tensor_scalar(spm, spx, -1.0, None, ALU.mult))
                V.tensor_tensor(spa, spx, spm, ALU.min).then_inc(dve_small, 1)
                V.tensor_scalar(spx, spx, 0.0, None, ALU.max)
                V.tensor_scalar(hbS, prmB[:, 20:36], 0.5, None, ALU.mult)

            def softplus():
                dve.wait_ge(act_small, 1)
                link(V.tensor_scalar(spm, spz, 2.0, None, ALU.add))
                link(V.reciprocal(spm, spm))
                link(V.tensor_tensor(spz, spz, spm, ALU.mult))
                link(V.tensor_tensor(sps, spz, spz, ALU.mult))
                link(V.tensor_scalar(spp, sps, 1.0 / 17, 1.0 / 15, ALU.mult, ALU.add))
                for deg in (13, 11, 9, 7, 5, 3, 1):
                    link(V.tensor_tensor(spp, spp, sps, ALU.mult))
                    link(V.tensor_scalar(spp, spp, 1.0 / deg, None, ALU.add))
                link(V.tensor_tensor(spp, spp, spz, ALU.mult))
                link(V.scalar_tensor_tensor(spp, spp, 2.0, spx, ALU.mult, ALU.add))
                V.tensor_scalar(hsS, spp[:, 48:56], -4.0, None, ALU.mult)
                V.tensor_scalar(nhsS, spp[:, 48:56], 4.0, None, ALU.mult).then_inc(dve_small, 1)
                dve.wait_ge(act_small, 3)
                V.tensor_scalar(bS, bS, 0.5, 0.5, ALU.mult, ALU.add)
                V.scalar_tensor_tensor(m3(gS, 6), m3(spp[:, 0:48], 6), -1.0, albc.unsqueeze(1).to_broadcast([P, 6, 8]),
                                       ALU.mult, ALU.mult).then_inc(gates_ready, 1)

            ada_lo(0, 1)
            for u in range(U_OUT0 + 1):
                if u + 1 < U_OUT0:
                    split_lo((u + 1) % 4, u + 1)
                if u == 16:
                    dve.wait_ge(a_col, ADAN // 4)
                    V.tensor_tensor(ada[:, ADA1:], X[:, 2, 0:2 * ADAN].rearrange("p (k w) -> p k w", w=2),
                                    adab[:, ADA1:].unsqueeze(2).to_broadcast([P, ADAN, 2]), ALU.add).then_inc(ada_ready, 1)
                    dve.wait_ge(ada_ready, 3)
                    cq = ada[:].rearrange("p (a k) w -> p a (k w)", a=12)
                    V.tensor_scalar(cq[:, 4:12:3], cq[:, 4:12:3], 1.0, None, ALU.add).then_inc(ada_ready, 1)
                    V.tensor_scalar(cq[:, 2:12:3], cq[:, 2:12:3], 1.0 / ALPHA, None, ALU.mult).then_inc(ada_ready, 1)
                    dve.wait_ge(ada_ready, 5)
                ada_lo(u, 3)
                ada_lo(u, 5)
                if u == 20:
                    softplus_in()
                    dve.wait_ge(sq_sum, 48)
                    V.tensor_scalar(ssS, ssS, EPS, None, ALU.add).then_inc(ss_ready, 1)
                if u == 21:
                    dve.wait_ge(rn_sqrt, 1)
                    link(V.reciprocal(rnS, rnS))
                    link(V.tensor_scalar(m3(rnS, 6)[:, :, 0:4], m3(rnS, 6)[:, :, 0:4], 128 ** -0.5, None, ALU.mult))
                if u == 22:
                    softplus()
                if u in (21, 23):
                    for t in (0, 1, 2) if u == 21 else (3, 4, 5):
                        V.tensor_tensor(qtok[:, t], qtok[:, t], bc_cols(m3(rnS, 6)[:, t, 0:4]), ALU.mult)
                        V.tensor_tensor(ktok[:, t], ktok[:, t], bc_cols(m3(rnS, 6)[:, t, 4:8]), ALU.mult).then_inc(qkn_ready, 1)
                if 1 <= u <= 12:
                    dve.wait_ge(tanh_done, u)
                    V.scalar_tensor_tensor(ybuf[:, (u - 1) % 2], tbuf[:, (u - 1) % 2], 1.0, ybuf[:, (u - 1) % 2],
                                           ALU.add, ALU.mult).then_inc(silu_done, 1)
                ada_lo(u, 7)
                ada_lo(u + 1, 1)
                if u < 16:
                    dve.wait_ge(evac_done, u + 1)
                    if 2 <= u < 12:
                        dve.wait_ge(tr_done, u - 1)
                    y = ybuf[:, u % 2] if u < 12 else xrT[:, u - 12]
                    for tap in range(4):
                        w = convw[:, tap * 12 + u:tap * 12 + u + 1] if u < 12 else prmB[:, tap * 4 + u - 12:tap * 4 + u - 11]
                        x = cbuf[:, u % 2, tap:tap + CW]
                        if tap == 0:
                            if u < 12:
                                ins = V.tensor_scalar(y, x, w, None, ALU.mult)
                            else:
                                ins = V.tensor_scalar(y, x, w, prmB[:, 16 + u - 12:17 + u - 12], ALU.mult, ALU.add)
                        else:
                            dve.wait_ge(conv_step, 4 * u + tap)
                            ins = V.scalar_tensor_tensor(y, x, w, y, ALU.mult, ALU.add)
                        ins.then_inc(conv_step, 1)
                elif u < 20:
                    dve.wait_ge(z_tanh, u - 15)
                    V.scalar_tensor_tensor(zT[:, u % 4], tbuf[:, u % 2, 0:TOK], 1.0, zT[:, u % 4], ALU.add, ALU.mult).then_inc(z_done, 1)
                elif u < 24:
                    tb = tbuf[:, u % 2, 0:TOK]
                    dve.wait_ge(g_sq, u - 19)
                    V.tensor_scalar(tb, tb, 8 * GELU1, 2 * GELU0, ALU.mult, ALU.add).then_inc(g_in, 1)
                    dve.wait_ge(g_in, 2 * (u - 20) + 1)
                    V.tensor_tensor(tb, tb, gT[:, u % 4], ALU.mult).then_inc(g_in, 1)
                    dve.wait_ge(g_tanh, u - 19)
                    V.scalar_tensor_tensor(gT[:, u % 4], tb, 1.0, gT[:, u % 4], ALU.add, ALU.mult).then_inc(g_done, 1)

            dve.wait_ge(cum_mm, 1)
            V.tensor_scalar(gamS, X[:, 2, 0:48], 1.0, None, ALU.mult).then_inc(dve_small, 1)
            dve.wait_ge(cum_mm, 2)
            dve.wait_ge(dve_small, 3)
            link(V.tensor_tensor(glS, X[:, 2, 64:112], gamS, ALU.subtract))
            V.tensor_scalar(glS, glS, 0.0, None, ALU.min).then_inc(dve_small, 1)
            dve.wait_ge(act_small, 6)
            link(V.tensor_tensor(bES, bES, bS, ALU.mult))

            for d in range(2):
                for c in range(4):
                    n = 4 * d + c
                    dve.wait_ge(lru_at, n + 1)
                    for s, e, off in ((0, CTX, 0), (CTX, TOK, GAP)):
                        V.scalar_tensor_tensor(lx[:, c, s:e], tii[n % 2][:, s:e], 1.0, xrT[:, c, s + off:e + off], ALU.add, ALU.mult)
                    link(V.tensor_tensor(aa2[n % 2][:], la[:, c], la[:, c], ALU.mult))
                    V.scalar_tensor_tensor(lw[:, c], aa2[n % 2][:], 1.0, thh[n % 2][:], ALU.add, ALU.mult).then_inc(lru_w, 1)
                dve.wait_ge(lru_sqrt, d + 1)
                for c in range(4):
                    link(V.tensor_tensor(lx[:, c], lx[:, c], lw[:, c], ALU.mult))
                    if d == 0:
                        link(V.tensor_tensor_scan(yl[:, c, 0:CTX], la[:, c, 0:CTX], lx[:, c, 0:CTX], 0.0, ALU.mult, ALU.add))
                        V.tensor_tensor_scan(yl[:, c, CTX:TOK], la[:, c, CTX:TOK], lx[:, c, CTX:TOK],
                                             yl[:, c, CTX - 1:CTX], ALU.mult, ALU.add).then_inc(lru_y, 1)
                    else:
                        rev = slice(CTX - 1, None, -1)
                        rl = slice(TOK - 1, CTX - 1, -1)
                        link(V.tensor_tensor_scan(lw[:, c, rev], la[:, c, rev], lx[:, c, rev], 0.0, ALU.mult, ALU.add))
                        link(V.tensor_tensor_scan(lw[:, c, rl], la[:, c, rl], lx[:, c, rl], lw[:, c, 0:1], ALU.mult, ALU.add))
                        link(V.tensor_tensor(yl[:, c], yl[:, c], lw[:, c], ALU.add))
                        V.tensor_tensor(gT[:, c], gT[:, c], yl[:, c], ALU.mult).then_inc(lru_y, 1)

            def v4(ap):
                return ap.rearrange("p (r c) -> p r c", r=4)

            def chain_dve(p, s):
                c = 2 * p + s
                dve.wait_ge(ch_v, 2 * c + 2)
                dve.wait_ge(state_zero, 3)
                if c >= 2:
                    dve.wait_ge(ch_o, c - 1)
                h = 64 * half_of(1, s)
                V.tensor_scalar(vn[s][h:h + 64, 4:8], v4(X[h:h + 64, 0, :]), 1.0, None, ALU.mult).then_inc(ch_vnb, 1)
                for r in range(8):
                    if r % 4 == 0:
                        dve.wait_ge(ch_s, 2 * c + r // 4 + 1)
                    V.scalar_tensor_tensor(S[:, r], S[:, r], cdS[:, 48 * s + 8 * p + r:48 * s + 8 * p + r + 1],
                                           X[:, 1 + r // 4, (r % 4) * P:(r % 4 + 1) * P], ALU.mult, ALU.add).then_inc(ch_state, 1)
                dve.wait_ge(ch_o, c + 1)
                first = (c < 3 - c) if c < 4 else (c < 15 - c)
                for d in range(2):
                    o = tile_of(d, p) * P + 64 * half_of(d, s)
                    src = X[:, 3, 256 * d:256 * d + 256].rearrange("p (h c) -> p h c", h=4)
                    if first:
                        last = V.tensor_scalar(oT[:, :, o:o + 64], src, 1.0, None, ALU.mult)
                    else:
                        last = V.tensor_tensor(oT[:, :, o:o + 64], src, oT[:, :, o:o + 64], ALU.add)
                last.then_inc(ch_out, 1)
                if c in (1, 7):
                    dve.wait_ge(ch_out, c + 1)

            dve.wait_ge(gc_in, 16)
            for p in range(7):
                if p < 6:
                    for d in range(2):
                        n = 2 * p + d
                        r = slice(4 * d, 4 * d + 4)
                        dve.wait_ge(gd_exp, n + 1)
                        if p >= 1:
                            dve.wait_ge(gd_qk_ready, n - 1)
                        link(V.tensor_tensor(dm[d][:], v4(G[:, 2 * d, :]), bc_cols(m3(gamS, 6)[:, p, r]), ALU.subtract))
                        V.tensor_scalar(dm[d][:], dm[d][:], 0.0, None, ALU.min).then_inc(gd_diff, 1)
                    for d in range(2):
                        n = 2 * p + d
                        dve.wait_ge(gd_dec, n + 1)
                        link(V.tensor_tensor(dm[d][:], dm[d][:], bc_mask(gc[:, CG_INCL + d]), ALU.mult))
                        dve.wait_ge(gd_g, n + 1)
                        if p >= 1:
                            dve.wait_ge(lv_ot, 2 * LEVELS * p)
                        V.tensor_tensor(att[d][:], v4(G[:, 2 * d + 1, :]), dm[d][:], ALU.mult).then_inc(gd_at0, 1)
                        dve.wait_ge(gd_brow, n + 1)
                        dve.wait_ge(gd_at0, n + 1)
                        V.tensor_tensor(att[d][:], att[d][:], v4(G[:, 2 * d, :]), ALU.mult).then_inc(gd_at, 1)
                    for d in range(2):
                        n = 2 * p + d
                        dve.wait_ge(gd_qk, n + 1)
                        if p >= 2:
                            dve.wait_ge(ch_o, 2 * (p - 1))
                        V.tensor_tensor(qk[d][p % 2][:], v4(G[:, 2 * d + 1, :]), dm[d][:], ALU.mult).then_inc(gd_qk_ready, 1)
                for lev in range(LEVELS):
                    if p < 6:
                        for d in range(2):
                            ni = 2 * (5 * p + lev) + d
                            if lev == 0:
                                dve.wait_ge(lv_p, 2 * LEVELS * p + d + 1)
                                V.tensor_tensor(xx[d][:], bc_mask(ident[:]), v4(G[:, 2 * d, :]), ALU.subtract).then_inc(lv_x, 1)
                                dve.wait_ge(lv_ot, 2 * LEVELS * p + d + 1)
                                V.tensor_tensor(xt[d][:], bc_mask(ident[:]), ot[d][0][:], ALU.subtract).then_inc(lv_xt, 1)
                                continue
                            if lev < 5:
                                dve.wait_ge(lv_e, 2 * (4 * p + lev - 1) + d + 1)
                                dve.wait_ge(lv_x, ni - 1)
                                V.tensor_tensor(xx[d][:], xx[d][:], v4(G[:, 2 * d + 1, :]), ALU.subtract).then_inc(lv_x, 1)
                            dve.wait_ge(lv_et, 2 * (5 * p + lev - 1) + d + 1)
                            dve.wait_ge(lv_xt, 2 * (LEVELS * p + lev - 1) + d + 1)
                            if lev == 5 and p >= 1:
                                dve.wait_ge(ch_o, 2 * p)
                            dst = tt[d] if lev == 5 else xt[d]
                            V.tensor_tensor(dst[:], xt[d][:], v4(G[:, 2 * d, :]), ALU.subtract).then_inc(lv_xt, 1)
                    if p >= 1 and lev in (1, 3):
                        chain_dve(p - 1, lev // 2)

            for h in range(4):
                dve.wait_ge(o_sq, h + 1)
                V.scalar_tensor_tensor(oT[:, h], oT[:, h], prmB[:, 44:45], zT[:, h], ALU.mult, ALU.mult).then_inc(o_z, 1)
            for h in range(4):
                dve.wait_ge(o_std, h + 1)
                link(V.reciprocal(osq[:, h], osq[:, h]))
                dve.wait_ge(o_z, h + 1)
                V.tensor_tensor(oT[:, h], oT[:, h], osq[:, h], ALU.mult).then_inc(o_y, 1)
            for k in range(4):
                dve.wait_ge(uhi_ready, 12 + k + 1)
                V.tensor_tensor(ulo[:, k], oT[:, k], uhi[:, k].bitcast(F32), ALU.subtract).then_inc(ulo_ready, 2)

            def residual(unit, par, f, layer, qg, span, rbase):
                dve.wait_ge(mm_done, unit + 1)
                for s, e, bank in PIECES:
                    if s >= span[0]:
                        who = ADA_CTX if bank == 0 else ADA_LAT
                        last = V.scalar_tensor_tensor(hT[:, f, s:e], G[:, 2 * (par % 2) + bank, 0:e - s],
                                                      adacol(layer, qg, f, who), hT[:, f, s:e], ALU.mult, ALU.add)
                last.then_inc(res_done, 1)

            def layer_norm(c, span, rbase, ubase=None):
                a, b = span
                for k in range(KD):
                    if k == 0:
                        dve.wait_ge(ln_mean, c + 1)
                        dve.wait_ge(res_done, rbase + 8)
                    for s, e, bank in PIECES:
                        if s >= a:
                            last = V.tensor_tensor(hT[:, k, s:e], hT[:, k, s:e], X[:, bank, 0:e - s], ALU.subtract)
                    last.then_inc(ln_xc, 1)
                dve.wait_ge(ln_std, c + 1)
                link(V.reciprocal(lrs[:, a:b], lstd[:, a:b]))
                for k in range(KD + 2):
                    if k < KD:
                        V.tensor_tensor(hT[:, k, a:b], hT[:, k, a:b], lrs[:, a:b], ALU.mult).then_inc(ln_xn, 1)
                    if ubase is not None and k >= 2:
                        low_u(ubase, k - 2, span)

            def mlp(layer, q, span, u0, h0, rbase, last_quarter):
                base = u0 + 16 * q
                a, b = span
                def split(j):
                    dve.wait_ge(w_hi, base + (j + 1))
                    V.tensor_tensor(wlo[:, j % 2], raw[:, (j // 2) % 2, :, (j % 2) * P:(j % 2 + 1) * P],
                                    whi[:, j % 2].bitcast(F32), ALU.subtract).then_inc(w_lo, 1)
                def low_h(j):
                    dve.wait_ge(h1hi_done, h0 + 8 * q + (j + 1))
                    V.tensor_tensor(h1lo[:, j, a:b], hh[:, j % 2, a:b], h1hi[:, j, a:b].bitcast(F32),
                                    ALU.subtract).then_inc(h1lo_done, 1)
                for j in range(8):
                    split(j + 1)
                    dve.wait_ge(relu_done, h0 + 8 * q + (j + 1))
                    dve.wait_ge(h1lo_done, h0 + 8 * q + (j + 1))
                    V.tensor_tensor(hh[:, j % 2, a:b], rt[:, j % 2, a:b], rt[:, j % 2, a:b], ALU.mult).then_inc(hh_done, 1)
                    if j >= 1:
                        low_h(j - 1)
                low_h(7)
                for f in range(8):
                    if not (last_quarter and f == 7):
                        split(8 + f + 1)
                    dve.wait_ge(mm_done, base + (8 + f + 1))
                    dve.wait_ge(res_done, rbase + 8 * q + f)
                    for s, e, bank in PIECES:
                        if s >= a:
                            who = ADA_CTX if bank == 0 else ADA_LAT
                            last = V.scalar_tensor_tensor(hT[:, f, s:e], G[:, 2 * (f % 2) + bank, 0:e - s],
                                                          adacol(layer, 5, f, who), hT[:, f, s:e], ALU.mult, ALU.add)
                    last.then_inc(res_done, 1)

            split_lo(0, U_OUT0)
            for j in range(8):
                split_lo((j + 1) % 4, U_OUT0 + j + 1)
                residual(U_OUT0 + j, j, j, 0, 2, (0, TOK), R_OUT0)
            layer_norm(0, (0, TOK), R_OUT0, 16)
            with dve.Fori(0, 4) as q:
                mlp(0, q, (0, TOK), U_MLP0, 0, R_MLP0, False)
            layer_norm(1, (0, TOK), R_MLP0 + 24, 24)

            dve.wait_ge(lam_in, 16)
            lv = lrow[:].rearrange("p (r d) -> p r d", r=4)
            link(V.tensor_tensor(rt1[:, 0:128].rearrange("p (a d) -> p a d", a=2), lv[:, 0:4:2], lv[:, 1:4:2], ALU.mult))
            V.tensor_reduce(nlam[:, 0:2], rt1[:, 0:128].rearrange("p (a d) -> p a d", a=2), AX.X, ALU.add).then_inc(lam_ready, 1)
            dve.wait_ge(rope_in, 16)
            dve.wait_ge(lam_ready, 1)
            for u in range(U_QKV, U_OUT1 + 1):
                j = u - U_QKV
                split_lo((u + 1) % 4, u + 1) if u < U_OUT1 else None
                jj = j - 1
                if 0 <= jj < 8 or 16 <= jj < 24:
                    i = jj if jj < 8 else jj - 8
                    dst = k1[:, jj, CTX:TOK] if jj < 8 else q1[:, jj - 16]
                    dve.wait_ge(evac_done, E_QKV + jj + 1)
                    if i >= 1:
                        dve.wait_ge(kq_ready, i)
                    V.tensor_tensor(rt1[:], kb[:, jj % 2, CTX:TOK], rc[:, P:P + LAT], ALU.mult).then_inc(rope_step, 1)
                    dve.wait_ge(rot_mm, i + 1)
                    V.tensor_tensor(rt2[:], X[:, i % 2, :], rc[:, P + LAT:P + 2 * LAT], ALU.mult).then_inc(rope_step, 1)
                    dve.wait_ge(rope_step, 2 * i + 2)
                    V.tensor_tensor(dst, rt1[:], rt2[:], ALU.add).then_inc(kq_ready, 1)

            dve.wait_ge(lam_ready, 2)
            link(V.tensor_tensor(nlam[:, 4:5], nlam[:, 3:4], nlam[:, 2:3], ALU.subtract))
            link(V.tensor_scalar(nlam[:, 4:5], nlam[:, 4:5], -LAM_INIT, None, ALU.add))
            for it in range(35):
                def maximum(m):
                    dve.wait_ge(sc_mm, 2 * it + m + 1)
                    if it >= 2:
                        dve.wait_ge(ex_ready, 2 * (it - 2) + m + 1)
                    V.tensor_reduce(nmx[:, it % 2, m:m + 1], Gf[:, 1024 * m:1024 * m + TOK], AX.X, ALU.max,
                                    negate=True).then_inc(mx_ready, 1)
                if it < 32:
                    maximum(0)
                if 1 <= it <= 32:
                    i = it - 1
                    dve.wait_ge(ex_ready, 2 * i + 2)
                    link(V.reciprocal(rrc[:, i % 2], rsm[:, i % 2]))
                    link(V.tensor_tensor(rrc[:, i % 2, 1:2], rrc[:, i % 2, 1:2], nlam[:, 4:5], ALU.mult))
                    if i >= 2:
                        dve.wait_ge(pt_mm, i - 1)
                    link(V.tensor_scalar(pc[:, i % 2], pp[:, i % 2, 0], rrc[:, i % 2, 0:1], None, ALU.mult))
                    V.scalar_tensor_tensor(pc[:, i % 2], pp[:, i % 2, 1], rrc[:, i % 2, 1:2], pc[:, i % 2],
                                           ALU.mult, ALU.add).then_inc(pc_ready, 1)
                if it < 32:
                    maximum(1)
                if it >= 3:
                    i = it - 3
                    h, qt = i // 4, i % 4
                    dve.wait_ge(pv_mm, i + 1)
                    V.tensor_scalar(oo[:, qt, h * P:(h + 1) * P], X[:, 2 + i % 2, 0:P], 1.0, None, ALU.mult).then_inc(o_ready, 1)
            dve.wait_ge(osq1, 32)
            V.tensor_scalar(ors[:, 0], ors[:, 0], 1.0 / P, EPS, ALU.mult, ALU.add).then_inc(oss1, 1)
            dve.wait_ge(act_small, 7)
            link(V.reciprocal(ors[:, 1], ors[:, 1]))
            for qt in range(4):
                v = oo[:, qt].rearrange("p (h c) -> p h c", h=8)
                V.tensor_tensor(v, v, ors[:, 1, 8 * qt:8 * qt + 8].unsqueeze(2).to_broadcast([P, 8, P]), ALU.mult).then_inc(on_ready, 1)
            for k in range(KD):
                dve.wait_ge(uhi_ready, 32 + k + 1)
                V.tensor_tensor(ulo[:, k, CTX:TOK], y1[:, k], uhi[:, k, CTX:TOK].bitcast(F32), ALU.subtract).then_inc(ulo_ready, 1)
            for j in range(8):
                split_lo((j + 1) % 4, U_OUT1 + j + 1)
                residual(U_OUT1 + j, j, j, 1, 2, (CTX, TOK), R_OUT1)
            layer_norm(2, (CTX, TOK), R_OUT1, 40)
            with dve.Fori(0, 3) as q:
                mlp(1, q, (CTX, TOK), U_MLP1, 32, R_MLP1, False)
            mlp(1, 3, (CTX, TOK), U_MLP1, 32, R_MLP1, True)
            layer_norm(3, (CTX, TOK), R_MLP1 + 24)

        @block.tensor
        def _(pe):
            mm = nc.tensor.matmul
            tr = nc.tensor.transpose

            def ada_cols(g):
                pe.wait_ge(a_row, g + 1)
                for w in range(4):
                    o = 8 * g + 2 * w
                    last = mm(X[:, 2, o:o + 2], grow[:, g % 2, w * P:(w + 1) * P], sel[:], start=True, stop=True)
                last.then_inc(a_col, 1)

            def ada_tile(i):
                if i % 4 == 0 and i > 0:
                    ada_cols(i // 4 - 1)
                wait_a_lo(pe, i)
                o = P * (i % 4)
                for k in range(KD):
                    hi = lambda: mm(X[0:4, 3, o:o + P], csp[:, k, 0:4], ahi[:, i % 3, k], start=(k == 0),
                                    stop=(k == KD - 1), skip_group_check=True)
                    lo = lambda: mm(X[0:2, 3, o:o + P], csp[:, k, 0:2], alo[:, i % 3, k], start=False, stop=False,
                                    skip_group_check=True)
                    for product in ((hi, lo) if k == 0 else (lo, hi)):
                        last = product()
                last.then_inc(a_mm, 1)

            def gemm(par, w_ready, src_hi, src_lo, span, k_waits=None, between=(), order=range(KD)):
                pe.wait_ge(w_lo, w_ready)
                pieces = [x for x in PIECES if x[0] >= span[0]]
                for k in order:
                    if callable(k_waits):
                        k_waits(k)
                    elif k_waits is not None:
                        pe.wait_ge(k_waits[0], k_waits[1] + k)
                    for w, x, first, final in ((whi, src_hi, True, False), (whi, src_lo, False, False), (wlo, src_hi, False, True)):
                        for s, e, bank in pieces:
                            last = mm(G[:, 2 * (par % 2) + bank, 0:e - s], w[:, par % 2, k], x[:, k, s:e],
                                      start=(k == order[0] and first), stop=(k == order[-1] and final))
                    if between:
                        ada_tile(between[k])
                last.then_inc(mm_done, 1)

            pe.wait_ge(const_in, 48)
            pe.wait_ge(ones_ready, 4)
            pe.wait_ge(x_in, 32)
            for k in range(KD):
                if k >= 2:
                    pe.wait_ge(h0_ready, k - 1)
                for t in range(NT):
                    bank, col = (0, t * P) if t < 2 else (1, (t - 2) * P)
                    last = tr(G[:, 2 * (k % 2) + bank, col:col + P], xtok[:, t, k * P:(k + 1) * P], ident[:])
                last.then_inc(tr_x, 1)
            pe.wait_ge(rows_in, 160)
            tr(X[:, 2, 0:112], rowsA[0:112], ident[0:112, 0:112]).then_inc(rows_mm, 1)
            tr(X[:, 2, 112:158], rowsB[0:46], ident[0:46, 0:46]).then_inc(rows_mm, 1)
            tr(X[:, 2, 160:256], rowsC[0:96], ident[0:96, 0:96]).then_inc(rows_mm, 1)
            pe.wait_ge(prm_ready, 1)
            pe.wait_ge(sil_ready, 1)
            for n in range(ADA0 + 1):
                if n < ADA0:
                    pe.wait_ge(ada_in[n % 2], 16 * (n // 2 + 1))
                    if n >= 2:
                        pe.wait_ge(ada_row, n - 1)
                    for k in range(KD):
                        last = mm(X[0:2, n % 2, :], sil[:, :, k], aw[:, n % 2, k], start=(k == 0), stop=(k == KD - 1))
                    last.then_inc(ada_mm, 1)
                if n >= 1:
                    pe.wait_ge(ada_row, n)
                    for w in range(4):
                        i = (n - 1) * 4 + w
                        o = 256 + 2 * i
                        last = mm(X[:, 2, o:o + 2], arow[:, (n - 1) % 2, w * P:(w + 1) * P], ident[0:2, 0:2],
                                  start=True, stop=True)
                    last.then_inc(ada_col, 1)

            def gates_rows():
                pe.wait_ge(wab_lo, 1)
                for k in range(KD):
                    for w, x, a, b in ((wabhi, uhi, True, False), (wabhi, ulo, False, False), (wablo, uhi, False, True)):
                        for s, e, bank in PIECES:
                            last = mm(X[0:16, bank, 0:e - s], w[:, k], x[:, k, s:e], start=(k == 0 and a),
                                      stop=(k == KD - 1 and b))
                last.then_inc(ab_mm, 1)

            def gates_tokens():
                pe.wait_ge(ab_rows, 1)
                pe.wait_ge(ada_ready, 3)
                for t in range(NT):
                    last = tr(X[:, 2, 16 * t:16 * t + 16], abT[:, t * P:(t + 1) * P], ident[0:16, 0:16])
                last.then_inc(ab_mm, 1)

            pe.wait_ge(ada_ready, 2)
            pe.wait_ge(csp_lo, 1)
            for u in range(U_OUT0):
                if u >= 2:
                    pe.wait_ge(evac_done, u - 1)
                gemm(u, u + 1, uhi, ulo, (0, TOK), (ulo_ready, 1) if u == 0 else None,
                     ada_tiles(u))
                if u == A_UNITS:
                    ada_cols(ADAN // 4 - 1)
                if u == 17:
                    gates_rows()
                if u == 18:
                    gates_tokens()
                if 2 <= u <= 13:
                    pe.wait_ge(silu_done, u - 1)
                    if u >= 3:
                        pe.wait_ge(tok_done, u - 2)
                    for t in range(NT):
                        o = t * P if t < 2 else LO + (t - 2) * P
                        last = tr(Xf[:, t * P:(t + 1) * P], ybuf[:, (u - 2) % 2, o:o + P], ident[:])
                    last.then_inc(tr_done, 1)
            pe.wait_ge(gc_in, 16)
            pe.wait_ge(gates_ready, 1)
            pe.wait_ge(ab_ready, 1)
            g3 = m3(gS, 6)
            cum = X[:, 2, 0:48].rearrange("p (t r) -> p t r", t=6)
            for d in range(2):
                last = mm(cum[:, :, 4 * d:4 * d + 4], gc[:, CG_CUM + d], g3[:, :, 4 * d:4 * d + 4], start=True, stop=True)
            last.then_inc(cum_mm, 1)
            pe.wait_ge(dve_small, 3)
            gm = m3(gamS, 6)
            tot = X[:, 2, 64:112].rearrange("p (t r) -> p t r", t=6)
            dec = X[:, 2, 128:224].rearrange("p (s t r) -> p s t r", s=2, t=6)
            for d in range(2):
                mm(tot[:, :, 4 * d:4 * d + 4], gc[:, CG_LAST + d], gm[:, :, 4 * d:4 * d + 4], start=True, stop=True)
            for s in range(2):
                for d in range(2):
                    row = CG_ROW + 2 * s + d
                    last = mm(dec[:, s, :, 4 * d:4 * d + 4], gc[:, row], gm[:, :, 4 * d:4 * d + 4], start=True, stop=True)
            last.then_inc(cum_mm, 1)

            pe.wait_ge(gw_in, 128)
            pe.wait_ge(evac_done, 24)
            for d in range(2):
                for c in range(4):
                    n = 4 * d + c
                    if n == 1:
                        pe.wait_ge(act_small, 6)
                    if n >= 2:
                        pe.wait_ge(gate_tanh, n - 1)
                    B = X if n % 2 else G
                    for g in range(2):
                        for s, e, bank in PIECES:
                            off = GAP * bank
                            last = mm(B[:, 2 * g + bank, 0:e - s], gw[:, (2 * d + g) * 4 + c], xrT[:, c, s + off:e + off],
                                      start=True, stop=True)
                    last.then_inc(gates_mm, 1)

            pe.wait_ge(gate_tanh, 8)
            for t in range(NT):
                pe.wait_ge(qkn_ready, t + 1)
                for w, src in ((0, qtok), (1, ktok)):
                    if t >= 1:
                        pe.wait_ge(qkT_ready, 2 * t + w - 1)
                    for h in range(HEADS):
                        last = tr(X[:, w, h * P:(h + 1) * P], src[:, t, h], ident[:])
                    last.then_inc(qkT_mm, 1)

            def four(bank, lhs, rhs, sem):
                for r in range(4):
                    last = mm(G[:, bank, r * P:(r + 1) * P], lhs(r), rhs(r), start=True, stop=True)
                last.then_inc(sem, 1)

            def row_of(small_array, p, d, sem):
                four(2 * d, lambda r: m3(small_array, 6)[:, p, 4 * d + r:4 * d + r + 1].to_broadcast([P, P]),
                     lambda r: ident[:], sem)

            def chain_pe(p, s):
                c = 2 * p + s
                pe.wait_ge(wt_ready, 2 * p + 2)
                pe.wait_ge(bv_ready, 2 * p + 2)
                pe.wait_ge(lv_xt, 2 * LEVELS * (p + 1))
                pe.wait_ge(state_zero, 3)
                if c >= 1:
                    pe.wait_ge(ch_vnf, c)
                    pe.wait_ge(ch_vnb, c)
                for d in range(2):
                    h = 64 * half_of(d, s)
                    for r in range(4):
                        mm(X[h:h + 64, 0, r * P:(r + 1) * P], tt[d][:, r, h:h + 64], bv[d][:, r], start=(r == 0), stop=False,
                           skip_group_check=True)
                for d in range(2):
                    h = 64 * half_of(d, s)
                    if c >= 1:
                        pe.wait_ge(ch_state, 8 * (c - 1) + 4 * d + 4)
                    for r in range(4):
                        last = mm(X[h:h + 64, 0, r * P:(r + 1) * P], wt[d][:, r, h:h + 64], S[:, 4 * d + r], start=False,
                                  stop=(r == 3), skip_group_check=True)
                    last.then_inc(ch_v, 1)
                pe.wait_ge(gd_qd, 2 * p + 2)
                if c >= 1:
                    pe.wait_ge(ch_out, c)
                for d in range(2):
                    h = 64 * half_of(d, s)
                    for r in range(4):
                        o = 256 * d + 64 * r
                        mm(X[:, 3, o:o + 64], S[:, 4 * d + r], qd[d][p % 2][:, r, h:h + 64], start=(d == 0 and r == 0), stop=False,
                           skip_group_check=True)
                pe.wait_ge(kd_ready, 2 * p + 2)
                for d in range(2):
                    pe.wait_ge((ch_vnf, ch_vnb)[d], c + 1)
                    for r in range(4):
                        last = mm(X[:, 1 + d, r * P:(r + 1) * P], kd[d][:, r], vn[s][:, 4 * d + r], start=True, stop=True)
                    last.then_inc(ch_s, 1)
                for d in range(2):
                    h = 64 * half_of(d, s)
                    for r in range(4):
                        o = 256 * d + 64 * r
                        last = mm(X[:, 3, o:o + 64], vn[s][:, 4 * d + r], qk[d][p % 2][:, r, h:h + 64], start=False,
                                  stop=(d == 1 and r == 3), skip_group_check=True)
                last.then_inc(ch_o, 1)

            for p in range(7):
                if p < 6:
                    for d in range(2):
                        if p == 0:
                            pe.wait_ge(gate_tanh, 8)
                        else:
                            pe.wait_ge(lv_xt, 2 * (LEVELS * p - 1) + d + 1)
                        row_of(gamS, p, d, gd_row)
                    if p == 0:
                        pe.wait_ge(qkT_ready, 12)
                    for d in range(2):
                        t = tile_of(d, p)
                        ts = slice(t * P, (t + 1) * P)
                        if p >= 1:
                            pe.wait_ge(wt_ready, 2 * (p - 1) + d + 1)
                        four(2 * d + 1, lambda r: kT[:, r, ts], lambda r: kT[:, r, ts], gd_g)
                    for d in range(2):
                        pe.wait_ge(gd_diff, 2 * p + d + 1)
                        row_of(bS, p, d, gd_brow)
                    for d in range(2):
                        t = tile_of(d, p)
                        ts = slice(t * P, (t + 1) * P)
                        pe.wait_ge(gd_at, 2 * p + d + 1)
                        four(2 * d + 1, lambda r: kT[:, r, ts], lambda r: qT[:, r, ts], gd_qk)
                for lev in range(LEVELS):
                    if p < 6:
                        for d in range(2):
                            pe.wait_ge(lv_ot, 2 * (LEVELS * p + lev) + d + 1)
                            if lev == 0:
                                pe.wait_ge(gd_at, 2 * p + d + 1)
                                four(2 * d, lambda r: ot[d][0][:, r], lambda r: ident[:], lv_p)
                            else:
                                pe.wait_ge(lv_x, 2 * (5 * p + lev - 1) + d + 1)
                                pe.wait_ge(lv_xt, 2 * (LEVELS * p + lev - 1) + d + 1)
                                four(2 * d, lambda r: ot[d][lev % 2][:, r], lambda r: xx[d][:, r], lv_p)
                        if lev > 0:
                            for d in range(2):
                                pe.wait_ge(lv_pm, 2 * (5 * p + lev - 1) + d + 1)
                                if lev == 1:
                                    pe.wait_ge(gd_qk_ready, 2 * p + d + 1)
                                if lev < 5:
                                    four(2 * d + 1, lambda r: xt[d][:, r], lambda r: pm[d][:, r], lv_e)
                                four(2 * d, lambda r: pm[d][:, r], lambda r: xt[d][:, r], lv_et)
                    if p >= 1 and lev in (1, 3):
                        chain_pe(p - 1, lev // 2)
                if p < 6:
                    for d in range(2):
                        pe.wait_ge(bk_ready, 2 * p + d + 1)
                        pe.wait_ge(lv_xt, 2 * (LEVELS * p + 5) + d + 1)
                        four(2 * d + 1, lambda r: dg[d][:, r], lambda r: tt[d][:, r], wt_mm)

            for h in range(HEADS):
                pe.wait_ge(o_sq, h + 1)
                B = (G, X)[h // 2]
                for s, e, bank in PIECES:
                    last = mm(B[:, 2 * (h % 2) + bank, 0:e - s], ones[:], osq[:, h, s:e], start=True, stop=True)
                last.then_inc(o_ms, 1)

            def mixer_waits(k):
                if k >= 4:
                    pe.wait_ge(glo_ready, k - 3)
                else:
                    pe.wait_ge(ulo_ready, 8 + 2 * (k + 1))
            for j in range(8):
                if j >= 2:
                    pe.wait_ge(res_done, R_OUT0 + j - 1)
                else:
                    pe.wait_ge(o_std, j + 1)
                gemm(j, U_OUT0 + j + 1, uhi, ulo, (0, TOK), mixer_waits if j == 0 else None, order=(4, 5, 6, 7, 0, 1, 2, 3))

            def layer_norm(c, span, rbase):
                pieces = [x for x in PIECES if x[0] >= span[0]]
                pe.wait_ge(acc_step, 6 * c + 6)
                for s, e, bank in pieces:
                    mm(X[:, bank, 0:e - s], onesD[:], acc[:, s:e], start=True, stop=False)
                pe.wait_ge(res_done, rbase + KD)
                for s, e, bank in pieces:
                    last = mm(X[:, bank, 0:e - s], onesD[:], hT[:, KD - 1, s:e], start=False, stop=True)
                last.then_inc(ln_mean, 1)
                for k in range(KD):
                    pe.wait_ge(ln_sq, 8 * c + k + 1)
                    for s, e, bank in pieces:
                        last = mm(X[:, 2 + bank, 0:e - s], onesD[:], lsq[:, k % 2, s:e], start=(k == 0), stop=(k == KD - 1))
                    last.then_inc(ln_var, 1)

            def mlp(q, span, u0, h0, rbase, ubase):
                base = u0 + 16 * q
                for j in range(8):
                    if j >= 2:
                        pe.wait_ge(relu_done, h0 + 8 * q + (j - 1))
                    else:
                        pe.wait_ge(res_done, rbase + 8 * q + (j - 1))
                    gemm(j, base + (j + 1), uhi, ulo, span, (ulo_ready, ubase + 1) if j == 0 else None)
                for f in range(8):
                    if f >= 2:
                        pe.wait_ge(res_done, rbase + 8 * q + (f - 1))
                    else:
                        pe.wait_ge(relu_done, h0 + 8 * q + (7 + f))
                    gemm(f, base + (8 + f + 1), h1hi, h1lo, span, (h1lo_done, h0 + 8 * q + 3) if f == 0 else None)

            layer_norm(0, (0, TOK), R_OUT0)
            with pe.Fori(0, 4) as q:
                mlp(q, (0, TOK), U_MLP0, 0, R_MLP0, 16)
            layer_norm(1, (0, TOK), R_MLP0 + 24)

            for u in range(U_QKV, U_OUT1 + 1):
                j = u - U_QKV
                if j < 24:
                    if j < 2:
                        pe.wait_ge(res_done, R_OUT1 + j - 1)
                    else:
                        pe.wait_ge(evac_done, E_QKV + j - 1)
                    gemm(u, u + 1, uhi, ulo, (0, TOK) if j < 16 else (CTX, TOK), (ulo_ready, 24 + 1) if j == 0 else None)
                jj = j - 1
                if 0 <= jj < 8 or 16 <= jj < 24:
                    i = jj if jj < 8 else jj - 8
                    pe.wait_ge(evac_done, E_QKV + jj + 1)
                    pe.wait_ge(rope_in, 16)
                    if i >= 2:
                        pe.wait_ge(kq_ready, i - 1)
                    mm(X[:, i % 2, :], rc[:, 0:P], kb[:, jj % 2, CTX:TOK], start=True, stop=True).then_inc(rot_mm, 1)
                elif 8 <= jj < 16:
                    pe.wait_ge(evac_done, E_QKV + jj + 1)
                    if jj >= 9:
                        pe.wait_ge(v_ready, jj - 8)
                    for t in range(NT):
                        last = tr(Xf[:, 1024 + t * P:1024 + (t + 1) * P], kb[:, jj % 2, t * P:(t + 1) * P], ident[:])
                    last.then_inc(vtr_mm, 1)

            pe.wait_ge(v_ready, 8)
            pe.wait_ge(kq_ready, 16)
            for it in range(35):
                if it < 32:
                    h, qt = it // 4, it % 4
                    for m in range(2):
                        if it >= 1:
                            pe.wait_ge(ex_ready, 2 * (it - 1) + m + 1)
                        r = slice(64 * m, 64 * m + 64)
                        for a, b in ((0, 512), (512, TOK)):
                            last = mm(Gf[:, 1024 * m + a:1024 * m + b], q1[r, h, qt * P:(qt + 1) * P], k1[r, h, a:b],
                                      start=True, stop=True)
                        last.then_inc(sc_mm, 1)
                if 2 <= it <= 33:
                    i = it - 2
                    pe.wait_ge(pc_ready, i + 1)
                    if i >= 1:
                        pe.wait_ge(pt_ready, i)
                    for t in range(NT):
                        last = tr(Xf[:, t * P:(t + 1) * P], pc[:, i % 2, t * P:(t + 1) * P], ident[:])
                    last.then_inc(pt_mm, 1)
                if it >= 3:
                    i = it - 3
                    h = i // 4
                    pe.wait_ge(pt_ready, i + 1)
                    if i >= 2:
                        pe.wait_ge(o_ready, i - 1)
                    for t in range(NT):
                        last = mm(X[:, 2 + i % 2, 0:P], pT[:, i % 2, t * P:(t + 1) * P], v1[:, t, h * P:(h + 1) * P],
                                  start=(t == 0), stop=(t == NT - 1))
                    last.then_inc(pv_mm, 1)
            pe.wait_ge(on_ready, 4)
            for k in range(KD):
                if k >= 2:
                    pe.wait_ge(y1_ready, k - 1)
                for qt in range(4):
                    last = tr(X[:, k % 2, qt * P:(qt + 1) * P], oo[:, qt, k * P:(k + 1) * P], ident[:])
                last.then_inc(ot_mm, 1)
            for j in range(8):
                if j >= 2:
                    pe.wait_ge(res_done, R_OUT1 + j - 1)
                gemm(j, U_OUT1 + j + 1, uhi, ulo, (CTX, TOK), (ulo_ready, 32 + 1) if j == 0 else None)
            layer_norm(2, (CTX, TOK), R_OUT1)
            with pe.Fori(0, 3) as q:
                mlp(q, (CTX, TOK), U_MLP1, 32, R_MLP1, 40)
            mlp(3, (CTX, TOK), U_MLP1, 32, R_MLP1, 40)
            layer_norm(3, (CTX, TOK), R_MLP1 + 24)
            pe.wait_ge(ln_h, 32)
            for t in range(4):
                for w in range(2):
                    if t >= 1:
                        pe.wait_ge(fin_ready, 2 * t + w - 1)
                    for k in range(4):
                        last = tr(G[:, w, k * P:(k + 1) * P], hT[:, 4 * w + k, CTX + t * P:CTX + (t + 1) * P], ident[:])
                    last.then_inc(fin_mm, 1)


_INS = ["x", "c", "ctx", "c_ctx", "ada_w", "ada_b", "ln_g", "ln_b", "mlp_w1", "mlp_w2", "mix_w_out", "ev_w_in",
        "ev_qkv_conv", "ev_a_log", "ev_dt_bias", "ev_gdn_norm", "ev_lru_conv_w", "ev_lru_conv_b", "ev_lru_gate_w",
        "ev_lru_gate_b", "ev_lru_lambda", "od_w_qkv", "od_lambda", "od_subln"]


def kernel(**inputs):
    import concourse.bacc as _bacc
    from concourse.bass_utils import run_bass_kernel_spmd as _run

    nc = _bacc.Bacc("TRN2", target_bir_lowering=False, num_devices=1, dynamic_dma_scratch_size=1024)
    arrays = {n: np.ascontiguousarray(inputs[n]) for n in _INS}
    arrays["c_eye"] = np.eye(P, dtype=np.float32)
    arrays["c_gdn"] = gdn_constants()
    arrays["c_rope"] = rope_constants()
    args = {n: nc.dram_tensor(f"in_{n}_dram", a.shape, mybir.dt.from_np(a.dtype), kind="ExternalInput").ap()
            for n, a in arrays.items()}
    out = nc.dram_tensor("out_0_dram", (1, LAT, D), F32, kind="ExternalOutput").ap()
    trunk(nc, args, out)
    r = _run(nc, [{f"in_{n}_dram": a for n, a in arrays.items()}], core_ids=[0])
    return r.results[0]["out_0_dram"]
```

```python
import math
from contextlib import ExitStack

import numpy as np
import concourse.bass as bass
from concourse import mybir

F32 = mybir.dt.float32
F32R = mybir.dt.float32r
ACT = mybir.ActivationFunctionType
ALU = mybir.AluOpType
AX = mybir.AxisListType

P = 128
D = 1024
KD = D // P
CTX, LAT = 256, 512
TOK = CTX + LAT
NT = TOK // P
DFF = 4 * D
HEADS = 4
GAP = 2
CW = TOK + GAP
LO = CTX + GAP
EPS = 1e-6
ALPHA = 4 ** 0.25
LAM_INIT = 0.8 - 0.6 * math.exp(-0.3)
QC, KC, VC, ZC, AC, XC, GC = 0, 512, 1024, 1536, 2048, 2064, 2576
GELU0 = math.sqrt(2 / math.pi)
GELU1 = GELU0 * 0.044715
LEVELS = 6
BWD_TILE = [1, 0, 5, 4, 3, 2]
PIECES = [(0, CTX, 0), (CTX, TOK, 1)]


def gdn_constants():
    j, i = np.arange(P)[:, None], np.arange(P)[None, :]
    same = (j // 64) == (i // 64)
    out = [(j <= i) & same, (j >= i) & same,
           (j % 64 == 63) & same, (j % 64 == 0) & same]
    for first in (63, 64, 127, 0):
        out.append(np.broadcast_to(j == first, (P, P)))
    out += [(j <= i) & same, (j >= i) & same]
    for lev in range(LEVELS):
        b = 1 << lev
        blk = (j // (2 * b)) == (i // (2 * b))
        out.append(blk & ((i // b) % 2 == 1) & ((j // b) % 2 == 0))
        out.append(blk & ((i // b) % 2 == 0) & ((j // b) % 2 == 1))
    return np.stack(out, 1).astype(np.float32)


def rope_constants():
    half = 32
    inv = (np.float32(10000.0) ** (-(np.arange(0, half, 2, dtype=np.float32) / np.float32(half)))).astype(np.float32)
    t = np.arange(LAT)
    ar = (t // 64).astype(np.float32)[:, None] * inv
    ac = (t % 64).astype(np.float32)[:, None] * inv
    ang = np.concatenate([ar, ar, ac, ac], -1).T.astype(np.float32)
    ang = np.concatenate([ang, ang], 0)
    rot = np.zeros((P, P), np.float32)
    for m in range(P):
        if (m // 16) % 2 == 0:
            rot[m + 16, m] = -1.0
        else:
            rot[m - 16, m] = 1.0
    return np.concatenate([rot, np.cos(ang), np.sin(ang)], 1).astype(np.float32)


CG_CUM, CG_LAST, CG_ROW, CG_INCL, CG_LEV = 0, 2, 4, 8, 10
NG = 10 + 2 * LEVELS


def trunk(nc, I, out):
    with ExitStack() as ctx:
        def at(name, kb, shape, dt=F32):
            return nc.alloc_sbuf_tensor_at(name, shape, dt, offset=int(kb * 1024))

        def sems(names):
            return [ctx.enter_context(nc.semaphore(n)) for n in names.split()]

        ident = at("ident", 2, [P, P])
        ones = at("ones", 2.5, [P, P])
        prmA = at("prmA", 3, [P, 112])
        prmB = at("prmB", 3.5, [P, 46])
        ada = at("ada", 3.75, [P, 96, 2])
        convw = at("convw", 4.5, [P, 48])
        sil = at("sil", 4.75, [P, 2, KD])
        nlam = at("nlam", 4.875, [P, 8])
        subg = at("subg", 4.9375, [P, 2])
        silt = at("silt", 5, [P, 2, KD])
        cols = at("cols", 5.125, [P, 2, KD])
        onesD = at("onesD", 5.25, [P, P])
        eps2 = at("eps2", 5.8125, [P, 2])
        hT = at("hT", 6, [P, KD, TOK])
        raw = at("raw", 30, [P, 2, KD, 256])
        whi = at("whi", 46, [P, 2, KD, P], F32R)
        wlo = at("wlo", 54, [P, 2, KD, P], F32R)
        uhi = at("uhi", 62, [P, KD, TOK], F32R)
        ulo = at("ulo", 86, [P, KD, TOK], F32R)
        uf = at("uf", 110, [P, 2, TOK])
        adab = at("adab", 1.125, [P, 96])
        csp = at("csp", 1.5, [P, KD, 4], F32R)
        sel = at("sel", 1.75, [4, 2])
        grow = at("grow", 111.5, [4, 2, 512])
        xtok = at("xtok", 152.5, [P, NT, D])
        rowsA = at("rowsA", 188.5, [P, P])
        rowsB = at("rowsB", 189, [P, P])
        rowsC = at("rowsC", 189.5, [P, P])
        araw = [at("araw0", 140, [P, 3, KD, P]), at("araw1", 176.5, [P, 3, KD, P])]
        ahi = at("ahi", 116, [P, 3, KD, P], F32R)
        alo = at("alo", 128, [P, 3, KD, P], F32R)
        zT = at("zT", 116, [P, 4, TOK])
        gT = at("gT", 128, [P, 4, TOK])
        xrT = at("xrT", 140, [P, 4, CW])
        qtok = at("qtok", 152.5, [P, NT, HEADS, P])
        ktok = at("ktok", 164.5, [P, NT, HEADS, P])
        vtok = at("vtok", 176.5, [P, NT, HEADS, P])
        cbuf = at("cbuf", 188.5, [P, 2, CW + 3])
        ybuf = at("ybuf", 194.75, [P, 2, CW])
        tbuf = at("tbuf", 201, [P, 2, CW])
        wab = at("wab", 110, [P, KD, 16])
        wabhi = at("wabhi", 110.5, [P, KD, 16], F32R)
        wablo = at("wablo", 111, [P, KD, 16], F32R)
        nsq = at("nsq", 196.5, [P, 2, P])
        abT = at("abT", 197.75, [16, TOK])
        sm = at("sm", 111.5, [P, 1150])
        la = at("la", 62, [P, 4, TOK])
        lw = at("lw", 74, [P, 4, TOK])
        lx = at("lx", 86, [P, 4, TOK])
        trr = [at("trr0", 98, [P, TOK]), at("trr1", 54, [P, TOK])]
        tii = [at("tii0", 101, [P, TOK]), at("tii1", 57, [P, TOK])]
        thh = [at("thh0", 104, [P, TOK]), at("thh1", 197, [P, TOK])]
        aa2 = [at("aa20", 107, [P, TOK]), at("aa21", 200, [P, TOK])]
        gw = at("gw", 188.5, [P, 16, P])
        yl = at("yl", 42, [P, 4, TOK])
        gc = at("gc", 30, [P, NG, P])
        kT = at("kT", 41, [P, HEADS, TOK])
        qT = at("qT", 53, [P, HEADS, TOK])
        dg = [at(f"dg{d}", 65 + 16 * d, [P, 4, P]) for d in range(2)]
        dm = [at(f"dm{d}", 67 + 16 * d, [P, 4, P]) for d in range(2)]
        att = [at(f"att{d}", 69 + 16 * d, [P, 4, P]) for d in range(2)]
        ot = [[at(f"ot{d}{e}", 71 + 2 * e + 16 * d, [P, 4, P]) for e in range(2)] for d in range(2)]
        xx = [at(f"xx{d}", 75 + 16 * d, [P, 4, P]) for d in range(2)]
        xt = [at(f"xt{d}", 77 + 16 * d, [P, 4, P]) for d in range(2)]
        pm = [at(f"pm{d}", 79 + 16 * d, [P, 4, P]) for d in range(2)]
        tt = [at(f"tt{d}", 97 + 2 * d, [P, 4, P]) for d in range(2)]
        wt = [at(f"wt{d}", 101 + 2 * d, [P, 4, P]) for d in range(2)]
        kd = [at(f"kd{d}", 105 + 2 * d, [P, 4, P]) for d in range(2)]
        bv = at("bv0", 109, [P, 4, P])
        bv = [bv, at("bv1", 116 + 88.5, [P, 4, P])]
        qk = [[at(f"qk{d}{b}", 188.5 + 4 * d + 2 * b, [P, 4, P]) for b in range(2)] for d in range(2)]
        qd = [[at(f"qd{d}{b}", 196.5 + 4 * d + 2 * b, [P, 4, P]) for b in range(2)] for d in range(2)]
        S = at("S", 140, [P, 8, P])
        vn = [at(f"vn{s}", 144 + 4 * s, [P, 8, P]) for s in range(2)]
        otk = at("otk", 152.5, [P, NT, HEADS, P])
        oT = at("oT", 140, [P, HEADS, TOK])
        eps1 = at("eps1", 1.875, [P, 1])
        orn = at("orn", 1.90625, [P, 24])
        k1 = at("k1", 116, [P, KD, TOK])
        v1 = at("v1", 140, [P, NT, D])
        q1 = at("q1", 164, [P, KD, LAT])
        kb = at("kb", 180, [P, 2, TOK])
        rc = at("rc", 186, [P, P + 2 * LAT])
        rt1 = at("rt1", 191, [P, LAT])
        rt2 = at("rt2", 193, [P, LAT])
        pp = at("pp", 180, [P, 2, 2, TOK])
        pc = at("pc", 192, [P, 2, TOK])
        pT = at("pT", 198, [P, 2, TOK])
        nmx = at("nmx", 204, [P, 2, 2])
        rsm = at("rsm", 204.125, [P, 2, 2])
        rrc = at("rrc", 204.25, [P, 2, 2])
        oo = at("oo", 62, [P, 4, D])
        ors = at("ors", 204.5, [P, 2, 32])
        oq = at("oq", 205, [P, 2, P])
        y1 = at("y1", 116, [P, KD, LAT])
        h1hi = at("h1hi", 116, [P, KD, TOK], F32R)
        h1lo = at("h1lo", 140, [P, KD, TOK], F32R)
        rt = at("rt", 164, [P, 2, TOK])
        hh = at("hh", 170, [P, 2, TOK])
        lsq = at("lsq", 176, [P, 2, TOK])
        lstd = at("lstd", 182, [1, TOK])
        lst = at("lst", 185, [P, NT])
        acc = at("acc", 198, [P, TOK])
        lrow = at("lrow", 195.5, [P, 2 * P])
        otok = at("otok", 116, [P, 4, D])

        G = ctx.enter_context(nc.psum_tensor("G", [P, 4, 512], F32))
        X = ctx.enter_context(nc.psum_tensor("X", [P, 4, 512], F32))
        Gf = G[:].rearrange("p a b -> p (a b)")
        Xf = X[:].rearrange("p a b -> p (a b)")

        (const_in, ones_ready, rows_in, cols_in, x_in, sil_t, sil_ready, rows_mm, prm_ready, tr_x, h0_ready) = sems(
            "const_in ones_ready rows_in cols_in x_in sil_t sil_ready rows_mm prm_ready tr_x h0_ready")
        araw_in = sems("araw_in0 araw_in1 araw_in2 araw_in3 araw_in4 araw_in5")
        (csp_hi, csp_lo, a_hi, a_lo_pool, a_lo_dve, a_mm, a_row, a_col) = sems("csp_hi csp_lo a_hi a_lo_pool a_lo_dve a_mm a_row a_col")
        (ada_ready,) = sems("ada_ready")
        (uf_ready, uhi_ready, ulo_ready) = sems("uf_ready uhi_ready ulo_ready")
        raw_in = sems("raw_in0 raw_in1")
        (w_hi, w_lo, mm_done, evac_done, res_done) = sems("w_hi w_lo mm_done evac_done res_done")
        (pad_zero, conv_step, tanh_done, silu_done, tr_done, tok_done, z_tanh, z_done, g_sq, g_in, g_tanh, g_done) = sems(
            "pad_zero conv_step tanh_done silu_done tr_done tok_done z_tanh z_done g_sq g_in g_tanh g_done")
        (ab_rows, wab_in, wab_hi, wab_lo, ab_mm, ab_ready, bc_in) = sems("ab_rows wab_in wab_hi wab_lo ab_mm ab_ready bc_in")
        (dve_chain, act_small, dve_small, cum_mm, gates_mm, gates_ready, gate_tanh, lru_at, lru_w, lru_sqrt, lru_y,
         gw_zero, gw_in) = sems(
            "dve_chain act_small dve_small cum_mm gates_mm gates_ready gate_tanh lru_at lru_w lru_sqrt lru_y gw_zero gw_in")
        (lru_scan, lru_pool) = sems("lru_scan lru_pool")
        (gc_in, ss_ready, qkn_ready, qkT_mm, qkT_ready, state_zero) = sems(
            "gc_in ss_ready qkn_ready qkT_mm qkT_ready state_zero")
        (gd_row, gd_g, gd_exp, gd_diff, gd_dec, gd_at0, gd_brow, gd_qk, gd_qk_ready, gd_at, gd_qd) = sems(
            "gd_row gd_g gd_exp gd_diff gd_dec gd_at0 gd_brow gd_qk gd_qk_ready gd_at gd_qd")
        (lv_ot, lv_p, lv_pm, lv_e, lv_et, lv_x, lv_xc, lv_xt, bk_ready, kd_ready, bv_ready, wt_mm, wt_ready) = sems(
            "lv_ot lv_p lv_pm lv_e lv_et lv_x lv_xc lv_xt bk_ready kd_ready bv_ready wt_mm wt_ready")
        (ch_v, ch_vnf, ch_vnb, ch_s, ch_o, ch_state, ch_out) = sems("ch_v ch_vnf ch_vnb ch_s ch_o ch_state ch_out")
        (o_sq, o_std, o_rcp, o_n, o_tr, o_z, o_y, glo_ready) = sems("o_sq o_std o_rcp o_n o_tr o_z o_y glo_ready")
        (ln_mean, ln_xc, ln_sq, ln_var, ln_std, ln_col, ln_rstd, ln_row, ln_xn, ln_h) = sems(
            "ln_mean ln_xc ln_sq ln_var ln_std ln_col ln_rstd ln_row ln_xn ln_h")
        (acc_step,) = sems("acc_step")
        (sq_sum, rn_sqrt) = sems("sq_sum rn_sqrt")
        (relu_done, hh_done, h1hi_done, h1lo_done) = sems("relu_done hh_done h1hi_done h1lo_done")
        (rope_in, lam_in, lam_ready, rot_mm, rope_step, kq_ready, vtr_mm, v_ready) = sems(
            "rope_in lam_in lam_ready rot_mm rope_step kq_ready vtr_mm v_ready")
        (sc_mm, mx_ready, ex_ready, pc_ready, pt_mm, pt_ready, pv_mm, o_ready) = sems(
            "sc_mm mx_ready ex_ready pc_ready pt_mm pt_ready pv_mm o_ready")
        (osq1, oss1, on_ready, ot_mm, y1_ready) = sems("osq1 oss1 on_ready ot_mm y1_ready")
        (fin_mm, fin_act, fin_dve, out_done) = sems("fin_mm fin_act fin_dve out_done")

        U_OUT0, U_MLP0, U_QKV, U_OUT1, U_MLP1, U_END = 24, 32, 96, 120, 128, 192
        R_OUT0, R_MLP0, R_OUT1, R_MLP1 = 0, 8, 40, 48
        E_QKV = 24
        EV_COLS = [c + 256 * t for c, n in ((QC, 6), (XC, 2), (ZC, 2), (GC, 2)) for t in range(n)]

        def pair_source(n):
            def view(w, r0, c0):
                return w[r0:r0 + D, c0:c0 + 256].rearrange("(k p) n -> p k n", p=P)
            u = 2 * n
            if u < U_OUT0:
                return view(I["ev_w_in"][0], 0, EV_COLS[n])
            if u < U_MLP0:
                return view(I["mix_w_out"][0], 0, 256 * (n - U_OUT0 // 2))
            if U_QKV <= u < U_OUT1:
                j = n - U_QKV // 2
                return view(I["od_w_qkv"][0], 0, (D + 256 * j) if j < 8 else 256 * (j - 8))
            if U_OUT1 <= u < U_MLP1:
                return view(I["mix_w_out"][1], 0, 256 * (n - U_OUT1 // 2))
            layer, m = (0, n - U_MLP0 // 2) if u < U_QKV else (1, n - U_MLP1 // 2)
            quarter, j = m // 8, m % 8
            if j < 4:
                return view(I["mlp_w1"][layer], 0, D * quarter + 256 * j)
            return view(I["mlp_w2"][layer], D * quarter, 256 * (j - 4))

        ADA1 = 2 * KD
        ADAN = 12 * KD
        ADA_PER = KD
        A_UNITS = (ADAN - ADA1) // ADA_PER
        assert A_UNITS <= 10

        def a_by_pool(i):
            return i % 2 == 0

        def ada_tiles(u):
            return range(ADA1 + ADA_PER * u, ADA1 + ADA_PER * (u + 1)) if u < A_UNITS else ()

        def a_buf(i):
            return araw[i % 6 // 3][:, i % 3]

        def wait_a_lo(eng, i):
            if a_by_pool(i):
                eng.wait_ge(a_lo_pool, i // 2 + 1)
            else:
                eng.wait_ge(a_lo_dve, i // 2 + 1)

        CHAIN_AT = (0, 3)
        NORM_BANKS = [(X, 2), (X, 0), (G, 2), (X, 2)]

        FIN_BANKS = [[(G, 0), (G, 1), (G, 2), (G, 3)], [(X, 2), (X, 3), (G, 0), (G, 1)]]

        block = ctx.enter_context(nc.Block())

        def small(o, n):
            return sm[:, o:o + n]
        abS = small(0, 96).rearrange("p (t w d h) -> p t w d h", t=6, w=2, d=2)
        spx = small(96, 56)
        spa, spz, sps, spp, spm = (small(152 + 56 * q, 56) for q in range(5))
        gS = small(432, 48)
        bS = small(480, 48)
        gamS = small(528, 48)
        glS = small(576, 48)
        bES = small(624, 48)
        cdS = small(672, 96)
        rnS = small(768, 48)
        hbS = small(816, 16)
        hsS = small(832, 8)
        nhsS = small(840, 8)
        albc = small(848, 8)
        dtbc = small(856, 8)
        ssS = small(864, 48)

        def m3(ap, a):
            return ap.rearrange("p (t r) -> p t r", t=a)

        def bc_cols(ap4):
            return ap4.unsqueeze(2).to_broadcast([P, 4, P])

        def bc_mask(ap):
            return ap.unsqueeze(1).to_broadcast([P, 4, P])

        ADA_LAT, ADA_CTX = 0, 1

        def adacol(layer, q, k, who):
            return ada[:, layer * 48 + q * 8 + k, who:who + 1]

        def half_of(d, s):
            return s if d == 0 else 1 - s

        def tile_of(d, p):
            return p if d == 0 else BWD_TILE[p]

        @block.sync
        def _(sp):
            sp.dma_start(ident[:], I["c_eye"]).then_inc(const_in, 16)
            sp.dma_start(sel[0:2], I["c_eye"][0:2, 0:2]).then_inc(const_in, 16)
            sp.dma_start(sel[2:4], I["c_eye"][0:2, 0:2]).then_inc(const_in, 16)
            sp.dma_start(cols[:, 0], I["c"][0].rearrange("(p j) -> p j", p=P)).then_inc(cols_in, 16)
            sp.dma_start(cols[:, 1], I["c_ctx"].rearrange("(p j) -> p j", p=P)).then_inc(cols_in, 16)

            sp.dma_start(xtok[:, 0:2], I["ctx"][0].rearrange("(t p) d -> p t d", p=P)).then_inc(x_in, 16)
            sp.dma_start(xtok[:, 2:6], I["x"][0].rearrange("(t p) d -> p t d", p=P)).then_inc(x_in, 16)
            sp.dma_start(rowsA[0:32], I["ln_g"].rearrange("l j (k p) -> (l j k) p", p=P)).then_inc(rows_in, 16)
            sp.dma_start(rowsA[32:64], I["ln_b"].rearrange("l j (k p) -> (l j k) p", p=P)).then_inc(rows_in, 16)
            sp.dma_start(rowsA[64:112], I["ev_qkv_conv"].rearrange("a t (k p) -> (a t k) p", p=P)).then_inc(rows_in, 16)
            sp.dma_start(rowsB[0:16], I["ev_lru_conv_w"].rearrange("a t (k p) -> (a t k) p", p=P)).then_inc(rows_in, 16)
            sp.dma_start(rowsB[16:20], I["ev_lru_conv_b"].rearrange("a (k p) -> (a k) p", p=P)).then_inc(rows_in, 16)
            sp.dma_start(rowsB[20:36], I["ev_lru_gate_b"].rearrange("a d g (k p) -> (a d g k) p", p=P)).then_inc(rows_in, 16)
            sp.dma_start(rowsB[36:44], I["ev_lru_lambda"].rearrange("a d (k p) -> (a d k) p", p=P)).then_inc(rows_in, 16)
            sp.dma_start(rowsB[44:45], I["ev_gdn_norm"]).then_inc(rows_in, 16)
            sp.dma_start(rowsB[45:46], I["od_subln"]).then_inc(rows_in, 16)
            sp.dma_start(rowsC[0:96], I["ada_b"].rearrange("l (k p) -> (l k) p", p=P)).then_inc(rows_in, 16)
            def load_pair(n):
                if n >= 2:
                    sp.wait_ge(w_lo, 2 * (n - 1))
                sp.dma_start(raw[:, n % 2], pair_source(n)).then_inc(raw_in[n % 2], 16)

            def load_atile(i):
                if i >= 6:
                    wait_a_lo(sp, i - 6)
                sp.dma_start(a_buf(i), I["ada_w"][i // 48].rearrange("(p j) n -> p j n", p=P)[
                    :, :, (i % 48) * P:(i % 48 + 1) * P]).then_inc(araw_in[i % 6], 16)

            for i in range(ADA1):
                load_atile(i)
            load_pair(0)
            load_pair(1)
            for i in range(ADA1, ADA1 + 6):
                load_atile(i)
            sp.wait_ge(ulo_ready, 8)
            sp.dma_start(wab[:], I["ev_w_in"][0][:, AC:AC + 16].rearrange("(k p) n -> p k n", p=P)).then_inc(wab_in, 16)
            for u in range(A_UNITS):
                for i in ada_tiles(u):
                    if i + 6 < ADAN:
                        load_atile(i + 6)
                    if u % 2 == 0 and i % ADA_PER == 2:
                        load_pair(u // 2 + 2)
            sp.wait_ge(a_col, ADAN // 4)
            sp.dma_start(albc, I["ev_a_log"].rearrange("a d h -> a (d h)").to_broadcast([P, 8])).then_inc(bc_in, 16)
            sp.dma_start(dtbc, I["ev_dt_bias"].rearrange("a d h -> a (d h)").to_broadcast([P, 8])).then_inc(bc_in, 16)

            for n in range(A_UNITS // 2 + 2, U_OUT0 // 2):
                load_pair(n)
            sp.wait_ge(gw_zero, 1)
            for e in range(2):
                for d in range(2):
                    for g in range(2):
                        sp.dma_start(gw[64 * e:64 * e + 64, (2 * d + g) * 4:(2 * d + g) * 4 + 4, 64 * e:64 * e + 64],
                                     I["ev_lru_gate_w"][0, d, g].rearrange("(c e) i j -> e i c j", e=2)[e]).then_inc(gw_in, 16)
            sp.wait_ge(w_lo, U_OUT0)
            sp.dma_start(gc[:], I["c_gdn"]).then_inc(gc_in, 16)
            sp.wait_ge(wt_ready, 12)
            for n in range(U_OUT0 // 2, U_QKV // 2 + 2):
                load_pair(n)
            sp.wait_ge(ln_h, 16)
            sp.dma_start(rc[:], I["c_rope"]).then_inc(rope_in, 16)
            sp.dma_start(lrow[:], I["od_lambda"].rearrange("a r d -> a (r d)").to_broadcast([P, 256])).then_inc(lam_in, 16)
            for n in range(U_QKV // 2 + 2, U_END // 2):
                load_pair(n)
            for w in range(2):
                for t in range(4):
                    sp.wait_ge((fin_act, fin_dve)[t % 2], 2 * w + t // 2 + 1)
                    sp.dma_start(out[0, t * P:(t + 1) * P, 512 * w:512 * w + 512], otok[:, t, 512 * w:512 * w + 512]).then_inc(out_done, 16)
            sp.wait_ge(out_done, 128)

        @block.gpsimd
        def _(pool):
            nc.gpsimd.memset(ones[:], 1.0).then_inc(ones_ready, 1)
            nc.gpsimd.memset(eps2[:], EPS / ALPHA ** 2).then_inc(ones_ready, 1)
            nc.gpsimd.memset(onesD[:], 1.0 / D).then_inc(ones_ready, 1)
            nc.gpsimd.memset(eps1[:], EPS).then_inc(ones_ready, 1)

            def modulate(m, ubase, layer, qs, span, ready, n_ready):
                for k in range(KD):
                    pool.wait_ge(ready, n_ready + k + 1)
                    if ubase or k >= 2:
                        pool.wait_ge(ulo_ready, ubase + max(0, k - 1))
                    for s, e, bank in PIECES:
                        if s >= span[0]:
                            who = ADA_CTX if bank == 0 else ADA_LAT
                            last = nc.gpsimd.tensor_scalar(uf[:, k % 2, s:e], hT[:, k, s:e], adacol(layer, qs + 1, k, who),
                                                           adacol(layer, qs, k, who), ALU.mult, ALU.add)
                    last.then_inc(uf_ready, 1)

            def sum_tiles(c, span, rbase):
                a, b = span
                for k in range(1, KD - 1):
                    pool.wait_ge(res_done, rbase + k + 1)
                    if k == 1:
                        if c:
                            pool.wait_ge(ln_mean, c)
                        first = hT[:, 0, a:b]
                    else:
                        pool.wait_ge(acc_step, 6 * c + k - 1)
                        first = acc[:, a:b]
                    nc.gpsimd.tensor_tensor(acc[:, a:b], first, hT[:, k, a:b], ALU.add).then_inc(acc_step, 1)

            def ada_remainders(a, b):
                for i in range(a, b):
                    if a_by_pool(i):
                        pool.wait_ge(a_hi, i + 1)
                        nc.gpsimd.tensor_tensor(alo[:, i % 3], a_buf(i), ahi[:, i % 3].bitcast(F32),
                                                ALU.subtract).then_inc(a_lo_pool, 1)

            ada_remainders(0, ADA1)
            pool.wait_ge(ada_ready, 2)
            modulate(0, 0, 0, 0, (0, TOK), h0_ready, 0)
            pool.wait_ge(ulo_ready, 8)
            nc.gpsimd.memset(cbuf[:], 0.0).then_inc(pad_zero, 1)
            ada_remainders(ADA1, ADAN)
            pool.wait_ge(tok_done, 12)
            pool.wait_ge(conv_step, 64)
            nc.gpsimd.memset(gw[:], 0.0).then_inc(gw_zero, 1)
            for c in range(2):
                pool.wait_ge(lru_scan, c + 1)
                nc.gpsimd.tensor_tensor(yl[:, c], yl[:, c], lw[:, c], ALU.add).then_inc(lru_pool, 1)
                pool.wait_ge(lru_pool, 2 * c + 1)
                nc.gpsimd.tensor_tensor(gT[:, c], gT[:, c], yl[:, c], ALU.mult).then_inc(lru_pool, 1)
            pool.wait_ge(lru_y, 6)
            nc.gpsimd.memset(vn[0][:], 0.0).then_inc(state_zero, 1)
            nc.gpsimd.memset(vn[1][:], 0.0).then_inc(state_zero, 1)
            nc.gpsimd.memset(S[:], 0.0).then_inc(state_zero, 1)
            pool.wait_ge(gc_in, 16)

            for p in range(6):
                for d in range(2):
                    n = 2 * p + d
                    t = tile_of(d, p)
                    pool.wait_ge(gd_exp, n + 1)
                    pool.wait_ge(qkT_ready, 12)
                    nc.gpsimd.tensor_tensor(qd[d][p % 2][:], qd[d][p % 2][:], qT[:, :, t * P:(t + 1) * P],
                                            ALU.mult).then_inc(gd_qd, 1)
                for lev in range(LEVELS):
                    for d in range(2):
                        n = 2 * p + d
                        pool.wait_ge(gd_at, n + 1)
                        if lev >= 2 or p > 0:
                            pool.wait_ge(lv_p, 2 * (LEVELS * p + lev - 2) + d + 1)
                        if lev == 2:
                            pool.wait_ge(lv_xt, 2 * LEVELS * p + d + 1)
                        nc.gpsimd.tensor_tensor(ot[d][lev % 2][:], att[d][:], bc_mask(gc[:, CG_LEV + 2 * lev + d]),
                                                ALU.mult).then_inc(lv_ot, 1)
                for d in range(2):
                    n = 2 * p + d
                    t = tile_of(d, p)
                    r = slice(4 * d, 4 * d + 4)
                    if p > 0:
                        pool.wait_ge(wt_mm, n - 1)
                    nc.gpsimd.tensor_tensor(dg[d][:], ktok[:, t], bc_cols(m3(bES, 6)[:, p, r]), ALU.mult).then_inc(bk_ready, 1)
                    if p > 0:
                        pool.wait_ge(ch_o, 2 * p)
                    nc.gpsimd.tensor_tensor(kd[d][:], ktok[:, t], bc_cols(m3(glS, 6)[:, p, r]), ALU.mult).then_inc(kd_ready, 1)
                    nc.gpsimd.tensor_tensor(bv[d][:], vtok[:, t], bc_cols(m3(bS, 6)[:, p, r]), ALU.mult).then_inc(bv_ready, 1)

            for k in range(4, KD):
                pool.wait_ge(ch_o, 12)
                pool.wait_ge(uhi_ready, 8 + k - 3)
                nc.gpsimd.tensor_tensor(ulo[:, k], gT[:, k % 4], uhi[:, k].bitcast(F32), ALU.subtract).then_inc(glo_ready, 1)

            pool.wait_ge(ada_ready, 5)
            sum_tiles(0, (0, TOK), R_OUT0)
            modulate(1, 16, 0, 3, (0, TOK), ln_h, 0)
            sum_tiles(1, (0, TOK), R_MLP0 + 24)
            modulate(2, 24, 1, 0, (0, TOK), ln_h, 8)
            sum_tiles(2, (CTX, TOK), R_OUT1)
            modulate(3, 40, 1, 3, (CTX, TOK), ln_h, 16)
            sum_tiles(3, (CTX, TOK), R_MLP1 + 24)

        @block.scalar
        def _(act):
            def split_hi(par, unit):
                act.wait_ge(raw_in[(par // 2) % 2], 16 * (unit // 4 + 1))
                if unit >= 2:
                    act.wait_ge(mm_done, unit - 1)
                nc.scalar.activation(whi[:, par % 2], raw[:, (par // 2) % 2, :, (par % 2) * P:(par % 2 + 1) * P],
                                     ACT.Copy).then_inc(w_hi, 1)

            def slot(par, piece):
                start, stop, bank = piece
                return G[:, 2 * (par % 2) + bank, 0:stop - start]

            act.wait_ge(cols_in, 32)
            nc.scalar.activation(silt[:], cols[:], ACT.Tanh, scale=0.5).then_inc(sil_t, 1)
            act.wait_ge(sil_ready, 1)
            nc.scalar.activation(csp[:, :, 0:2], sil[:].rearrange("p w k -> p k w"), ACT.Copy).then_inc(csp_hi, 1)

            def ada_hi(i):
                act.wait_ge(araw_in[i % 6], 16 * (i // 6 + 1))
                if i >= 3:
                    act.wait_ge(a_mm, i - 2)
                nc.scalar.activation(ahi[:, i % 3], a_buf(i), ACT.Copy).then_inc(a_hi, 1)

            def ada_rows(g):
                act.wait_ge(a_mm, 4 * g + 4)
                if g >= 2:
                    act.wait_ge(a_col, g - 1)
                nc.scalar.activation(grow[:, g % 2], X[0:4, 3, :], ACT.Copy).then_inc(a_row, 1)

            def ada_his(a, b):
                for i in range(a, min(b, ADAN)):
                    ada_hi(i)
                    if i % 4 == 0 and i not in (0, ADA1):
                        ada_rows(i // 4 - 1)

            ada_his(0, 3)
            for k in range(KD):
                act.wait_ge(tr_x, k + 1)
                for pc_ in PIECES:
                    last = nc.scalar.activation(hT[:, k, pc_[0]:pc_[1]], slot(k, pc_), ACT.Copy)
                last.then_inc(h0_ready, 1)
            ada_his(3, ADA1)
            ada_rows(ADA1 // 4 - 1)

            def round_u(m, k, span, units):
                act.wait_ge(uf_ready, 8 * m + k + 1)
                if units:
                    act.wait_ge(mm_done, units)
                nc.scalar.activation(uhi[:, k, span[0]:span[1]], uf[:, k % 2, span[0]:span[1]], ACT.Copy).then_inc(uhi_ready, 1)

            split_hi(0, 0)
            for k in range(KD):
                round_u(0, k, (0, TOK), 0)
                if k == 4:
                    ada_hi(ADA1)
                if k == 6:
                    ada_hi(ADA1 + 1)
            act.wait_ge(wab_in, 16)
            nc.scalar.activation(wabhi[:], wab[:], ACT.Copy).then_inc(wab_hi, 1)

            def gates_in():
                act.wait_ge(ab_mm, 2)
                psab = X[:, 2, 0:96].rearrange("p (t w d h) -> p t w d h", t=6, w=2, d=2)
                nc.scalar.activation(abS[:, :, :, 0, :], psab[:, :, :, 0, :], ACT.Copy)
                for p in range(6):
                    last = nc.scalar.activation(abS[:, p, :, 1, :], psab[:, BWD_TILE[p], :, 1, :], ACT.Copy)
                last.then_inc(ab_ready, 1)

            def gates_exp():
                act.wait_ge(dve_small, 1)
                nc.scalar.activation(spz, spa, ACT.Exp).then_inc(act_small, 1)
                act.wait_ge(bc_in, 32)
                nc.scalar.activation(albc, albc, ACT.Exp).then_inc(act_small, 1)
                for w in range(6):
                    last = nc.scalar.activation(m3(bS, 6)[:, w].rearrange("p (d h) -> p d h", d=2), abS[:, w, 1], ACT.Tanh,
                                                scale=0.5)
                last.then_inc(act_small, 1)

            act.wait_ge(pad_zero, 1)
            for u in range(U_OUT0 + 2):
                if u + 1 < U_OUT0:
                    split_hi((u + 1) % 4, u + 1)
                if u < A_UNITS:
                    ada_his(ADA1 + ADA_PER * u + 2, ADA1 + ADA_PER * u + 5)
                if 1 <= u <= 12:
                    act.wait_ge(conv_step, 4 * u)
                    if u >= 3:
                        act.wait_ge(silu_done, u - 2)
                    nc.scalar.activation(tbuf[:, (u - 1) % 2], ybuf[:, (u - 1) % 2], ACT.Tanh).then_inc(tanh_done, 1)
                if u < A_UNITS:
                    ada_his(ADA1 + ADA_PER * u + 5, ADA1 + ADA_PER * u + 10)
                if u == A_UNITS - 1:
                    ada_rows(ADAN // 4 - 1)
                if u == 18:
                    act.wait_ge(ab_mm, 1)
                    nc.scalar.activation(abT[:, 0:CTX], X[0:16, 0, 0:CTX], ACT.Copy)
                    nc.scalar.activation(abT[:, CTX:TOK], X[0:16, 1, :], ACT.Copy).then_inc(ab_rows, 1)
                if 14 <= u < 20:
                    act.wait_ge(tok_done, 12)
                    for r in range(8):
                        n = 8 * (u - 14) + r
                        if n >= 2:
                            act.wait_ge(sq_sum, n - 1)
                        src = (qtok, ktok)[r // 4]
                        nc.scalar.activation(nsq[:, n % 2], src[:, u - 14, r % 4], ACT.Square,
                                             accum_out=ssS[:, n:n + 1]).then_inc(sq_sum, 1)
                if u == 20:
                    act.wait_ge(ss_ready, 1)
                    nc.scalar.activation(rnS, ssS, ACT.Sqrt).then_inc(rn_sqrt, 1)
                if u == 19:
                    gates_in()
                if u == 21:
                    gates_exp()
                if 2 <= u <= 13:
                    act.wait_ge(tr_done, u - 1)
                    dst = (qtok, ktok, vtok)[(u - 2) // 4]
                    nc.scalar.activation(dst[:, :, (u - 2) % 4, :], Xf[:, 0:TOK].rearrange("p (t c) -> p t c", t=NT),
                                         ACT.Copy).then_inc(tok_done, 1)
                if u >= U_OUT0:
                    continue
                act.wait_ge(mm_done, u + 1)
                if u < 16:
                    if u >= 2:
                        act.wait_ge(conv_step, 4 * (u - 1))
                    nc.scalar.activation(cbuf[:, u % 2, 2:2 + CTX], slot(u, PIECES[0]), ACT.Copy)
                    nc.scalar.activation(cbuf[:, u % 2, 4 + CTX:4 + TOK], slot(u, PIECES[1]), ACT.Copy).then_inc(evac_done, 1)
                else:
                    dst = zT if u < 20 else gT
                    for pc_ in PIECES:
                        last = nc.scalar.activation(dst[:, u % 4, pc_[0]:pc_[1]], slot(u, pc_), ACT.Copy, scale=0.5)
                    last.then_inc(evac_done, 1)
                    act.wait_ge(evac_done, u + 1)
                    if u < 20:
                        if u >= 18:
                            act.wait_ge(z_done, u - 17)
                        else:
                            act.wait_ge(silu_done, 12)
                        nc.scalar.activation(tbuf[:, u % 2, 0:TOK], zT[:, u % 4], ACT.Tanh).then_inc(z_tanh, 1)
                    else:
                        if u >= 22:
                            act.wait_ge(g_done, u - 21)
                        else:
                            act.wait_ge(z_done, u - 17)
                        nc.scalar.activation(tbuf[:, u % 2, 0:TOK], gT[:, u % 4], ACT.Square).then_inc(g_sq, 1)
                        act.wait_ge(g_in, 2 * (u - 19))
                        nc.scalar.activation(tbuf[:, u % 2, 0:TOK], tbuf[:, u % 2, 0:TOK], ACT.Tanh).then_inc(g_tanh, 1)

            act.wait_ge(dve_small, 4)
            act.wait_ge(cum_mm, 2)
            nc.scalar.activation(glS, glS, ACT.Exp).then_inc(act_small, 1)
            nc.scalar.activation(bES, gamS, ACT.Exp).then_inc(act_small, 1)
            nc.scalar.activation(cdS, X[:, 2, 128:224], ACT.Exp).then_inc(act_small, 1)

            for d in range(2):
                for c in range(4):
                    n = 4 * d + c
                    act.wait_ge(gates_mm, n + 1)
                    act.wait_ge(dve_small, 2)
                    if n >= 2:
                        act.wait_ge(lru_w, n - 1)
                    if d == 1:
                        act.wait_ge(lru_y, c + 1)
                    B = X if n % 2 else G
                    for pc_ in PIECES:
                        nc.scalar.activation(trr[n % 2][:, pc_[0]:pc_[1]], B[:, pc_[2], 0:pc_[1] - pc_[0]], ACT.Tanh, scale=0.5,
                                             bias=hbS[:, (2 * d) * 4 + c:(2 * d) * 4 + c + 1])
                    for pc_ in PIECES:
                        last = nc.scalar.activation(tii[n % 2][:, pc_[0]:pc_[1]], B[:, 2 + pc_[2], 0:pc_[1] - pc_[0]], ACT.Tanh,
                                                    scale=0.5, bias=hbS[:, (2 * d + 1) * 4 + c:(2 * d + 1) * 4 + c + 1])
                    last.then_inc(gate_tanh, 1)
                    act.wait_ge(gate_tanh, n + 1)
                    nc.scalar.activation(la[:, c], trr[n % 2][:], ACT.Exp, scale=hsS[:, n:n + 1], bias=hsS[:, n:n + 1])
                    nc.scalar.activation(thh[n % 2][:], trr[n % 2][:], ACT.Tanh, scale=nhsS[:, n:n + 1],
                                         bias=nhsS[:, n:n + 1]).then_inc(lru_at, 1)
                act.wait_ge(lru_w, 4 * d + 4)
                nc.scalar.activation(lw[:], lw[:], ACT.Sqrt, scale=0.25).then_inc(lru_sqrt, 1)

            act.wait_ge(lru_pool, 4)
            act.wait_ge(lru_y, 6)
            for t in range(NT):
                for w, dst in ((0, qT), (1, kT)):
                    act.wait_ge(qkT_mm, 2 * t + w + 1)
                    nc.scalar.activation(dst[:, :, t * P:(t + 1) * P], X[:, w, :].rearrange("p (h c) -> p h c", h=4),
                                         ACT.Copy).then_inc(qkT_ready, 1)

            def chain_act(p, s):
                c = 2 * p + s
                act.wait_ge(ch_v, 2 * c + 1)
                act.wait_ge(state_zero, 3)
                if c >= 2:
                    act.wait_ge(ch_o, c - 1)
                h = 64 * half_of(0, s)
                nc.scalar.activation(vn[s][h:h + 64, 0:4], X[h:h + 64, 0, :].rearrange("p (r c) -> p r c", r=4),
                                     ACT.Copy).then_inc(ch_vnf, 1)

            squared = [0]

            def square_out(t):
                for h in range(HEADS):
                    n = squared[0]
                    if n >= 2:
                        act.wait_ge(o_sq, n - 1)
                    else:
                        act.wait_ge(wt_mm, 12)
                    nc.scalar.activation(att[0][:, n % 2], otk[:, t, h], ACT.Square,
                                         accum_out=orn[:, t * HEADS + h:t * HEADS + h + 1]).then_inc(o_sq, 1)
                    squared[0] += 1

            for p in range(7):
                if p < 6:
                    for d in range(2):
                        n = 2 * p + d
                        act.wait_ge(gd_row, n + 1)
                        if p >= 2:
                            act.wait_ge(ch_o, 2 * (p - 1))
                        nc.scalar.activation(qd[d][p % 2][:], G[:, 2 * d, :].rearrange("p (r c) -> p r c", r=4),
                                             ACT.Exp).then_inc(gd_exp, 1)
                    for d in range(2):
                        n = 2 * p + d
                        act.wait_ge(gd_diff, n + 1)
                        nc.scalar.activation(dm[d][:], dm[d][:], ACT.Exp).then_inc(gd_dec, 1)
                for lev in range(LEVELS):
                    if p < 6 and lev > 0:
                        for d in range(2):
                            act.wait_ge(lv_p, 2 * (LEVELS * p + lev) + d + 1)
                            if lev > 1:
                                act.wait_ge(lv_et, 2 * (5 * p + lev - 2) + d + 1)
                            nc.scalar.activation(pm[d][:], G[:, 2 * d, :].rearrange("p (r c) -> p r c", r=4),
                                                 ACT.Copy).then_inc(lv_pm, 1)
                        for d in range(2):
                            if lev < 5:
                                act.wait_ge(lv_e, 2 * (4 * p + lev - 1) + d + 1)
                                nc.scalar.activation(xx[d][:], G[:, 2 * d + 1, :].rearrange("p (r c) -> p r c", r=4),
                                                     ACT.Copy).then_inc(lv_xc, 1)
                    if p >= 1 and lev in CHAIN_AT:
                        chain_act(p - 1, CHAIN_AT.index(lev))
                    if p == 6 and lev == 2:
                        act.wait_ge(ch_out, 10)
                        for t in (0, 1, 3, 4):
                            square_out(t)
                if p < 6:
                    for d in range(2):
                        n = 2 * p + d
                        act.wait_ge(wt_mm, n + 1)
                        if p >= 1:
                            act.wait_ge(ch_o, 2 * p)
                        nc.scalar.activation(wt[d][:], G[:, 2 * d + 1, :].rearrange("p (r c) -> p r c", r=4), ACT.Copy,
                                             scale=-1.0).then_inc(wt_ready, 1)

            split_hi(0, U_OUT0)
            for k in range(4, KD):
                nc.scalar.activation(uhi[:, k], gT[:, k % 4], ACT.Copy).then_inc(uhi_ready, 1)
            act.wait_ge(ch_out, 12)
            for t in (2, 5):
                square_out(t)
            act.wait_ge(o_sq, 24)
            nc.scalar.activation(orn[:], orn[:], ACT.Sqrt, scale=1.0 / P, bias=eps1[:]).then_inc(o_std, 1)
            for k in range(4):
                act.wait_ge(o_y, k + 1)
                nc.scalar.activation(uhi[:, k], oT[:, k], ACT.Copy).then_inc(uhi_ready, 1)
            for j in range(8):
                split_hi((j + 1) % 4, U_OUT0 + j + 1)

            def layer_norm(c, span, m=None, units=0):
                a, b = span
                for k in range(KD):
                    act.wait_ge(ln_xc, 8 * c + k + 1)
                    if k >= 2:
                        act.wait_ge(ln_var, 8 * c + k - 1)
                    nc.scalar.activation(lsq[:, k % 2, a:b], hT[:, k, a:b], ACT.Square).then_inc(ln_sq, 1)
                act.wait_ge(ln_var, 8 * c + 8)
                for s, e, bank in PIECES:
                    if s >= a:
                        last = nc.scalar.activation(lstd[:, s:e], X[0:1, 2 + bank, 0:e - s], ACT.Sqrt, bias=eps2[0:1, 0:1])
                last.then_inc(ln_std, 1)
                for k in range(KD):
                    act.wait_ge(ln_xn, 8 * c + k + 1)
                    nc.scalar.activation(hT[:, k, a:b], hT[:, k, a:b], ACT.Identity, scale=prmA[:, c * 8 + k:c * 8 + k + 1],
                                         bias=prmA[:, 32 + c * 8 + k:32 + c * 8 + k + 1]).then_inc(ln_h, 1)
                    if m is not None and k >= 1:
                        round_u(m, k - 1, span, units)
                if m is not None:
                    round_u(m, KD - 1, span, units)

            def mlp(layer, q, span, u0, h0, last_quarter):
                base = u0 + 16 * q
                def split(j):
                    pair_uses = (u0 // 4 + 4 * q) + (j // 4) + 1
                    act.wait_ge(raw_in[(j // 2) % 2], 16 * pair_uses)
                    act.wait_ge(mm_done, base + (j - 1))
                    nc.scalar.activation(whi[:, j % 2], raw[:, (j // 2) % 2, :, (j % 2) * P:(j % 2 + 1) * P],
                                         ACT.Copy).then_inc(w_hi, 1)
                def round_h(j):
                    act.wait_ge(hh_done, h0 + 8 * q + (j + 3))
                    act.wait_ge(mm_done, base)
                    nc.scalar.activation(h1hi[:, j, span[0]:span[1]], hh[:, j % 2, span[0]:span[1]],
                                         ACT.Copy).then_inc(h1hi_done, 1)
                for j in range(8):
                    split(j + 1)
                    act.wait_ge(mm_done, base + (j + 1))
                    act.wait_ge(hh_done, h0 + 8 * q + (j + 1))
                    for s, e, bank in PIECES:
                        if s >= span[0]:
                            last = nc.scalar.activation(rt[:, j % 2, s:e], G[:, 2 * (j % 2) + bank, 0:e - s], ACT.Relu)
                    last.then_inc(relu_done, 1)
                    if j >= 1:
                        round_h(j - 1)
                round_h(7)
                for f in range(8):
                    if not (last_quarter and f == 7):
                        split(8 + f + 1)

            layer_norm(0, (0, TOK), 1, U_MLP0)
            with act.Fori(0, 4) as q:
                mlp(0, q, (0, TOK), U_MLP0, 0, False)
            layer_norm(1, (0, TOK), 2, U_QKV)

            for u in range(U_QKV, U_OUT1):
                j = u - U_QKV
                if u + 1 < U_OUT1 + 1:
                    split_hi((u + 1) % 4, u + 1)
                if 9 <= j <= 16:
                    act.wait_ge(vtr_mm, j - 8)
                    nc.scalar.activation(v1[:, :, (j - 9) * P:(j - 8) * P], Xf[:, 1024:1024 + TOK].rearrange("p (t c) -> p t c", t=NT),
                                         ACT.Copy).then_inc(v_ready, 1)
                act.wait_ge(mm_done, u + 1)
                if j < 8:
                    if j >= 2:
                        act.wait_ge(kq_ready, j - 1)
                    nc.scalar.activation(k1[:, j, 0:CTX], slot(u, PIECES[0]), ACT.Copy)
                    nc.scalar.activation(kb[:, j % 2, CTX:TOK], slot(u, PIECES[1]), ACT.Copy).then_inc(evac_done, 1)
                elif j < 16:
                    act.wait_ge(kq_ready, min(8, j - 1))
                    if j >= 10:
                        act.wait_ge(vtr_mm, j - 9)
                    nc.scalar.activation(kb[:, j % 2, 0:CTX], slot(u, PIECES[0]), ACT.Copy)
                    nc.scalar.activation(kb[:, j % 2, CTX:TOK], slot(u, PIECES[1]), ACT.Copy).then_inc(evac_done, 1)
                else:
                    act.wait_ge(vtr_mm, min(8, j - 9))
                    if j >= 18:
                        act.wait_ge(kq_ready, j - 9)
                    nc.scalar.activation(kb[:, j % 2, CTX:TOK], slot(u, PIECES[1]), ACT.Copy, scale=0.125).then_inc(evac_done, 1)

            act.wait_ge(lam_ready, 1)
            nc.scalar.activation(nlam[:, 2:4], nlam[:, 0:2], ACT.Exp).then_inc(lam_ready, 1)
            for it in range(36):
                if it < 32:
                    for m in range(2):
                        act.wait_ge(mx_ready, 2 * it + m + 1)
                        if it >= 2:
                            act.wait_ge(pc_ready, it - 1)
                        nc.scalar.activation(pp[:, it % 2, m], Gf[:, 1024 * m:1024 * m + TOK], ACT.Exp,
                                             bias=nmx[:, it % 2, m:m + 1], accum_out=rsm[:, it % 2, m:m + 1]).then_inc(ex_ready, 1)
                if it >= 4:
                    i = it - 4
                    h, qt = i // 4, i % 4
                    act.wait_ge(o_ready, i + 1)
                    if i >= 2:
                        act.wait_ge(osq1, i - 1)
                    nc.scalar.activation(oq[:, i % 2], oo[:, qt, h * P:(h + 1) * P], ACT.Square,
                                         accum_out=ors[:, 0, 8 * qt + h:8 * qt + h + 1]).then_inc(osq1, 1)
                if 2 <= it <= 33:
                    i = it - 2
                    act.wait_ge(pt_mm, i + 1)
                    if i >= 2:
                        act.wait_ge(pv_mm, i - 1)
                    nc.scalar.activation(pT[:, i % 2], Xf[:, 0:TOK], ACT.Copy).then_inc(pt_ready, 1)
            act.wait_ge(oss1, 1)
            nc.scalar.activation(ors[:, 1], ors[:, 0], ACT.Sqrt).then_inc(act_small, 1)
            for k in range(KD):
                act.wait_ge(ot_mm, k + 1)
                nc.scalar.activation(y1[:, k], X[:, k % 2, :], ACT.Copy, scale=subg[:, 0:1]).then_inc(y1_ready, 1)
            act.wait_ge(y1_ready, 8)
            act.wait_ge(ot_mm, 8)
            for k in range(KD):
                nc.scalar.activation(uhi[:, k, CTX:TOK], y1[:, k], ACT.Copy).then_inc(uhi_ready, 1)
            for j in range(8):
                split_hi((j + 1) % 4, U_OUT1 + j + 1)
            layer_norm(2, (CTX, TOK), 3, U_MLP1)
            with act.Fori(0, 3) as q:
                mlp(1, q, (CTX, TOK), U_MLP1, 32, False)
            mlp(1, 3, (CTX, TOK), U_MLP1, 32, True)
            layer_norm(3, (CTX, TOK))
            for w in range(2):
                for t in (0, 2):
                    act.wait_ge(fin_mm, 4 * w + t + 1)
                    B, b = FIN_BANKS[w][t]
                    nc.scalar.activation(otok[:, t, 512 * w:512 * w + 512], B[:, b, :], ACT.Copy).then_inc(fin_act, 1)

        @block.vector
        def _(dve):
            V = nc.vector
            chain = [0]

            def link(ins):
                chain[0] += 1
                ins.then_inc(dve_chain, 1)
                dve.wait_ge(dve_chain, chain[0])

            def split_lo(par, unit):
                dve.wait_ge(w_hi, unit + 1)
                V.tensor_tensor(wlo[:, par % 2], raw[:, (par // 2) % 2, :, (par % 2) * P:(par % 2 + 1) * P],
                                whi[:, par % 2].bitcast(F32), ALU.subtract).then_inc(w_lo, 1)

            def low_u(ubase, k, span):
                a, b = span
                dve.wait_ge(uhi_ready, ubase + k + 1)
                V.tensor_tensor(ulo[:, k, a:b], uf[:, k % 2, a:b], uhi[:, k, a:b].bitcast(F32), ALU.subtract).then_inc(ulo_ready, 1)

            dve.sem_inc(hh_done, 2)
            dve.sem_inc(h1lo_done, 2)
            dve.wait_ge(sil_t, 1)
            link(V.scalar_tensor_tensor(sil[:], silt[:], 1.0, cols[:], ALU.add, ALU.mult))
            V.tensor_scalar(sil[:], sil[:], 0.5, None, ALU.mult).then_inc(sil_ready, 1)
            dve.wait_ge(csp_hi, 1)
            V.tensor_tensor(csp[:, :, 2:4], sil[:].rearrange("p w k -> p k w"), csp[:, :, 0:2].bitcast(F32),
                            ALU.subtract).then_inc(csp_lo, 1)
            def ada_remainder(i):
                dve.wait_ge(a_hi, i + 1)
                V.tensor_tensor(alo[:, i % 3], a_buf(i), ahi[:, i % 3].bitcast(F32), ALU.subtract).then_inc(a_lo_dve, 1)

            def ada_lo(u, j):
                if u < A_UNITS:
                    ada_remainder(ADA1 + ADA_PER * u + j)

            ada_remainder(1)
            dve.wait_ge(rows_mm, 3)
            V.tensor_scalar(prmA[:], X[:, 2, 256:368], 1.0, None, ALU.mult)
            V.tensor_scalar(prmB[:], X[:, 2, 368:414], 1.0, None, ALU.mult)
            V.tensor_scalar(adab[:], X[:, 2, 414:510], 1.0, None, ALU.mult).then_inc(prm_ready, 1)
            dve.wait_ge(prm_ready, 1)
            V.tensor_scalar(convw[:], prmA[:, 64:112], 0.5, None, ALU.mult)
            link(V.tensor_scalar(subg[:, 0:1], prmB[:, 45:46], 1.0 - LAM_INIT, None, ALU.mult))
            for i in range(3, ADA1, 2):
                ada_remainder(i)
            dve.wait_ge(a_col, ADA1 // 4)
            V.tensor_tensor(ada[:, 0:ADA1], X[:, 2, 0:2 * ADA1].rearrange("p (k w) -> p k w", w=2),
                            adab[:, 0:ADA1].unsqueeze(2).to_broadcast([P, ADA1, 2]), ALU.add).then_inc(ada_ready, 1)
            dve.wait_ge(ada_ready, 1)
            V.tensor_scalar(ada[:, KD:2 * KD], ada[:, KD:2 * KD], 1.0, None, ALU.add).then_inc(ada_ready, 1)
            dve.wait_ge(ada_ready, 2)
            split_lo(0, 0)
            for k in range(KD):
                low_u(0, k, (0, TOK))
            dve.wait_ge(wab_hi, 1)
            V.tensor_tensor(wablo[:], wab[:], wabhi[:].bitcast(F32), ALU.subtract).then_inc(wab_lo, 1)

            def softplus_in():
                dve.wait_ge(ab_ready, 1)
                dve.wait_ge(bc_in, 32)
                for p in range(6):
                    V.tensor_tensor(spx[:, 8 * p:8 * p + 8].rearrange("p (d h) -> p d h", d=2), abS[:, p, 0],
                                    dtbc.rearrange("p (d h) -> p d h", d=2), ALU.add)
                link(V.tensor_scalar(spx[:, 48:56], prmB[:, 36:44], -1.0, None, ALU.mult))
                link(V.tensor_scalar(spm, spx, -1.0, None, ALU.mult))
                V.tensor_tensor(spa, spx, spm, ALU.min).then_inc(dve_small, 1)
                V.tensor_scalar(spx, spx, 0.0, None, ALU.max)
                V.tensor_scalar(hbS, prmB[:, 20:36], 0.5, None, ALU.mult)

            def softplus():
                dve.wait_ge(act_small, 1)
                link(V.tensor_scalar(spm, spz, 2.0, None, ALU.add))
                link(V.reciprocal(spm, spm))
                link(V.tensor_tensor(spz, spz, spm, ALU.mult))
                link(V.tensor_tensor(sps, spz, spz, ALU.mult))
                link(V.tensor_scalar(spp, sps, 1.0 / 17, 1.0 / 15, ALU.mult, ALU.add))
                for deg in (13, 11, 9, 7, 5, 3, 1):
                    link(V.tensor_tensor(spp, spp, sps, ALU.mult))
                    link(V.tensor_scalar(spp, spp, 1.0 / deg, None, ALU.add))
                link(V.tensor_tensor(spp, spp, spz, ALU.mult))
                link(V.scalar_tensor_tensor(spp, spp, 2.0, spx, ALU.mult, ALU.add))
                V.tensor_scalar(hsS, spp[:, 48:56], -4.0, None, ALU.mult)
                V.tensor_scalar(nhsS, spp[:, 48:56], 4.0, None, ALU.mult).then_inc(dve_small, 1)
                dve.wait_ge(act_small, 3)
                V.tensor_scalar(bS, bS, 0.5, 0.5, ALU.mult, ALU.add)
                V.scalar_tensor_tensor(m3(gS, 6), m3(spp[:, 0:48], 6), -1.0, albc.unsqueeze(1).to_broadcast([P, 6, 8]),
                                       ALU.mult, ALU.mult).then_inc(gates_ready, 1)

            ada_lo(0, 1)
            for u in range(U_OUT0 + 1):
                if u + 1 < U_OUT0:
                    split_lo((u + 1) % 4, u + 1)
                if u == 16:
                    dve.wait_ge(a_col, ADAN // 4)
                    V.tensor_tensor(ada[:, ADA1:], X[:, 2, 2 * ADA1:2 * ADAN].rearrange("p (k w) -> p k w", w=2),
                                    adab[:, ADA1:].unsqueeze(2).to_broadcast([P, ADAN - ADA1, 2]), ALU.add).then_inc(ada_ready, 1)
                    dve.wait_ge(ada_ready, 3)
                    cq = ada[:].rearrange("p (a k) w -> p a (k w)", a=12)
                    V.tensor_scalar(cq[:, 4:12:3], cq[:, 4:12:3], 1.0, None, ALU.add).then_inc(ada_ready, 1)
                    V.tensor_scalar(cq[:, 2:12:3], cq[:, 2:12:3], 1.0 / ALPHA, None, ALU.mult).then_inc(ada_ready, 1)
                    dve.wait_ge(ada_ready, 5)
                ada_lo(u, 3)
                ada_lo(u, 5)
                if u == 20:
                    softplus_in()
                    dve.wait_ge(sq_sum, 48)
                    V.tensor_scalar(ssS, ssS, EPS, None, ALU.add).then_inc(ss_ready, 1)
                if u == 21:
                    dve.wait_ge(rn_sqrt, 1)
                    link(V.reciprocal(rnS, rnS))
                    link(V.tensor_scalar(m3(rnS, 6)[:, :, 0:4], m3(rnS, 6)[:, :, 0:4], 128 ** -0.5, None, ALU.mult))
                if u == 22:
                    softplus()
                if u in (21, 23):
                    for t in (0, 1, 2) if u == 21 else (3, 4, 5):
                        V.tensor_tensor(qtok[:, t], qtok[:, t], bc_cols(m3(rnS, 6)[:, t, 0:4]), ALU.mult)
                        V.tensor_tensor(ktok[:, t], ktok[:, t], bc_cols(m3(rnS, 6)[:, t, 4:8]), ALU.mult).then_inc(qkn_ready, 1)
                if 1 <= u <= 12:
                    dve.wait_ge(tanh_done, u)
                    V.scalar_tensor_tensor(ybuf[:, (u - 1) % 2], tbuf[:, (u - 1) % 2], 1.0, ybuf[:, (u - 1) % 2],
                                           ALU.add, ALU.mult).then_inc(silu_done, 1)
                ada_lo(u, 7)
                ada_lo(u + 1, 1)
                if u < 16:
                    dve.wait_ge(evac_done, u + 1)
                    if 2 <= u < 12:
                        dve.wait_ge(tr_done, u - 1)
                    y = ybuf[:, u % 2] if u < 12 else xrT[:, u - 12]
                    for tap in range(4):
                        w = convw[:, tap * 12 + u:tap * 12 + u + 1] if u < 12 else prmB[:, tap * 4 + u - 12:tap * 4 + u - 11]
                        x = cbuf[:, u % 2, tap:tap + CW]
                        if tap == 0:
                            if u < 12:
                                ins = V.tensor_scalar(y, x, w, None, ALU.mult)
                            else:
                                ins = V.tensor_scalar(y, x, w, prmB[:, 16 + u - 12:17 + u - 12], ALU.mult, ALU.add)
                        else:
                            dve.wait_ge(conv_step, 4 * u + tap)
                            ins = V.scalar_tensor_tensor(y, x, w, y, ALU.mult, ALU.add)
                        ins.then_inc(conv_step, 1)
                elif u < 20:
                    dve.wait_ge(z_tanh, u - 15)
                    V.scalar_tensor_tensor(zT[:, u % 4], tbuf[:, u % 2, 0:TOK], 1.0, zT[:, u % 4], ALU.add, ALU.mult).then_inc(z_done, 1)
                elif u < 24:
                    tb = tbuf[:, u % 2, 0:TOK]
                    dve.wait_ge(g_sq, u - 19)
                    V.tensor_scalar(tb, tb, 8 * GELU1, 2 * GELU0, ALU.mult, ALU.add).then_inc(g_in, 1)
                    dve.wait_ge(g_in, 2 * (u - 20) + 1)
                    V.tensor_tensor(tb, tb, gT[:, u % 4], ALU.mult).then_inc(g_in, 1)
                    dve.wait_ge(g_tanh, u - 19)
                    V.scalar_tensor_tensor(gT[:, u % 4], tb, 1.0, gT[:, u % 4], ALU.add, ALU.mult).then_inc(g_done, 1)

            dve.wait_ge(cum_mm, 1)
            V.tensor_scalar(gamS, X[:, 2, 0:48], 1.0, None, ALU.mult).then_inc(dve_small, 1)
            dve.wait_ge(cum_mm, 2)
            dve.wait_ge(dve_small, 3)
            link(V.tensor_tensor(glS, X[:, 2, 64:112], gamS, ALU.subtract))
            V.tensor_scalar(glS, glS, 0.0, None, ALU.min).then_inc(dve_small, 1)
            dve.wait_ge(act_small, 6)
            link(V.tensor_tensor(bES, bES, bS, ALU.mult))

            for d in range(2):
                for c in range(4):
                    n = 4 * d + c
                    dve.wait_ge(lru_at, n + 1)
                    for s, e, off in ((0, CTX, 0), (CTX, TOK, GAP)):
                        V.scalar_tensor_tensor(lx[:, c, s:e], tii[n % 2][:, s:e], 1.0, xrT[:, c, s + off:e + off], ALU.add, ALU.mult)
                    link(V.tensor_tensor(aa2[n % 2][:], la[:, c], la[:, c], ALU.mult))
                    V.scalar_tensor_tensor(lw[:, c], aa2[n % 2][:], 1.0, thh[n % 2][:], ALU.add, ALU.mult).then_inc(lru_w, 1)
                dve.wait_ge(lru_sqrt, d + 1)
                for c in range(4):
                    link(V.tensor_tensor(lx[:, c], lx[:, c], lw[:, c], ALU.mult))
                    if d == 0:
                        link(V.tensor_tensor_scan(yl[:, c, 0:CTX], la[:, c, 0:CTX], lx[:, c, 0:CTX], 0.0, ALU.mult, ALU.add))
                        V.tensor_tensor_scan(yl[:, c, CTX:TOK], la[:, c, CTX:TOK], lx[:, c, CTX:TOK],
                                             yl[:, c, CTX - 1:CTX], ALU.mult, ALU.add).then_inc(lru_y, 1)
                    else:
                        rev = slice(CTX - 1, None, -1)
                        rl = slice(TOK - 1, CTX - 1, -1)
                        link(V.tensor_tensor_scan(lw[:, c, rev], la[:, c, rev], lx[:, c, rev], 0.0, ALU.mult, ALU.add))
                        ins = V.tensor_tensor_scan(lw[:, c, rl], la[:, c, rl], lx[:, c, rl], lw[:, c, 0:1], ALU.mult, ALU.add)
                        if c < 2:
                            ins.then_inc(lru_scan, 1)
                            continue
                        link(ins)
                        link(V.tensor_tensor(yl[:, c], yl[:, c], lw[:, c], ALU.add))
                        V.tensor_tensor(gT[:, c], gT[:, c], yl[:, c], ALU.mult).then_inc(lru_y, 1)

            def v4(ap):
                return ap.rearrange("p (r c) -> p r c", r=4)

            def chain_dve(p, s):
                c = 2 * p + s
                dve.wait_ge(ch_v, 2 * c + 2)
                dve.wait_ge(state_zero, 3)
                if c >= 2:
                    dve.wait_ge(ch_o, c - 1)
                h = 64 * half_of(1, s)
                V.tensor_scalar(vn[s][h:h + 64, 4:8], v4(X[h:h + 64, 0, :]), 1.0, None, ALU.mult).then_inc(ch_vnb, 1)
                for r in range(8):
                    if r % 4 == 0:
                        dve.wait_ge(ch_s, 2 * c + r // 4 + 1)
                    V.scalar_tensor_tensor(S[:, r], S[:, r], cdS[:, 48 * s + 8 * p + r:48 * s + 8 * p + r + 1],
                                           X[:, 1 + r // 4, (r % 4) * P:(r % 4 + 1) * P], ALU.mult, ALU.add).then_inc(ch_state, 1)
                dve.wait_ge(ch_o, c + 1)
                first = (c < 3 - c) if c < 4 else (c < 15 - c)
                for d in range(2):
                    h = 64 * half_of(d, s)
                    src = v4(X[h:h + 64, 3, :])
                    dst = otk[h:h + 64, tile_of(d, p)]
                    if first:
                        last = V.tensor_scalar(dst, src, 1.0, None, ALU.mult)
                    else:
                        last = V.tensor_tensor(dst, src, dst, ALU.add)
                last.then_inc(ch_out, 1)
                if c in (1, 7):
                    dve.wait_ge(ch_out, c + 1)

            dve.wait_ge(z_done, 4)
            for h in range(HEADS):
                V.tensor_scalar(zT[:, h], zT[:, h], prmB[:, 44:45], None, ALU.mult).then_inc(o_z, 1)
            dve.wait_ge(gc_in, 16)
            for p in range(7):
                if p < 6:
                    for d in range(2):
                        n = 2 * p + d
                        r = slice(4 * d, 4 * d + 4)
                        dve.wait_ge(gd_exp, n + 1)
                        if p >= 1:
                            dve.wait_ge(gd_qk_ready, n - 1)
                        link(V.tensor_tensor(dm[d][:], v4(G[:, 2 * d, :]), bc_cols(m3(gamS, 6)[:, p, r]), ALU.subtract))
                        V.tensor_scalar(dm[d][:], dm[d][:], 0.0, None, ALU.min).then_inc(gd_diff, 1)
                    for d in range(2):
                        n = 2 * p + d
                        dve.wait_ge(gd_dec, n + 1)
                        link(V.tensor_tensor(dm[d][:], dm[d][:], bc_mask(gc[:, CG_INCL + d]), ALU.mult))
                        dve.wait_ge(gd_g, n + 1)
                        if p >= 1:
                            dve.wait_ge(lv_ot, 2 * LEVELS * p)
                        V.tensor_tensor(att[d][:], v4(G[:, 2 * d + 1, :]), dm[d][:], ALU.mult).then_inc(gd_at0, 1)
                        dve.wait_ge(gd_brow, n + 1)
                        dve.wait_ge(gd_at0, n + 1)
                        V.tensor_tensor(att[d][:], att[d][:], v4(G[:, 2 * d, :]), ALU.mult).then_inc(gd_at, 1)
                    for d in range(2):
                        n = 2 * p + d
                        dve.wait_ge(gd_qk, n + 1)
                        if p >= 2:
                            dve.wait_ge(ch_o, 2 * (p - 1))
                        V.tensor_tensor(qk[d][p % 2][:], v4(G[:, 2 * d + 1, :]), dm[d][:], ALU.mult).then_inc(gd_qk_ready, 1)
                for lev in range(LEVELS):
                    if p < 6:
                        for d in range(2):
                            if lev == 0:
                                dve.wait_ge(lv_p, 2 * LEVELS * p + d + 1)
                                V.tensor_tensor(xx[d][:], bc_mask(ident[:]), v4(G[:, 2 * d, :]), ALU.subtract).then_inc(lv_x, 1)
                                dve.wait_ge(lv_ot, 2 * LEVELS * p + d + 1)
                                V.tensor_tensor(xt[d][:], bc_mask(ident[:]), ot[d][0][:], ALU.subtract).then_inc(lv_xt, 1)
                                continue
                            dve.wait_ge(lv_et, 2 * (5 * p + lev - 1) + d + 1)
                            dve.wait_ge(lv_xt, 2 * (LEVELS * p + lev - 1) + d + 1)
                            if lev == 5 and p >= 1:
                                dve.wait_ge(ch_o, 2 * p)
                            dst = tt[d] if lev == 5 else xt[d]
                            V.tensor_tensor(dst[:], xt[d][:], v4(G[:, 2 * d, :]), ALU.subtract).then_inc(lv_xt, 1)
                    if p >= 1 and lev in CHAIN_AT:
                        chain_dve(p - 1, CHAIN_AT.index(lev))

            dve.wait_ge(o_std, 1)
            V.reciprocal(orn[:], orn[:]).then_inc(o_rcp, 1)
            dve.wait_ge(o_rcp, 1)
            for t in range(NT):
                V.tensor_tensor(otk[:, t], otk[:, t], bc_cols(orn[:, t * HEADS:(t + 1) * HEADS]), ALU.mult).then_inc(o_n, 1)
            for h in range(HEADS):
                dve.wait_ge(o_tr, h + 1)
                dve.wait_ge(o_z, h + 1)
                B, b = NORM_BANKS[h]
                for s, e, bank in PIECES:
                    last = V.tensor_tensor(oT[:, h, s:e], zT[:, h, s:e], B[:, b + bank, 0:e - s], ALU.mult)
                last.then_inc(o_y, 1)
            for k in range(4):
                dve.wait_ge(uhi_ready, 12 + k + 1)
                V.tensor_tensor(ulo[:, k], oT[:, k], uhi[:, k].bitcast(F32), ALU.subtract).then_inc(ulo_ready, 2)

            def residual(unit, par, f, layer, qg, span, rbase):
                dve.wait_ge(mm_done, unit + 1)
                for s, e, bank in PIECES:
                    if s >= span[0]:
                        who = ADA_CTX if bank == 0 else ADA_LAT
                        last = V.scalar_tensor_tensor(hT[:, f, s:e], G[:, 2 * (par % 2) + bank, 0:e - s],
                                                      adacol(layer, qg, f, who), hT[:, f, s:e], ALU.mult, ALU.add)
                last.then_inc(res_done, 1)

            def layer_norm(c, span, rbase, ubase=None):
                a, b = span
                for k in range(KD):
                    if k == 0:
                        dve.wait_ge(ln_mean, c + 1)
                        dve.wait_ge(res_done, rbase + 8)
                    for s, e, bank in PIECES:
                        if s >= a:
                            last = V.tensor_tensor(hT[:, k, s:e], hT[:, k, s:e], X[:, bank, 0:e - s], ALU.subtract)
                    last.then_inc(ln_xc, 1)
                dve.wait_ge(ln_col, c + 1)
                V.reciprocal(lst[:, a // P:NT], X[:, 2, a // P:NT]).then_inc(ln_rstd, 1)
                dve.wait_ge(ln_row, c + 1)
                for k in range(KD + 2):
                    if k < KD:
                        for s, e, bank in PIECES:
                            if s >= a:
                                last = V.tensor_tensor(hT[:, k, s:e], hT[:, k, s:e], X[:, bank, 0:e - s], ALU.mult)
                        last.then_inc(ln_xn, 1)
                    if ubase is not None and k >= 2:
                        low_u(ubase, k - 2, span)

            def mlp(layer, q, span, u0, h0, rbase, last_quarter):
                base = u0 + 16 * q
                a, b = span
                def split(j):
                    dve.wait_ge(w_hi, base + (j + 1))
                    V.tensor_tensor(wlo[:, j % 2], raw[:, (j // 2) % 2, :, (j % 2) * P:(j % 2 + 1) * P],
                                    whi[:, j % 2].bitcast(F32), ALU.subtract).then_inc(w_lo, 1)
                def low_h(j):
                    dve.wait_ge(h1hi_done, h0 + 8 * q + (j + 1))
                    V.tensor_tensor(h1lo[:, j, a:b], hh[:, j % 2, a:b], h1hi[:, j, a:b].bitcast(F32),
                                    ALU.subtract).then_inc(h1lo_done, 1)
                for j in range(8):
                    split(j + 1)
                    dve.wait_ge(relu_done, h0 + 8 * q + (j + 1))
                    dve.wait_ge(h1lo_done, h0 + 8 * q + (j + 1))
                    V.tensor_tensor(hh[:, j % 2, a:b], rt[:, j % 2, a:b], rt[:, j % 2, a:b], ALU.mult).then_inc(hh_done, 1)
                    if j >= 1:
                        low_h(j - 1)
                low_h(7)
                for f in range(8):
                    if not (last_quarter and f == 7):
                        split(8 + f + 1)
                    dve.wait_ge(mm_done, base + (8 + f + 1))
                    dve.wait_ge(res_done, rbase + 8 * q + f)
                    for s, e, bank in PIECES:
                        if s >= a:
                            who = ADA_CTX if bank == 0 else ADA_LAT
                            last = V.scalar_tensor_tensor(hT[:, f, s:e], G[:, 2 * (f % 2) + bank, 0:e - s],
                                                          adacol(layer, 5, f, who), hT[:, f, s:e], ALU.mult, ALU.add)
                    last.then_inc(res_done, 1)

            split_lo(0, U_OUT0)
            for j in range(8):
                split_lo((j + 1) % 4, U_OUT0 + j + 1)
                residual(U_OUT0 + j, j, j, 0, 2, (0, TOK), R_OUT0)
            layer_norm(0, (0, TOK), R_OUT0, 16)
            with dve.Fori(0, 4) as q:
                mlp(0, q, (0, TOK), U_MLP0, 0, R_MLP0, False)
            layer_norm(1, (0, TOK), R_MLP0 + 24, 24)

            dve.wait_ge(lam_in, 16)
            lv = lrow[:].rearrange("p (r d) -> p r d", r=4)
            link(V.tensor_tensor(rt1[:, 0:128].rearrange("p (a d) -> p a d", a=2), lv[:, 0:4:2], lv[:, 1:4:2], ALU.mult))
            V.tensor_reduce(nlam[:, 0:2], rt1[:, 0:128].rearrange("p (a d) -> p a d", a=2), AX.X, ALU.add).then_inc(lam_ready, 1)
            dve.wait_ge(rope_in, 16)
            dve.wait_ge(lam_ready, 1)
            for u in range(U_QKV, U_OUT1 + 1):
                j = u - U_QKV
                split_lo((u + 1) % 4, u + 1) if u < U_OUT1 else None
                jj = j - 1
                if 0 <= jj < 8 or 16 <= jj < 24:
                    i = jj if jj < 8 else jj - 8
                    dst = k1[:, jj, CTX:TOK] if jj < 8 else q1[:, jj - 16]
                    dve.wait_ge(evac_done, E_QKV + jj + 1)
                    if i >= 1:
                        dve.wait_ge(kq_ready, i)
                    V.tensor_tensor(rt1[:], kb[:, jj % 2, CTX:TOK], rc[:, P:P + LAT], ALU.mult).then_inc(rope_step, 1)
                    dve.wait_ge(rot_mm, i + 1)
                    V.tensor_tensor(rt2[:], X[:, i % 2, :], rc[:, P + LAT:P + 2 * LAT], ALU.mult).then_inc(rope_step, 1)
                    dve.wait_ge(rope_step, 2 * i + 2)
                    V.tensor_tensor(dst, rt1[:], rt2[:], ALU.add).then_inc(kq_ready, 1)

            dve.wait_ge(lam_ready, 2)
            link(V.tensor_tensor(nlam[:, 4:5], nlam[:, 3:4], nlam[:, 2:3], ALU.subtract))
            link(V.tensor_scalar(nlam[:, 4:5], nlam[:, 4:5], -LAM_INIT, None, ALU.add))
            for it in range(35):
                def maximum(m):
                    dve.wait_ge(sc_mm, 2 * it + m + 1)
                    if it >= 2:
                        dve.wait_ge(ex_ready, 2 * (it - 2) + m + 1)
                    V.tensor_reduce(nmx[:, it % 2, m:m + 1], Gf[:, 1024 * m:1024 * m + TOK], AX.X, ALU.max,
                                    negate=True).then_inc(mx_ready, 1)
                if it < 32:
                    maximum(0)
                if 1 <= it <= 32:
                    i = it - 1
                    dve.wait_ge(ex_ready, 2 * i + 2)
                    link(V.reciprocal(rrc[:, i % 2], rsm[:, i % 2]))
                    link(V.tensor_tensor(rrc[:, i % 2, 1:2], rrc[:, i % 2, 1:2], nlam[:, 4:5], ALU.mult))
                    if i >= 2:
                        dve.wait_ge(pt_mm, i - 1)
                    link(V.tensor_scalar(pc[:, i % 2], pp[:, i % 2, 0], rrc[:, i % 2, 0:1], None, ALU.mult))
                    V.scalar_tensor_tensor(pc[:, i % 2], pp[:, i % 2, 1], rrc[:, i % 2, 1:2], pc[:, i % 2],
                                           ALU.mult, ALU.add).then_inc(pc_ready, 1)
                if it < 32:
                    maximum(1)
                if it >= 3:
                    i = it - 3
                    h, qt = i // 4, i % 4
                    dve.wait_ge(pv_mm, i + 1)
                    V.tensor_scalar(oo[:, qt, h * P:(h + 1) * P], X[:, 2 + i % 2, 0:P], 1.0, None, ALU.mult).then_inc(o_ready, 1)
            dve.wait_ge(osq1, 32)
            V.tensor_scalar(ors[:, 0], ors[:, 0], 1.0 / P, EPS, ALU.mult, ALU.add).then_inc(oss1, 1)
            dve.wait_ge(act_small, 7)
            link(V.reciprocal(ors[:, 1], ors[:, 1]))
            for qt in range(4):
                v = oo[:, qt].rearrange("p (h c) -> p h c", h=8)
                V.tensor_tensor(v, v, ors[:, 1, 8 * qt:8 * qt + 8].unsqueeze(2).to_broadcast([P, 8, P]), ALU.mult).then_inc(on_ready, 1)
            for k in range(KD):
                dve.wait_ge(uhi_ready, 32 + k + 1)
                V.tensor_tensor(ulo[:, k, CTX:TOK], y1[:, k], uhi[:, k, CTX:TOK].bitcast(F32), ALU.subtract).then_inc(ulo_ready, 1)
            for j in range(8):
                split_lo((j + 1) % 4, U_OUT1 + j + 1)
                residual(U_OUT1 + j, j, j, 1, 2, (CTX, TOK), R_OUT1)
            layer_norm(2, (CTX, TOK), R_OUT1, 40)
            with dve.Fori(0, 3) as q:
                mlp(1, q, (CTX, TOK), U_MLP1, 32, R_MLP1, False)
            mlp(1, 3, (CTX, TOK), U_MLP1, 32, R_MLP1, True)
            layer_norm(3, (CTX, TOK), R_MLP1 + 24)
            for w in range(2):
                for t in (1, 3):
                    dve.wait_ge(fin_mm, 4 * w + t + 1)
                    B, b = FIN_BANKS[w][t]
                    V.tensor_scalar(otok[:, t, 512 * w:512 * w + 512], B[:, b, :], 1.0, None, ALU.mult).then_inc(fin_dve, 1)

        @block.tensor
        def _(pe):
            mm = nc.tensor.matmul
            tr = nc.tensor.transpose

            def ada_cols(g):
                pe.wait_ge(a_row, g + 1)
                for w in range(4):
                    o = 8 * g + 2 * w
                    last = mm(X[:, 2, o:o + 2], grow[:, g % 2, w * P:(w + 1) * P], sel[:], start=True, stop=True)
                last.then_inc(a_col, 1)

            def ada_tile(i):
                if i % 4 == 0 and i not in (0, ADA1):
                    ada_cols(i // 4 - 1)
                wait_a_lo(pe, i)
                o = P * (i % 4)
                for k in range(KD):
                    hi = lambda: mm(X[0:4, 3, o:o + P], csp[:, k, 0:4], ahi[:, i % 3, k], start=(k == 0),
                                    stop=(k == KD - 1), skip_group_check=True)
                    lo = lambda: mm(X[0:2, 3, o:o + P], csp[:, k, 0:2], alo[:, i % 3, k], start=False, stop=False,
                                    skip_group_check=True)
                    for product in ((hi, lo) if k == 0 else (lo, hi)):
                        last = product()
                last.then_inc(a_mm, 1)

            def gemm(par, w_ready, src_hi, src_lo, span, k_waits=None, between=(), order=range(KD)):
                pe.wait_ge(w_lo, w_ready)
                pieces = [x for x in PIECES if x[0] >= span[0]]
                for k in order:
                    if callable(k_waits):
                        k_waits(k)
                    elif k_waits is not None:
                        pe.wait_ge(k_waits[0], k_waits[1] + k)
                    for w, x, first, final in ((whi, src_hi, True, False), (whi, src_lo, False, False), (wlo, src_hi, False, True)):
                        for s, e, bank in pieces:
                            last = mm(G[:, 2 * (par % 2) + bank, 0:e - s], w[:, par % 2, k], x[:, k, s:e],
                                      start=(k == order[0] and first), stop=(k == order[-1] and final))
                    if between:
                        ada_tile(between[k])
                last.then_inc(mm_done, 1)

            pe.wait_ge(const_in, 48)
            pe.wait_ge(ones_ready, 4)
            pe.wait_ge(x_in, 32)
            for k in range(KD):
                if k >= 2:
                    pe.wait_ge(h0_ready, k - 1)
                for t in range(NT):
                    bank, col = (0, t * P) if t < 2 else (1, (t - 2) * P)
                    last = tr(G[:, 2 * (k % 2) + bank, col:col + P], xtok[:, t, k * P:(k + 1) * P], ident[:])
                last.then_inc(tr_x, 1)
            pe.wait_ge(rows_in, 160)
            tr(X[:, 2, 256:368], rowsA[0:112], ident[0:112, 0:112]).then_inc(rows_mm, 1)
            tr(X[:, 2, 368:414], rowsB[0:46], ident[0:46, 0:46]).then_inc(rows_mm, 1)
            tr(X[:, 2, 414:510], rowsC[0:96], ident[0:96, 0:96]).then_inc(rows_mm, 1)
            pe.wait_ge(prm_ready, 1)
            pe.wait_ge(csp_lo, 1)
            for i in range(ADA1):
                ada_tile(i)
            ada_cols(ADA1 // 4 - 1)

            def gates_rows():
                pe.wait_ge(wab_lo, 1)
                for k in range(KD):
                    for w, x, a, b in ((wabhi, uhi, True, False), (wabhi, ulo, False, False), (wablo, uhi, False, True)):
                        for s, e, bank in PIECES:
                            last = mm(X[0:16, bank, 0:e - s], w[:, k], x[:, k, s:e], start=(k == 0 and a),
                                      stop=(k == KD - 1 and b))
                last.then_inc(ab_mm, 1)

            def gates_tokens():
                pe.wait_ge(ab_rows, 1)
                pe.wait_ge(ada_ready, 3)
                for t in range(NT):
                    last = tr(X[:, 2, 16 * t:16 * t + 16], abT[:, t * P:(t + 1) * P], ident[0:16, 0:16])
                last.then_inc(ab_mm, 1)

            pe.wait_ge(ada_ready, 2)
            for u in range(U_OUT0):
                if u >= 2:
                    pe.wait_ge(evac_done, u - 1)
                gemm(u, u + 1, uhi, ulo, (0, TOK), (ulo_ready, 1) if u == 0 else None,
                     ada_tiles(u))
                if u == A_UNITS:
                    ada_cols(ADAN // 4 - 1)
                if u == 17:
                    gates_rows()
                if u == 18:
                    gates_tokens()
                if 2 <= u <= 13:
                    pe.wait_ge(silu_done, u - 1)
                    if u >= 3:
                        pe.wait_ge(tok_done, u - 2)
                    for t in range(NT):
                        o = t * P if t < 2 else LO + (t - 2) * P
                        last = tr(Xf[:, t * P:(t + 1) * P], ybuf[:, (u - 2) % 2, o:o + P], ident[:])
                    last.then_inc(tr_done, 1)
            pe.wait_ge(gc_in, 16)
            pe.wait_ge(gates_ready, 1)
            pe.wait_ge(ab_ready, 1)
            g3 = m3(gS, 6)
            cum = X[:, 2, 0:48].rearrange("p (t r) -> p t r", t=6)
            for d in range(2):
                last = mm(cum[:, :, 4 * d:4 * d + 4], gc[:, CG_CUM + d], g3[:, :, 4 * d:4 * d + 4], start=True, stop=True)
            last.then_inc(cum_mm, 1)
            pe.wait_ge(dve_small, 3)
            gm = m3(gamS, 6)
            tot = X[:, 2, 64:112].rearrange("p (t r) -> p t r", t=6)
            dec = X[:, 2, 128:224].rearrange("p (s t r) -> p s t r", s=2, t=6)
            for d in range(2):
                mm(tot[:, :, 4 * d:4 * d + 4], gc[:, CG_LAST + d], gm[:, :, 4 * d:4 * d + 4], start=True, stop=True)
            for s in range(2):
                for d in range(2):
                    row = CG_ROW + 2 * s + d
                    last = mm(dec[:, s, :, 4 * d:4 * d + 4], gc[:, row], gm[:, :, 4 * d:4 * d + 4], start=True, stop=True)
            last.then_inc(cum_mm, 1)

            pe.wait_ge(gw_in, 128)
            pe.wait_ge(evac_done, 24)
            for d in range(2):
                for c in range(4):
                    n = 4 * d + c
                    if n == 1:
                        pe.wait_ge(act_small, 6)
                    if n >= 2:
                        pe.wait_ge(gate_tanh, n - 1)
                    B = X if n % 2 else G
                    for g in range(2):
                        for s, e, bank in PIECES:
                            off = GAP * bank
                            last = mm(B[:, 2 * g + bank, 0:e - s], gw[:, (2 * d + g) * 4 + c], xrT[:, c, s + off:e + off],
                                      start=True, stop=True)
                    last.then_inc(gates_mm, 1)

            pe.wait_ge(gate_tanh, 8)
            for t in range(NT):
                pe.wait_ge(qkn_ready, t + 1)
                for w, src in ((0, qtok), (1, ktok)):
                    if t >= 1:
                        pe.wait_ge(qkT_ready, 2 * t + w - 1)
                    for h in range(HEADS):
                        last = tr(X[:, w, h * P:(h + 1) * P], src[:, t, h], ident[:])
                    last.then_inc(qkT_mm, 1)

            def four(bank, lhs, rhs, sem):
                for r in range(4):
                    last = mm(G[:, bank, r * P:(r + 1) * P], lhs(r), rhs(r), start=True, stop=True)
                last.then_inc(sem, 1)

            def row_of(small_array, p, d, sem):
                four(2 * d, lambda r: m3(small_array, 6)[:, p, 4 * d + r:4 * d + r + 1].to_broadcast([P, P]),
                     lambda r: ident[:], sem)

            def chain_pe(p, s):
                c = 2 * p + s
                pe.wait_ge(wt_ready, 2 * p + 2)
                pe.wait_ge(bv_ready, 2 * p + 2)
                pe.wait_ge(lv_xt, 2 * LEVELS * (p + 1))
                pe.wait_ge(state_zero, 3)
                if c >= 1:
                    pe.wait_ge(ch_vnf, c)
                    pe.wait_ge(ch_vnb, c)
                for d in range(2):
                    h = 64 * half_of(d, s)
                    for r in range(4):
                        mm(X[h:h + 64, 0, r * P:(r + 1) * P], tt[d][:, r, h:h + 64], bv[d][:, r], start=(r == 0), stop=False,
                           skip_group_check=True)
                for d in range(2):
                    h = 64 * half_of(d, s)
                    if c >= 1:
                        pe.wait_ge(ch_state, 8 * (c - 1) + 4 * d + 4)
                    for r in range(4):
                        last = mm(X[h:h + 64, 0, r * P:(r + 1) * P], wt[d][:, r, h:h + 64], S[:, 4 * d + r], start=False,
                                  stop=(r == 3), skip_group_check=True)
                    last.then_inc(ch_v, 1)
                pe.wait_ge(gd_qd, 2 * p + 2)
                if c >= 1:
                    pe.wait_ge(ch_out, c)
                for d in range(2):
                    h = 64 * half_of(d, s)
                    for r in range(4):
                        mm(X[h:h + 64, 3, r * P:(r + 1) * P], qd[d][p % 2][:, r, h:h + 64], S[:, 4 * d + r], start=(r == 0),
                           stop=False, skip_group_check=True)
                pe.wait_ge(kd_ready, 2 * p + 2)
                for d in range(2):
                    pe.wait_ge((ch_vnf, ch_vnb)[d], c + 1)
                    for r in range(4):
                        last = mm(X[:, 1 + d, r * P:(r + 1) * P], kd[d][:, r], vn[s][:, 4 * d + r], start=True, stop=True)
                    last.then_inc(ch_s, 1)
                for d in range(2):
                    h = 64 * half_of(d, s)
                    for r in range(4):
                        last = mm(X[h:h + 64, 3, r * P:(r + 1) * P], qk[d][p % 2][:, r, h:h + 64], vn[s][:, 4 * d + r],
                                  start=False, stop=(r == 3), skip_group_check=True)
                last.then_inc(ch_o, 1)

            for p in range(7):
                if p < 6:
                    for d in range(2):
                        if p == 0:
                            pe.wait_ge(gate_tanh, 8)
                        else:
                            pe.wait_ge(lv_xt, 2 * (LEVELS * p - 1) + d + 1)
                        row_of(gamS, p, d, gd_row)
                    if p == 0:
                        pe.wait_ge(qkT_ready, 12)
                    for d in range(2):
                        t = tile_of(d, p)
                        ts = slice(t * P, (t + 1) * P)
                        if p >= 1:
                            pe.wait_ge(wt_ready, 2 * (p - 1) + d + 1)
                        four(2 * d + 1, lambda r: kT[:, r, ts], lambda r: kT[:, r, ts], gd_g)
                    for d in range(2):
                        pe.wait_ge(gd_diff, 2 * p + d + 1)
                        row_of(bS, p, d, gd_brow)
                    for d in range(2):
                        t = tile_of(d, p)
                        ts = slice(t * P, (t + 1) * P)
                        pe.wait_ge(gd_at, 2 * p + d + 1)
                        four(2 * d + 1, lambda r: kT[:, r, ts], lambda r: qT[:, r, ts], gd_qk)
                for lev in range(LEVELS):
                    if p < 6:
                        for d in range(2):
                            pe.wait_ge(lv_ot, 2 * (LEVELS * p + lev) + d + 1)
                            if lev == 0:
                                pe.wait_ge(gd_at, 2 * p + d + 1)
                                for r in range(4):
                                    last = tr(G[:, 2 * d, r * P:(r + 1) * P], ot[d][0][:, r], ident[:])
                                last.then_inc(lv_p, 1)
                            else:
                                if lev == 1:
                                    pe.wait_ge(lv_x, 2 * p + d + 1)
                                else:
                                    pe.wait_ge(lv_xc, 2 * (4 * p + lev - 2) + d + 1)
                                pe.wait_ge(lv_xt, 2 * (LEVELS * p + lev - 1) + d + 1)
                                four(2 * d, lambda r: ot[d][lev % 2][:, r], lambda r: xx[d][:, r], lv_p)
                        if lev > 0:
                            for d in range(2):
                                pe.wait_ge(lv_pm, 2 * (5 * p + lev - 1) + d + 1)
                                four(2 * d, lambda r: pm[d][:, r], lambda r: xt[d][:, r], lv_et)
                            for d in range(2):
                                if lev < 5:
                                    if lev == 1:
                                        pe.wait_ge(gd_qk_ready, 2 * p + d + 1)
                                    pe.wait_ge(lv_xt, 2 * (LEVELS * p + lev) + d + 1)
                                    for r in range(4):
                                        last = tr(G[:, 2 * d + 1, r * P:(r + 1) * P], xt[d][:, r], ident[:])
                                    last.then_inc(lv_e, 1)
                    if p >= 1 and lev in CHAIN_AT:
                        chain_pe(p - 1, CHAIN_AT.index(lev))
                if p < 6:
                    for d in range(2):
                        pe.wait_ge(bk_ready, 2 * p + d + 1)
                        pe.wait_ge(lv_xt, 2 * (LEVELS * p + 5) + d + 1)
                        four(2 * d + 1, lambda r: dg[d][:, r], lambda r: tt[d][:, r], wt_mm)

            pe.wait_ge(o_n, NT)
            for h in range(HEADS):
                if h == 3:
                    pe.wait_ge(o_y, 1)
                B, b = NORM_BANKS[h]
                for t in range(NT):
                    bank, col = (0, t * P) if t < 2 else (1, (t - 2) * P)
                    last = tr(B[:, b + bank, col:col + P], otk[:, t, h], ident[:])
                last.then_inc(o_tr, 1)

            def mixer_waits(k):
                if k >= 4:
                    pe.wait_ge(glo_ready, k - 3)
                else:
                    pe.wait_ge(ulo_ready, 8 + 2 * (k + 1))
            for j in range(8):
                if j >= 2:
                    pe.wait_ge(res_done, R_OUT0 + j - 1)
                elif j == 1:
                    pe.wait_ge(o_y, 3)
                gemm(j, U_OUT0 + j + 1, uhi, ulo, (0, TOK), mixer_waits if j == 0 else None, order=(4, 5, 6, 7, 0, 1, 2, 3))

            def layer_norm(c, span, rbase):
                pieces = [x for x in PIECES if x[0] >= span[0]]
                pe.wait_ge(acc_step, 6 * c + 6)
                for s, e, bank in pieces:
                    mm(X[:, bank, 0:e - s], onesD[:], acc[:, s:e], start=True, stop=False)
                pe.wait_ge(res_done, rbase + KD)
                for s, e, bank in pieces:
                    last = mm(X[:, bank, 0:e - s], onesD[:], hT[:, KD - 1, s:e], start=False, stop=True)
                last.then_inc(ln_mean, 1)
                for k in range(KD):
                    pe.wait_ge(ln_sq, 8 * c + k + 1)
                    for s, e, bank in pieces:
                        last = mm(X[:, 2 + bank, 0:e - s], onesD[:], lsq[:, k % 2, s:e], start=(k == 0), stop=(k == KD - 1))
                    last.then_inc(ln_var, 1)
                pe.wait_ge(ln_std, c + 1)
                for t in range(span[0] // P, NT):
                    last = tr(X[:, 2, t:t + 1], lstd[:, t * P:(t + 1) * P], ident[0:1, 0:1])
                last.then_inc(ln_col, 1)
                pe.wait_ge(ln_rstd, c + 1)
                for t in range(span[0] // P, NT):
                    bank, col = (0, t * P) if t < 2 else (1, (t - 2) * P)
                    last = mm(X[:, bank, col:col + P], lst[:, t:t + 1].to_broadcast([P, P]), ident[:], start=True, stop=True)
                last.then_inc(ln_row, 1)

            def mlp(q, span, u0, h0, rbase, ubase):
                base = u0 + 16 * q
                for j in range(8):
                    if j >= 2:
                        pe.wait_ge(relu_done, h0 + 8 * q + (j - 1))
                    else:
                        pe.wait_ge(res_done, rbase + 8 * q + (j - 1))
                    gemm(j, base + (j + 1), uhi, ulo, span, (ulo_ready, ubase + 1) if j == 0 else None)
                for f in range(8):
                    if f >= 2:
                        pe.wait_ge(res_done, rbase + 8 * q + (f - 1))
                    else:
                        pe.wait_ge(relu_done, h0 + 8 * q + (7 + f))
                    gemm(f, base + (8 + f + 1), h1hi, h1lo, span, (h1lo_done, h0 + 8 * q + 3) if f == 0 else None)

            layer_norm(0, (0, TOK), R_OUT0)
            with pe.Fori(0, 4) as q:
                mlp(q, (0, TOK), U_MLP0, 0, R_MLP0, 16)
            layer_norm(1, (0, TOK), R_MLP0 + 24)

            for u in range(U_QKV, U_OUT1 + 1):
                j = u - U_QKV
                if j < 24:
                    if j < 2:
                        pe.wait_ge(res_done, R_OUT1 + j - 1)
                    else:
                        pe.wait_ge(evac_done, E_QKV + j - 1)
                    gemm(u, u + 1, uhi, ulo, (0, TOK) if j < 16 else (CTX, TOK), (ulo_ready, 24 + 1) if j == 0 else None)
                jj = j - 1
                if 0 <= jj < 8 or 16 <= jj < 24:
                    i = jj if jj < 8 else jj - 8
                    pe.wait_ge(evac_done, E_QKV + jj + 1)
                    pe.wait_ge(rope_in, 16)
                    if i >= 2:
                        pe.wait_ge(kq_ready, i - 1)
                    mm(X[:, i % 2, :], rc[:, 0:P], kb[:, jj % 2, CTX:TOK], start=True, stop=True).then_inc(rot_mm, 1)
                elif 8 <= jj < 16:
                    pe.wait_ge(evac_done, E_QKV + jj + 1)
                    if jj >= 9:
                        pe.wait_ge(v_ready, jj - 8)
                    for t in range(NT):
                        last = tr(Xf[:, 1024 + t * P:1024 + (t + 1) * P], kb[:, jj % 2, t * P:(t + 1) * P], ident[:])
                    last.then_inc(vtr_mm, 1)

            pe.wait_ge(v_ready, 8)
            pe.wait_ge(kq_ready, 16)
            for it in range(35):
                if it < 32:
                    h, qt = it // 4, it % 4
                    for m in range(2):
                        if it >= 1:
                            pe.wait_ge(ex_ready, 2 * (it - 1) + m + 1)
                        r = slice(64 * m, 64 * m + 64)
                        for a, b in ((0, 512), (512, TOK)):
                            last = mm(Gf[:, 1024 * m + a:1024 * m + b], q1[r, h, qt * P:(qt + 1) * P], k1[r, h, a:b],
                                      start=True, stop=True)
                        last.then_inc(sc_mm, 1)
                if 2 <= it <= 33:
                    i = it - 2
                    pe.wait_ge(pc_ready, i + 1)
                    if i >= 1:
                        pe.wait_ge(pt_ready, i)
                    for t in range(NT):
                        last = tr(Xf[:, t * P:(t + 1) * P], pc[:, i % 2, t * P:(t + 1) * P], ident[:])
                    last.then_inc(pt_mm, 1)
                if it >= 3:
                    i = it - 3
                    h = i // 4
                    pe.wait_ge(pt_ready, i + 1)
                    if i >= 2:
                        pe.wait_ge(o_ready, i - 1)
                    for t in range(NT):
                        last = mm(X[:, 2 + i % 2, 0:P], pT[:, i % 2, t * P:(t + 1) * P], v1[:, t, h * P:(h + 1) * P],
                                  start=(t == 0), stop=(t == NT - 1))
                    last.then_inc(pv_mm, 1)
            pe.wait_ge(on_ready, 4)
            for k in range(KD):
                if k >= 2:
                    pe.wait_ge(y1_ready, k - 1)
                for qt in range(4):
                    last = tr(X[:, k % 2, qt * P:(qt + 1) * P], oo[:, qt, k * P:(k + 1) * P], ident[:])
                last.then_inc(ot_mm, 1)
            for j in range(8):
                if j >= 2:
                    pe.wait_ge(res_done, R_OUT1 + j - 1)
                gemm(j, U_OUT1 + j + 1, uhi, ulo, (CTX, TOK), (ulo_ready, 32 + 1) if j == 0 else None)
            layer_norm(2, (CTX, TOK), R_OUT1)
            with pe.Fori(0, 3) as q:
                mlp(q, (CTX, TOK), U_MLP1, 32, R_MLP1, 40)
            mlp(3, (CTX, TOK), U_MLP1, 32, R_MLP1, 40)
            layer_norm(3, (CTX, TOK), R_MLP1 + 24)
            for w in range(2):
                for k in range(4):
                    pe.wait_ge(ln_h, 24 + 4 * w + k + 1)
                    for t in range(4):
                        if w == 1 and k == 0 and t >= 2:
                            pe.wait_ge((fin_act, fin_dve)[t % 2], 1)
                        B, b = FIN_BANKS[w][t]
                        last = tr(B[:, b, k * P:(k + 1) * P], hT[:, 4 * w + k, CTX + t * P:CTX + (t + 1) * P], ident[:])
                        if k == 3:
                            last.then_inc(fin_mm, 1)


_INS = ["x", "c", "ctx", "c_ctx", "ada_w", "ada_b", "ln_g", "ln_b", "mlp_w1", "mlp_w2", "mix_w_out", "ev_w_in",
        "ev_qkv_conv", "ev_a_log", "ev_dt_bias", "ev_gdn_norm", "ev_lru_conv_w", "ev_lru_conv_b", "ev_lru_gate_w",
        "ev_lru_gate_b", "ev_lru_lambda", "od_w_qkv", "od_lambda", "od_subln"]


def kernel(**inputs):
    import concourse.bacc as _bacc
    from concourse.bass_utils import run_bass_kernel_spmd as _run

    nc = _bacc.Bacc("TRN2", target_bir_lowering=False, num_devices=1, dynamic_dma_scratch_size=1024)
    arrays = {n: np.ascontiguousarray(inputs[n]) for n in _INS}
    arrays["c_eye"] = np.eye(P, dtype=np.float32)
    arrays["c_gdn"] = gdn_constants()
    arrays["c_rope"] = rope_constants()
    args = {n: nc.dram_tensor(f"in_{n}_dram", a.shape, mybir.dt.from_np(a.dtype), kind="ExternalInput").ap()
            for n, a in arrays.items()}
    out = nc.dram_tensor("out_0_dram", (1, LAT, D), F32, kind="ExternalOutput").ap()
    trunk(nc, args, out)
    r = _run(nc, [{f"in_{n}_dram": a for n, a in arrays.items()}], core_ids=[0])
    return r.results[0]["out_0_dram"]
```
